# Optimizing a Trainium2 kernel written in Bass

```python
import jax
import jax.numpy as jnp
from jax import lax
import numpy as np

D_MODEL = 1024
BATCH = 1
SEQ = 256
DEPTH = 2
DEC_BATCH = 1
DEC_SEQ = 64
PAST_LEN = 512

CHUNK = 64
N_MEM = 256
N_EVEN = (DEPTH + 1) // 2
N_ODD = DEPTH // 2
EPS = 1e-6
A_GROUPS = 4
A_DIM = D_MODEL // 2
A_GDIM = A_DIM // A_GROUPS
A_CHUNK = 128
B_HEADS = 4
B_DIM = D_MODEL // 2
B_HDIM = B_DIM // B_HEADS
EVEN_SPLITS = (A_DIM, 2 * A_DIM, 2 * A_DIM + B_DIM, 2 * A_DIM + 2 * B_DIM, 2 * A_DIM + 3 * B_DIM)
EVEN_IN = 2 * A_DIM + 4 * B_DIM
C_HEADS = 16
C_KV_HEADS = 4
C_HDIM = D_MODEL // C_HEADS
C_GROUP = C_HEADS // C_KV_HEADS
WINDOW = 128
ROPE_THETA = 10000.0
ODD_SPLITS = (C_HEADS * C_HDIM, (C_HEADS + C_KV_HEADS) * C_HDIM)
ODD_IN = (C_HEADS + 2 * C_KV_HEADS) * C_HDIM
X_HEADS = 4
X_HDIM = 128
D_FF = 2816
N_EXPERTS = 8
TOP_K = 2

kernel_name = 'hybrid_streaming_encoder_step'

F32 = jnp.float32

def rms_norm(x, g):
    xf = x.astype(F32)
    y = xf * lax.rsqrt(jnp.mean(xf * xf, axis=-1, keepdims=True) + EPS)
    return (y * g.astype(F32)).astype(x.dtype)

def layer_norm(x, g, b):
    xf = x.astype(F32)
    xc = xf - jnp.mean(xf, axis=-1, keepdims=True)
    y = xc * lax.rsqrt(jnp.mean(xc * xc, axis=-1, keepdims=True) + EPS)
    return (y * g.astype(F32) + b.astype(F32)).astype(x.dtype)

def rope(x, pos):
    half = x.shape[-1] // 2
    inv = 1.0 / (ROPE_THETA ** (jnp.arange(half, dtype=F32) / half))
    ang = pos.astype(F32)[:, None] * inv[None, :]
    cos = jnp.cos(ang)[None, :, None, :]
    sin = jnp.sin(ang)[None, :, None, :]
    xf = x.astype(F32)
    x1, x2 = xf[..., :half], xf[..., half:]
    return jnp.concatenate([x1 * cos - x2 * sin, x2 * cos + x1 * sin], axis=-1).astype(x.dtype)

def gmlp_spatial_gate(u, v, w_s, b_s, ln_g, ln_b):
    B, L = u.shape[:2]
    n = min(A_CHUNK, L)
    v = layer_norm(jax.nn.gelu(v), ln_g, ln_b)
    w = jnp.where(jnp.tril(jnp.ones((n, n), bool))[None], w_s[:, :n, :n], jnp.zeros((), w_s.dtype))
    vc = v.reshape(B, L // n, n, A_GROUPS, A_GDIM)
    s = jnp.einsum('gts,bcsgd->bctgd', w, vc) + jnp.transpose(b_s[:, :n])[None, None, :, :, None]
    out = jax.nn.gelu(u) * s.reshape(B, L, A_GROUPS, A_GDIM)
    return out.reshape(B, L, A_DIM), v

def hgrn2_scan(q, f_logit, i, lb, S0):
    B, L, H, K = q.shape
    q = jax.nn.silu(q.astype(F32))
    f = lb + (1.0 - lb) * jax.nn.sigmoid(f_logit.astype(F32))
    logf = jnp.log(f)
    k = 1.0 - f
    n = min(CHUNK, L)
    nc = L // n

    def blocks(t):
        return t.reshape(B, nc, n, H, t.shape[-1]).transpose(1, 0, 3, 2, 4)

    causal = jnp.tril(jnp.ones((n, n), bool))[:, :, None]

    def step(S, blk):
        qb, kb, vb, gb = blk
        G = jnp.cumsum(gb, axis=2)
        o = jnp.einsum('bhtk,bhkv->bhtv', qb * jnp.exp(G), S)
        decay = jnp.exp(jnp.where(causal, G[:, :, :, None, :] - G[:, :, None, :, :], -jnp.inf))
        att = jnp.einsum('bhtk,bhsk,bhtsk->bhts', qb, kb, decay)
        o = o + jnp.einsum('bhts,bhsv->bhtv', att, vb)
        G_end = G[:, :, -1:, :]
        S = jnp.exp(G_end[:, :, 0, :, None]) * S + jnp.einsum('bhsk,bhsv->bhkv', kb * jnp.exp(G_end - G), vb)
        return S, o

    S, o = lax.scan(step, S0.astype(F32), (blocks(q), blocks(k), blocks(i.astype(F32)), blocks(logf)))
    return o.transpose(1, 0, 3, 2, 4).reshape(B, L, H, -1), S

def even_mixer(h, S0, w_in, w_out, w_s, b_s, ln_g, ln_b, lb, out_g):
    B, L, _ = h.shape
    u, v, q, f, i, g = jnp.split(h @ w_in, EVEN_SPLITS, axis=-1)
    grp = lambda t: t.reshape(B, L, A_GROUPS, A_GDIM)
    hds = lambda t: t.reshape(B, L, B_HEADS, B_HDIM)
    a_out, v_rows = gmlp_spatial_gate(grp(u), grp(v), w_s, b_s, ln_g, ln_b)
    o, S = hgrn2_scan(hds(q), hds(f), hds(i), lb.reshape(B_HEADS, B_HDIM), S0)
    b_out = rms_norm(o, out_g) * jax.nn.silu(hds(g).astype(F32))
    mixed = jnp.concatenate([a_out.astype(h.dtype), b_out.reshape(B, L, B_DIM).astype(h.dtype)], axis=-1)
    return mixed @ w_out, v_rows, S

def attn_qkv(h, pos, w_in, q_g, k_g):
    B, L, _ = h.shape
    q, k, v = jnp.split(h @ w_in, ODD_SPLITS, axis=-1)
    q = rope(rms_norm(q.reshape(B, L, C_HEADS, C_HDIM), q_g), pos)
    k = rope(rms_norm(k.reshape(B, L, C_KV_HEADS, C_HDIM), k_g), pos)
    return q, k, v.reshape(B, L, C_KV_HEADS, C_HDIM)

def sink_softmax(s, sinks):
    sk = jnp.broadcast_to(sinks.astype(F32).reshape(C_KV_HEADS, C_GROUP, 1, 1), s.shape[:-1] + (1,))
    return jax.nn.softmax(jnp.concatenate([s, sk], axis=-1), axis=-1)[..., :-1]

def swa_prompt(q, k, v, sinks):
    B, L = q.shape[:2]
    nc = L // CHUNK
    nb = WINDOW // CHUNK
    pad = ((0, 0), (WINDOW, 0), (0, 0), (0, 0))
    kp = jnp.pad(k, pad).reshape(B, nc + nb, CHUNK, C_KV_HEADS, C_HDIM)
    vp = jnp.pad(v, pad).reshape(B, nc + nb, CHUNK, C_KV_HEADS, C_HDIM)
    kw = jnp.concatenate([kp[:, j:j + nc] for j in range(nb + 1)], axis=2)
    vw = jnp.concatenate([vp[:, j:j + nc] for j in range(nb + 1)], axis=2)
    key_pos = jnp.arange(nc)[:, None] * CHUNK - WINDOW + jnp.arange(WINDOW + CHUNK)[None, :]
    valid = key_pos >= 0
    qc = q.reshape(B, nc, CHUNK, C_KV_HEADS, C_GROUP, C_HDIM)
    s = jnp.einsum('bnqhgd,bnkhd->bnhgqk', qc, kw).astype(F32) * (C_HDIM ** -0.5)
    s = jnp.where(valid[None, :, None, None, None, :], s, -jnp.inf)
    p = sink_softmax(s, sinks)
    o = jnp.einsum('bnhgqk,bnkhd->bnqhgd', p.astype(v.dtype), vw)
    return o.reshape(B, L, C_HEADS * C_HDIM)

def swa_sample(q, k, v, ck, cv, sinks):
    B, L = q.shape[:2]
    kk = jnp.concatenate([ck.astype(k.dtype), k], axis=1)
    vv = jnp.concatenate([cv.astype(v.dtype), v], axis=1)
    qg = q.reshape(B, L, C_KV_HEADS, C_GROUP, C_HDIM)
    s = jnp.einsum('bqhgd,bkhd->bhgqk', qg, kk).astype(F32) * (C_HDIM ** -0.5)
    p = sink_softmax(s, sinks)
    o = jnp.einsum('bhgqk,bkhd->bqhgd', p.astype(vv.dtype), vv)
    return o.reshape(B, L, C_HEADS * C_HDIM)

def memory_kv(mem, g_mem, w_k, w_v, k_g):
    B, M, _ = mem.shape
    m = rms_norm(mem, g_mem)
    mk = rms_norm((m @ w_k).reshape(B, M, X_HEADS, X_HDIM), k_g)
    mv = (m @ w_v).reshape(B, M, X_HEADS, X_HDIM)
    return mk, mv

def cross_attn(h, mk, mv, w_q, w_o, q_g):
    B, L, _ = h.shape
    q = rms_norm((h @ w_q).reshape(B, L, X_HEADS, X_HDIM), q_g)
    s = jnp.einsum('bqhd,bkhd->bhqk', q, mk.astype(q.dtype)).astype(F32) * (X_HDIM ** -0.5)
    p = jax.nn.softmax(s, axis=-1)
    o = jnp.einsum('bhqk,bkhd->bqhd', p.astype(mv.dtype), mv)
    return o.reshape(B, L, X_HEADS * X_HDIM) @ w_o

def swiglu(h, w1, w3, w2):
    return (jax.nn.silu(h @ w1) * (h @ w3)) @ w2

def moe_swiglu(h, router, w1, w3, w2):
    logits = (h @ router).astype(F32)
    top_v, top_i = lax.top_k(logits, TOP_K)
    gates = jax.nn.softmax(top_v, axis=-1)
    gate_full = jnp.sum(jax.nn.one_hot(top_i, N_EXPERTS, dtype=F32) * gates[..., None], axis=-2)
    out = jnp.zeros(h.shape, F32)
    for e in range(N_EXPERTS):
        out = out + gate_full[..., e:e + 1] * swiglu(h, w1[e], w3[e], w2[e]).astype(F32)
    return out

def setup_inputs(seed: int = 0) -> dict:
    key = jax.random.key(seed)
    keys = jax.random.split(key, 64)
    ctr = [0]

    def nrm(shape, scale=1.0):
        kk = keys[ctr[0]]
        ctr[0] += 1
        return jax.random.normal(kk, shape, F32) * scale

    def gain(shape):
        return 1.0 + 0.05 * nrm(shape)

    swa_rows = min(WINDOW, PAST_LEN)
    d = D_MODEL
    return {
        'x_prompt': nrm((BATCH, SEQ, d)),
        'x_sample': nrm((DEC_BATCH, DEC_SEQ, d)),
        'mem_prompt': nrm((BATCH, N_MEM, d)),
        'cache_mem_k': nrm((DEPTH, DEC_BATCH, N_MEM, X_HEADS, X_HDIM)),
        'cache_mem_v': nrm((DEPTH, DEC_BATCH, N_MEM, X_HEADS, X_HDIM), 0.5),
        'state_hgrn': nrm((N_EVEN, DEC_BATCH, B_HEADS, B_HDIM, B_HDIM), 0.5),
        'cache_swa_k': nrm((N_ODD, DEC_BATCH, swa_rows, C_KV_HEADS, C_HDIM)),
        'cache_swa_v': nrm((N_ODD, DEC_BATCH, swa_rows, C_KV_HEADS, C_HDIM), 0.5),
        'norm_mix': gain((DEPTH, d)),
        'norm_xattn': gain((DEPTH, d)),
        'norm_ffn': gain((DEPTH, d)),
        'even_w_in': nrm((N_EVEN, d, EVEN_IN), d ** -0.5),
        'even_w_out': nrm((N_EVEN, A_DIM + B_DIM, d), (A_DIM + B_DIM) ** -0.5),
        'gmlp_w_s': nrm((N_EVEN, A_GROUPS, A_CHUNK, A_CHUNK), A_CHUNK ** -0.5),
        'gmlp_b_s': gain((N_EVEN, A_GROUPS, A_CHUNK)),
        'gmlp_ln_g': gain((N_EVEN, A_GROUPS, A_GDIM)),
        'gmlp_ln_b': nrm((N_EVEN, A_GROUPS, A_GDIM), 0.02),
        'hgrn_lb_logits': nrm((N_EVEN + 1, B_DIM), 0.5),
        'hgrn_out_norm': gain((N_EVEN, B_HDIM)),
        'attn_w_in': nrm((N_ODD, d, ODD_IN), d ** -0.5),
        'attn_w_out': nrm((N_ODD, C_HEADS * C_HDIM, d), (C_HEADS * C_HDIM) ** -0.5),
        'attn_q_norm': gain((N_ODD, C_HDIM)),
        'attn_k_norm': gain((N_ODD, C_HDIM)),
        'attn_sinks': nrm((N_ODD, C_HEADS), 0.5),
        'xattn_mem_norm': gain((DEPTH, d)),
        'xattn_w_q': nrm((DEPTH, d, X_HEADS * X_HDIM), d ** -0.5),
        'xattn_w_k': nrm((DEPTH, d, X_HEADS * X_HDIM), d ** -0.5),
        'xattn_w_v': nrm((DEPTH, d, X_HEADS * X_HDIM), d ** -0.5),
        'xattn_w_o': nrm((DEPTH, X_HEADS * X_HDIM, d), (X_HEADS * X_HDIM) ** -0.5),
        'xattn_q_norm': gain((DEPTH, X_HDIM)),
        'xattn_k_norm': gain((DEPTH, X_HDIM)),
        'ffn_w1': nrm((N_EVEN, d, D_FF), d ** -0.5),
        'ffn_w3': nrm((N_EVEN, d, D_FF), d ** -0.5),
        'ffn_w2': nrm((N_EVEN, D_FF, d), D_FF ** -0.5),
        'moe_router': nrm((N_ODD, d, N_EXPERTS), d ** -0.5),
        'moe_w1': nrm((N_ODD, N_EXPERTS, d, D_FF), d ** -0.5),
        'moe_w3': nrm((N_ODD, N_EXPERTS, d, D_FF), d ** -0.5),
        'moe_w2': nrm((N_ODD, N_EXPERTS, D_FF, d), D_FF ** -0.5),
    }

def reference(x_prompt, x_sample, mem_prompt, cache_mem_k, cache_mem_v, state_hgrn, cache_swa_k, cache_swa_v,
              norm_mix, norm_xattn, norm_ffn,
              even_w_in, even_w_out, gmlp_w_s, gmlp_b_s, gmlp_ln_g, gmlp_ln_b, hgrn_lb_logits, hgrn_out_norm,
              attn_w_in, attn_w_out, attn_q_norm, attn_k_norm, attn_sinks,
              xattn_mem_norm, xattn_w_q, xattn_w_k, xattn_w_v, xattn_w_o, xattn_q_norm, xattn_k_norm,
              ffn_w1, ffn_w3, ffn_w2, moe_router, moe_w1, moe_w3, moe_w2):
    lb_all = jnp.cumsum(jax.nn.softmax(hgrn_lb_logits.astype(F32), axis=0), axis=0)
    L_p = x_prompt.shape[1]
    pos_p = jnp.arange(L_p, dtype=jnp.int32)
    pos_s = PAST_LEN + jnp.arange(x_sample.shape[1], dtype=jnp.int32)
    xp, xs = x_prompt, x_sample
    mem_k_p, mem_v_p, hgrn_p, gmlp_v_s, hgrn_s = [], [], [], [], []
    swk_p, swv_p, swk_s, swv_s = [], [], [], []
    for l in range(DEPTH):
        j = l // 2
        hp = rms_norm(xp, norm_mix[l])
        hs = rms_norm(xs, norm_mix[l])
        if l % 2 == 0:
            wts = (even_w_in[j], even_w_out[j], gmlp_w_s[j], gmlp_b_s[j], gmlp_ln_g[j], gmlp_ln_b[j],
                   lb_all[j], hgrn_out_norm[j])
            S0 = jnp.zeros((xp.shape[0], B_HEADS, B_HDIM, B_HDIM), F32)
            mp, _, Sp = even_mixer(hp, S0, *wts)
            ms, v_rows, Ss = even_mixer(hs, state_hgrn[j], *wts)
            hgrn_p.append(Sp)
            hgrn_s.append(Ss)
            gmlp_v_s.append(v_rows)
        else:
            qp, kp, vp = attn_qkv(hp, pos_p, attn_w_in[j], attn_q_norm[j], attn_k_norm[j])
            mp = swa_prompt(qp, kp, vp, attn_sinks[j]) @ attn_w_out[j]
            qs, ks, vs = attn_qkv(hs, pos_s, attn_w_in[j], attn_q_norm[j], attn_k_norm[j])
            ms = swa_sample(qs, ks, vs, cache_swa_k[j], cache_swa_v[j], attn_sinks[j]) @ attn_w_out[j]
            rows = min(WINDOW, L_p)
            swk_p.append(kp[:, L_p - rows:])
            swv_p.append(vp[:, L_p - rows:])
            swk_s.append(ks)
            swv_s.append(vs)
        xp = xp + mp.astype(xp.dtype)
        xs = xs + ms.astype(xs.dtype)
        mk, mv = memory_kv(mem_prompt, xattn_mem_norm[l], xattn_w_k[l], xattn_w_v[l], xattn_k_norm[l])
        mem_k_p.append(mk)
        mem_v_p.append(mv)
        xp = xp + cross_attn(rms_norm(xp, norm_xattn[l]), mk, mv, xattn_w_q[l], xattn_w_o[l],
                             xattn_q_norm[l]).astype(xp.dtype)
        xs = xs + cross_attn(rms_norm(xs, norm_xattn[l]), cache_mem_k[l], cache_mem_v[l], xattn_w_q[l],
                             xattn_w_o[l], xattn_q_norm[l]).astype(xs.dtype)
        hp = rms_norm(xp, norm_ffn[l])
        hs = rms_norm(xs, norm_ffn[l])
        if l % 2 == 0:
            xp = xp + swiglu(hp, ffn_w1[j], ffn_w3[j], ffn_w2[j]).astype(xp.dtype)
            xs = xs + swiglu(hs, ffn_w1[j], ffn_w3[j], ffn_w2[j]).astype(xs.dtype)
        else:
            xp = xp + moe_swiglu(hp, moe_router[j], moe_w1[j], moe_w3[j], moe_w2[j]).astype(xp.dtype)
            xs = xs + moe_swiglu(hs, moe_router[j], moe_w1[j], moe_w3[j], moe_w2[j]).astype(xs.dtype)
    return (xp, xs, jnp.stack(mem_k_p), jnp.stack(mem_v_p), jnp.stack(hgrn_p), jnp.stack(gmlp_v_s),
            jnp.stack(hgrn_s), jnp.stack(swk_p), jnp.stack(swv_p), jnp.stack(swk_s), jnp.stack(swv_s))


_drawn_inputs = setup_inputs


def setup_inputs(seed=0):
    import zlib

    import numpy as np

    out = dict(_drawn_inputs(seed))
    spreads = {}
    factors = {'norm_xattn': 8.819, 'attn_q_norm': 4.397, 'attn_sinks': 36.457, 'xattn_q_norm': 3.357}
    for name, (base, spread) in spreads.items():
        noise = np.random.default_rng([zlib.crc32(name.encode()), seed]).standard_normal(out[name].shape)
        drawn = base * np.exp(spread * noise) if base else spread * noise
        out[name] = jnp.asarray(drawn.astype(out[name].dtype))
    for name, factor in factors.items():
        out[name] = (out[name] * factor).astype(out[name].dtype)
    return out
```

```python
from contextlib import ExitStack

import numpy as np
import concourse.bass as bass
from concourse import mybir

F32 = mybir.dt.float32
I32 = mybir.dt.int32
U32 = mybir.dt.uint32
ALU = mybir.AluOpType
ACT = mybir.ActivationFunctionType
AX = mybir.AxisListType

P = 128
D = 1024
KC = D // P
TP = 256
TS = 64
T = TP + TS
BLOCKS = [(0, 128), (128, 128), (256, 64)]
MEM = 256
XH = 4
FF = 2816
FC = FF // P
E = 8
EPS = 1e-6
CH = 64
NCH = T // CH
HT = 4 * T
LEVELS = (32, 16, 8, 4, 2, 1)
PASSES = 3 * E

C_ID, C_UT, C_TRIL, C_IOTA, C_LEV = 0, 128, 256, 384, 512
C_COS = C_LEV + 7 * 64
C_SIN = C_COS + 3 * 32
C_BASE = C_SIN + 3 * 32
NCONST = C_BASE + PASSES + 8

R_MIX, R_XAT, R_FFN, R_MEM, R_LNG, R_LNB, R_LB0, R_LB1, R_OUT, R_XQ = 0, 16, 32, 48, 64, 68, 72, 76, 80, 81
NROW = 83
NORM_COL = [R_MIX, R_XAT, R_FFN, R_MIX + 8, R_XAT + 8, R_FFN + 8]


def constants():
    c = np.zeros((P, NCONST), np.float32)
    r = np.arange(P)
    c[:, C_ID:C_ID + P] = np.eye(P)
    c[:, C_UT:C_UT + P] = r[:, None] < r[None, :]
    c[:, C_TRIL:C_TRIL + P] = r[:, None] <= r[None, :]
    c[:, C_IOTA:C_IOTA + P] = r[None, :]
    s, t = np.arange(CH)[:, None], np.arange(CH)[None, :]
    for n, b in enumerate(LEVELS):
        m = (s // (2 * b) == t // (2 * b)) & (s % (2 * b) < b) & (t % (2 * b) >= b)
        c[:CH, C_LEV + n * CH:C_LEV + (n + 1) * CH] = m
    c[:CH, C_LEV + 6 * CH:C_LEV + 7 * CH] = s == t
    half = 32
    inv = np.float32(1.0) / np.power(np.float32(10000.0), np.arange(half, dtype=np.float32) / np.float32(half))
    pos = np.concatenate([np.arange(TP), 512 + np.arange(TS)]).astype(np.float32)
    ang = (pos[:, None] * inv[None, :]).astype(np.float32)
    for b, (t0, n) in enumerate(BLOCKS):
        c[:n, C_COS + b * half:C_COS + (b + 1) * half] = np.cos(ang[t0:t0 + n])
        c[:n, C_SIN + b * half:C_SIN + (b + 1) * half] = np.sin(ang[t0:t0 + n])
    c[:, C_BASE:C_BASE + PASSES + 8] = P * (np.arange(PASSES + 8) // E)[None, :]
    return c


def build(nc, a):
    ctx = ExitStack()
    arena = ctx.enter_context(nc.sbuf_tensor("arena", [P, 53200], F32))
    flag = ctx.enter_context(nc.sbuf_tensor("flag", [1, 1], I32))
    bank = [ctx.enter_context(nc.psum_tensor(f"bank{b}", [P, 512], F32))[:, :] for b in range(8)]
    bank_full = [ctx.enter_context(nc.semaphore(f"bank_full{b}")) for b in range(8)]
    bank_free = [ctx.enter_context(nc.semaphore(f"bank_free{b}")) for b in range(8)]
    named = {}

    def sg(name):
        if name not in named:
            named[name] = ctx.enter_context(nc.semaphore(name))
        return named[name]

    top = [0]

    def take(n, rows=P):
        at = top[0]
        top[0] += n
        assert top[0] <= 53200, top[0]
        return arena[0:rows, at:at + n]

    def split(ap, k):
        return ap.rearrange("p (k n) -> p k n", k=k)

    const = take(NCONST)
    ident = const[:, C_ID:C_ID + P]
    prow = take(P)
    prm = take(96)
    ones = take(P)
    ones_d = take(P)
    ones_h = take(P)
    eps = take(1)
    lb = take(4)
    omlb = take(4)
    kg = split(take(2 * P), 2)
    qkg = split(take(2 * 64), 2)
    sinkc = take(8)
    rstd = take(T)
    stat = take(64)
    routr = split(take(KC * E), KC)
    xT = split(take(KC * T), KC)
    hT = split(take(KC * T), KC)
    ring_at = top[0]
    RING = [take(4096) for _ in range(3)]
    mem_kT_p = take(2 * 4 * MEM).rearrange("p (l h m) -> p l h m", l=2, h=XH)
    mem_kT_s = take(2 * 4 * MEM).rearrange("p (l h m) -> p l h m", l=2, h=XH)
    mem_v_p = take(2 * 2 * 512).rearrange("p (l c n) -> p l c n", l=2, c=2)
    mem_v_s = take(2 * 2 * 512).rearrange("p (l c n) -> p l c n", l=2, c=2)
    work = top[0]

    qT = take(HT)
    kT = take(HT)
    G = take(HT)
    gateT = take(HT)
    iT = take(HT)
    vT = take(HT)
    uT = take(HT)
    X = [take(HT) for _ in range(3)]
    att = take(HT)
    gsq = take(HT)
    vb = split(take(20 * P), 20)
    kp_at = top[0]
    kp = split(take(20 * P), 20)
    vnat = split(take(3 * 512), 3)
    ws = split(take(512), 4)
    wsT = split(take(512), 4)
    bsr = take(512, 1)
    Sp = split(take(512), 4)
    Ss = split(take(512), 4)
    gend = take(20)
    sq = split(arena[:, work + 7 * HT:work + 7 * HT + KC * T], KC)
    oT = X[2]
    memn = split(arena[:, kp_at:kp_at + 2 * D], 2)
    mkn = [split(gsq[:, 0:2 * 512], 2), split(X[0][:, 0:2 * 512], 2)]
    xin = split(arena[:, work + 2 * HT:work + 2 * HT + 3 * D], 3)

    top[0] = work
    qx = take(HT)
    qn = take(HT)
    xsq = take(HT)
    oxT = take(HT)
    prob = [split(take(4 * MEM), 4) for _ in range(2)]
    probT = [split(take(8 * P), 8) for _ in range(2)]
    xstat = [take(16) for _ in range(2)]
    assert top[0] <= work + 9 * HT
    top[0] = work
    gT = split(take(FC * T), FC)
    sil = [take(T) for _ in range(2)]
    assert top[0] <= work + 7 * HT
    W13 = [RING[0][:, s * 2048:(s + 1) * 2048].rearrange("p (k w n) -> p k w n", k=KC, w=2) for s in range(2)]
    W2S = [RING[1 + s][:, 0:11 * 256].rearrange("p (k n) -> p k n", k=11) for s in range(2)]
    top[0] = work + 9 * HT
    qkv = split(take(3 * 1536), 3)
    rot = split(take(3 * 1280), 3)
    rtmp = take(1280)
    top[0] = max(top[0], work + 17 * HT)
    ckn = take(256)
    cvn = take(256)
    gcs = take(3 * 4 * 64).rearrange("p (b f n) -> p b f n", b=3, f=4)
    hstat = split(take(3 * 48), 3)
    assert top[0] <= 53200, top[0]
    top[0] = work
    qT2 = take(16 * T, 64).rearrange("p (c kv par hh t) -> p c kv par hh t", c=NCH, kv=4, par=2, hh=2)
    kT2 = split(take(4 * T, 64), 4)
    kTs = split(take(4 * 192, 64), 4)
    sp_prob = [split(take(4 * 256), 4) for _ in range(2)]
    assert top[0] <= work + 9 * HT
    top[0] = work + 9 * HT + 3 * 1536
    sp_probT = [[split(take(4 * P), 4) for _ in range(2)] for _ in range(2)]
    sstat = [take(24) for _ in range(2)]
    o2T = hT
    WE = [arena[:, ring_at + s * 6144:ring_at + s * 6144 + 4096].rearrange("p (k w n) -> p k w n", k=KC, w=2)
          for s in range(4)]
    WD = [split(arena[:, ring_at + s * 6144 + 4096:ring_at + (s + 1) * 6144], 2) for s in range(4)]
    moe_at = ring_at + 4 * 6144
    assert moe_at <= work + 7 * HT
    top[0] = work + 9 * HT
    hnat = split(take(3 * D), 3)
    xnat = split(take(3 * D), 3)
    xg = split(take(KC * P), KC)
    ysb = take(D)
    onehot = split(take(3 * P), 3)
    gated = split(take(3 * P), 3)
    scat = take(T)
    act1 = take(256)
    hid = take(256)
    hidT = split(take(256), 2)
    logit = split(take(24), 3)
    top8 = split(take(24), 3)
    idx8 = split(take(24), 3)
    idxf = split(take(24), 3)
    eq = take(48).rearrange("p (b k e) -> p b k e", b=3, k=2)
    gsel = take(12).rearrange("p (b n) -> p b n", b=3)
    chosen = split(take(24), 3)
    gates = split(take(3 * (PASSES + 8)), 3)
    slot = split(take(3 * (PASSES + 8)), 3)
    rank = split(take(24), 3)
    load = take(8)
    maxload = take(1)
    assert top[0] <= 53200, top[0]

    KEYS = [(0, 64, 0, 0), (0, 128, 0, 0), (0, 192, 0, 64), (64, 192, 64, 128), (0, 192, 0, 64)]
    use, uses_of, order, turn = {}, [0] * 8, [], {"proj": 0, "misc": 0}

    def plan(key, kind):
        if kind == "proj":
            b = turn["proj"] % 3
            turn["proj"] += 1
        elif kind == "misc":
            b = 4 + turn["misc"] % 4
            turn["misc"] += 1
        else:
            b = kind
        use[key] = (b, uses_of[b])
        uses_of[b] += 1
        order.append(key)

    def plan_norm(n):
        plan(("norm", n), 3)

    def plan_xattn(l):
        for h in range(XH):
            plan(("xq", l, h), "proj")
        for h in range(XH):
            plan(("xqn", l, h), 3)
        for b in range(3):
            for k in range(2):
                plan(("xs", l, b, k), "misc")
            if b:
                plan_xattn_tail(l, b - 1)
        plan_xattn_tail(l, 2)
        for m in range(KC):
            plan(("xo", l, m), "proj")

    def plan_xattn_tail(l, b):
        plan(("xpT", l, b, 0), 0)
        plan(("xpT", l, b, 1), 1)
        plan(("xpv", l, b), 2)

    plan("prm", "misc")
    for b in range(3):
        for k in range(2):
            plan(("xin", b, k), "misc")
    plan_norm(0)
    for w in "fqig":
        for h in range(4):
            plan((w, h), "proj")
        if w == "i":
            for g in range(5):
                plan(("iT", g), "misc")
    for h in range(4):
        plan(("v", h), "proj")
    for n in range(3):
        for g in range(3):
            plan(("att", n, g), "misc")
    for h in range(4):
        plan(("u", h), "proj")
    for g in range(4):
        plan(("mean", g), "misc")
    for g in range(3):
        plan(("att", 3, g), "misc")
    for g in range(4):
        plan(("var", g), 3)
    for n in range(4, 7):
        for g in range(3):
            plan(("att", n, g), "misc")
    plan("wsT", "misc")
    for l in range(2):
        for c in range(2):
            plan(("ckT", l, c), "misc")
        for g in range(4):
            plan(("mT", l, g), "misc")
        for w in "kv":
            for c in range(2):
                plan(("mem" + w, l, c), "proj")
        for c in range(2):
            plan(("mkT", l, c), "misc")
    for b in range(3):
        plan(("vn", b), "misc")
    for g in range(4):
        plan(("gate", g), "misc")
    for g in range(5):
        plan(("kp", g), "misc")
    for c in range(NCH):
        plan(("S", c), 6 + c % 2)
        plan(("o", c), 4 + c % 2)
    turn["misc"] = 0
    for h in range(4):
        plan(("on", h), 3)
    for m in range(KC):
        plan(("wo", m), "proj")
    plan_norm(1)
    plan_xattn(0)
    plan_norm(2)
    uses_before_ffn = list(uses_of)
    plan_norm(3)
    for b in range(3):
        for u in range(3):
            plan(("qkv", b, u), "proj")
    plan("cskT", "misc")
    for b in range(3):
        for g in range(5):
            plan(("qkT", b, g), "misc")

    def plan_swa_tail(c, g):
        plan(("spT", c, g, 0), 0)
        if KEYS[c][3]:
            plan(("spT", c, g, 1), 1)
        plan(("spv", c, g), 2)

    GROUPS = [(c, g) for c in range(NCH) for g in range(2)]
    for n, (c, g) in enumerate(GROUPS):
        for k in range(2):
            plan(("ss", c, g, k), "misc")
        if n:
            plan_swa_tail(*GROUPS[n - 1])
    plan_swa_tail(*GROUPS[-1])
    for m in range(KC):
        plan(("ao", m), "proj")
    plan_norm(4)
    plan_xattn(1)
    plan_norm(5)
    for b in range(3):
        plan(("logit", b), 3)
    for b in range(3):
        for k in range(2):
            plan(("hnat", b, k), "misc")
    for b in range(3):
        for k in range(2):
            plan(("xnat", b, k), "misc")
    for b in range(3):
        plan(("rank", b), 3)
    plan("load", 3)
    H, Y, TR, GA, O = bank[0], [bank[1], bank[2]], bank[4], [bank[5], bank[6]], [bank[7], bank[3]]

    def full(eng, key):
        b, n = use[key]
        eng.wait_ge(bank_full[b], n + 1)
        return bank[b]

    def read(eng, key):
        b, n = use[key]
        eng.wait_ge(bank_free[b], n + 1)

    def freed(key):
        return bank_free[use[key][0]]

    UNITS = ["f", "q", "i", "g", "v", "u", "k0", "v0", "k1", "v1", "wo0", "wo1", "xq0", "xo0",
             "qkv0", "qkv1", "qkv2", "ao0", "ao1", "xq1", "xo1"]
    FIRST = 14
    unit_no = {u: n for n, u in enumerate(UNITS)}

    LAST_USE = {u: (u, 3) for u in "fqigvu"} | {f"{w}{l}": ("mem" + w, l, 1) for w in "kv" for l in (0, 1)} \
        | {"wo0": ("wo", 3), "wo1": ("wo", 7), "ao0": ("ao", 3), "ao1": ("ao", 7)} \
        | {f"xq{l}": ("xq", l, 3) for l in (0, 1)} | {f"xo{l}": ("xo", l, 7) for l in (0, 1)} \
        | {f"qkv{u}": ("qkv", 2, u) for u in range(3)}

    def unit_slot(n):
        return (n if n < FIRST else n - FIRST) % 3

    def unit_fill(n):
        return sum(unit_slot(k) == unit_slot(n) for k in range(n + 1))

    def weights(eng, name):
        n = unit_no[name]
        eng.wait_ge(sg(f"ring_full{unit_slot(n)}"), 16 * unit_fill(n))
        return RING[unit_slot(n)]

    def cols(w, c0):
        return w[:, c0:c0 + 512].rearrange("(k p) n -> p k n", p=P)

    def unit_source(name):
        even = {"u": 0, "v": 512, "q": 1024, "f": 1536, "i": 2048, "g": 2560}
        if name in even:
            return cols(a["even_w_in"][0], even[name])
        kind, n = name[:-1], int(name[-1])
        if kind == "k":
            return cols(a["xattn_w_k"][n], 0)
        if kind == "v":
            return cols(a["xattn_w_v"][n], 0)
        if kind == "xq":
            return cols(a["xattn_w_q"][n], 0)
        if kind == "xo":
            return a["xattn_w_o"][n].rearrange("(k p) n -> p k n", p=P)
        return cols({"wo": a["even_w_out"], "qkv": a["attn_w_in"], "ao": a["attn_w_out"]}[kind][0], 512 * n)

    block = ctx.enter_context(nc.Block())

    @block.sync
    def _(sp):
        for b, (t0, n) in enumerate(BLOCKS):
            src = a["x_prompt"][0, t0:t0 + n] if t0 < TP else a["x_sample"][0]
            sp.dma_start(xin[0:n, b], src).then_inc(sg("x_loaded"), 16)

        def load_unit(n):
            name = UNITS[n]
            k = 4 if name[:2] == "xo" else KC
            sp.dma_start(split(RING[unit_slot(n)], k), unit_source(name)).then_inc(sg(f"ring_full{unit_slot(n)}"), 16)

        for n in range(FIRST):
            if n >= 3:
                full(sp, LAST_USE[UNITS[n - 3]])
            load_unit(n)

        def load_w13(i):
            for s in range(2):
                c0 = bass.ds(i * 256 + s * P, P)
                for w, src in enumerate((a["ffn_w1"][0], a["ffn_w3"][0])):
                    sp.dma_start(W13[s][:, :, w], src[:, c0].rearrange("(k p) n -> p k n", p=P)) \
                        .then_inc(sg(f"w13_full{s}"), 16)

        def load_w2(m, s):
            src = a["ffn_w2"][0][s * 11 * P:(s + 1) * 11 * P, bass.ds(m * 256, 256)]
            sp.dma_start(W2S[s], src.rearrange("(k p) n -> p k n", p=P)).then_inc(sg(f"w2_full{s}"), 16)

        full(sp, LAST_USE["xq0"])
        load_w13(0)
        full(sp, LAST_USE["xo0"])
        load_w2(0, 0)
        load_w2(0, 1)
        with sp.Fori(1, 11) as i:
            for s in range(2):
                sp.wait_ge(sg("ffn_h_done"), 2 * i + s - 1)
                c0 = bass.ds(i * 256 + s * P, P)
                for w, src in enumerate((a["ffn_w1"][0], a["ffn_w3"][0])):
                    sp.dma_start(W13[s][:, :, w], src[:, c0].rearrange("(k p) n -> p k n", p=P)) \
                        .then_inc(sg(f"w13_full{s}"), 16)
        with sp.Fori(1, 4) as m:
            for s in range(2):
                sp.wait_ge(sg("ffn_half" if s == 0 else "ffn_y"), m if s == 0 else 2 * m)
                load_w2(m, s)
        for n in range(FIRST, len(UNITS)):
            if n == FIRST:
                sp.wait_ge(sg("ffn_h_done"), FC)
            elif n == FIRST + 1:
                sp.wait_ge(sg("ffn_half"), 4)
            elif n == FIRST + 2:
                sp.wait_ge(sg("ffn_y"), 8)
            else:
                full(sp, LAST_USE[UNITS[n - 3]])
            load_unit(n)

        def load_expert_block(e, j):
            s = j % 4
            for w, src in enumerate((a["moe_w1"][0], a["moe_w3"][0])):
                v = src[bass.ds(e, 1), :, j * 256:(j + 1) * 256].rearrange("e (k p) n -> p (e k) n", p=P)
                sp.dma_start(WE[s][:, :, w], v).then_inc(sg(f"moe13_full{s}"), 16)
            v = a["moe_w2"][0][bass.ds(e, 1), j * 256:(j + 1) * 256, :].rearrange("e (k p) n -> p (e k) n", p=P)
            sp.dma_start(WD[s], v).then_inc(sg(f"moe2_full{s}"), 16)

        def load_expert(e, first):
            for j in range(11):
                prev = 11 * first + j - 4 if j >= 4 else 11 * first - 11 + {0: 8, 1: 9, 2: 10, 3: 7}[j]
                sp.wait_ge(sg("moe_h_done"), prev + 1)
                sp.wait_ge(sg("moe_y_done"), prev + 1)
                load_expert_block(e, j)

        full(sp, LAST_USE["xo1"])
        for j in range(11):
            if j >= 4:
                sp.wait_ge(sg("moe_h_done"), j - 3)
                sp.wait_ge(sg("moe_y_done"), j - 3)
            load_expert_block(0, j)
        with sp.Fori(1, E) as e:
            load_expert(e, e)
        sp.wait_ge(sg("flag_ready"), 1)
        overloaded = sp.value_load(flag[0:1, 0:1])
        with sp.If(overloaded > P):
            for r in (1, 2):
                with sp.Fori(0, E) as e:
                    load_expert(e, e + E * r)

    @block.gpsimd
    def _(pool):
        pool.dma_start(const[:], a["shape_constants"]).then_inc(sg("const_loaded"), 16)
        rows = lambda x: x.rearrange("(k p) -> k p", p=P)
        for l in range(2):
            for name, r in (("norm_mix", R_MIX), ("norm_xattn", R_XAT), ("norm_ffn", R_FFN), ("xattn_mem_norm", R_MEM)):
                pool.dma_start(prow[r + 8 * l:r + 8 * l + 8, :], rows(a[name][l])).then_inc(sg("prm_loaded"), 16)
            pool.dma_start(prow[R_LB0 + 4 * l:R_LB0 + 4 * l + 4, :], rows(a["hgrn_lb_logits"][l])) \
                .then_inc(sg("prm_loaded"), 16)
        pool.dma_start(prow[R_LNG:R_LNG + 4, :], a["gmlp_ln_g"][0]).then_inc(sg("prm_loaded"), 16)
        pool.dma_start(prow[R_LNB:R_LNB + 4, :], a["gmlp_ln_b"][0]).then_inc(sg("prm_loaded"), 16)
        pool.dma_start(prow[R_OUT:R_OUT + 1, :], a["hgrn_out_norm"]).then_inc(sg("prm_loaded"), 16)
        pool.dma_start(prow[R_XQ:R_XQ + 2, :], a["xattn_q_norm"]).then_inc(sg("prm_loaded"), 16)
        pool.memset(ones, 1.0).then_inc(sg("const_set"), 1)
        pool.memset(ones_d, 1.0 / D).then_inc(sg("const_set"), 1)
        pool.memset(ones_h, 1.0 / P).then_inc(sg("const_set"), 1)
        pool.memset(eps, EPS).then_inc(sg("const_set"), 1)
        pool.dma_start(kg, a["xattn_k_norm"].partition_broadcast(P)).then_inc(sg("small_loaded"), 16)
        pool.dma_start(qkg[:, 0], a["attn_q_norm"][0].partition_broadcast(P)).then_inc(sg("small_loaded"), 16)
        pool.dma_start(qkg[:, 1], a["attn_k_norm"][0].partition_broadcast(P)).then_inc(sg("small_loaded"), 16)
        by_half = a["attn_sinks"][0].rearrange("(kv hh par) -> hh kv par", kv=4, hh=2)
        for hh in range(2):
            pool.dma_start(sinkc[hh * 64:hh * 64 + 64, :].rearrange("p (kv par) -> p kv par", kv=4),
                           by_half[hh].partition_broadcast(64)).then_inc(sg("small_loaded"), 16)
        pool.dma_start(routr, a["moe_router"][0].rearrange("(k p) e -> p k e", p=P)).then_inc(sg("small_loaded"), 16)
        pool.dma_start(memn, a["mem_prompt"][0].rearrange("(c p) n -> p c n", p=P)).then_inc(sg("memn_loaded"), 16)
        for l in range(2):
            pool.dma_start(split(mem_kT_p[:, l].rearrange("p h m -> p (h m)"), 2),
                           a["cache_mem_k"][l, 0].rearrange("(c p) h d -> p c (h d)", p=P)) \
                .then_inc(sg("cache_loaded"), 16)
            pool.dma_start(mem_v_s[:, l], a["cache_mem_v"][l, 0].rearrange("(c p) h d -> p c (h d)", p=P)) \
                .then_inc(sg("cache_loaded"), 16)
        pool.dma_start(ws, a["gmlp_w_s"][0].rearrange("g t s -> t g s")).then_inc(sg("ws_loaded"), 16)
        pool.dma_start(bsr, a["gmlp_b_s"].rearrange("o g t -> o (g t)")).then_inc(sg("ws_loaded"), 16)
        pool.dma_start(Ss, a["state_hgrn"][0, 0].rearrange("h k v -> k h v")).then_inc(sg("state_loaded"), 16)
        pool.wait_ge(bank_full[use[("norm", 0)][0]], use[("norm", 0)][1] + 1)
        pool.memset(X[0], 1.0).then_inc(sg("scan_ones"), 1)
        pool.wait_ge(sg("scan_ones"), 1)
        pool.memset(X[0].rearrange("p (c t) -> p c t", t=CH)[:, :, 0:1], 0.0).then_inc(sg("scan_mask"), 1)
        def level_keys(n):
            b = LEVELS[n]
            x = X[n % 3].rearrange("p (n two b) -> p n two b", two=2, b=b)[:, :, 0]
            k = kT.rearrange("p (n two b) -> p n two b", two=2, b=b)[:, :, 0]
            pool.wait_ge(sg("level_exp"), n + 1)
            pool.wait_ge(sg("k_ready"), 4)
            pool.tensor_tensor(x, x, k, ALU.mult).then_inc(sg("level_k"), 1)

        for n in range(6):
            level_keys(n)
        full(pool, ("att", 6, 2))
        pool.wait_ge(sg("end_exp"), 1)
        pool.tensor_tensor(kT, kT, X[1], ALU.mult).then_inc(sg("kp_ready"), 1)
        out_sem = sg("out_written")
        pool.wait_ge(sg("const_loaded"), 16)
        pool.wait_ge(sg("small_loaded"), 96)
        for l in range(2):
            pool.wait_ge(sg("mk_ready"), 2 * l + 2)
            pool.dma_start(a["mem_k_prompt"][l, 0].rearrange("(c p) h d -> p c (h d)", p=P), mkn[l]) \
                .then_inc(out_sem, 16)
            read(pool, ("memv", l, 1))
            pool.dma_start(a["mem_v_prompt"][l, 0].rearrange("(c p) h d -> p c (h d)", p=P), mem_v_p[:, l]) \
                .then_inc(out_sem, 16)
        read(pool, ("vn", 2))
        pool.dma_start(a["gmlp_v_sample"][0, 0].rearrange("t g d -> t (g d)"), vnat[0:TS, 2]).then_inc(out_sem, 16)
        read(pool, ("S", 4))
        pool.dma_start(a["hgrn_state_prompt"][0, 0].rearrange("h k v -> k h v"), Sp).then_inc(out_sem, 16)
        pool.dma_start(a["hgrn_state_sample"][0, 0].rearrange("h k v -> k h v"), Ss).then_inc(out_sem, 16)
        pool.wait_ge(out_sem, 16 * 7)
        full(pool, ("wo", KC - 1))
        pool.dma_start(ckn, a["cache_swa_k"][0, 0].rearrange("t h d -> t (h d)")).then_inc(sg("swa_cache_loaded"), 16)
        pool.dma_start(cvn, a["cache_swa_v"][0, 0].rearrange("t h d -> t (h d)")).then_inc(sg("swa_cache_loaded"), 16)
        for b, (t0, n) in enumerate(BLOCKS):
            for i in range(2):
                for f, at in enumerate((C_COS, C_SIN)):
                    trig = const[0:n, at + b * 32:at + b * 32 + 32].unsqueeze(1).broadcast_to([n, 2, 32])
                    pool.tensor_tensor(gcs[0:n, b, 2 * i + f].rearrange("p (x n) -> p x n", x=2),
                                       qkg[0:n, i].rearrange("p (x n) -> p x n", x=2), trig, ALU.mult) \
                        .then_inc(sg("rope_tables"), 1)
        pool.wait_ge(sg("rope_tables"), 12)
        for b, (t0, n) in enumerate(BLOCKS):
            pool.wait_ge(sg("qk_scaled"), b + 1)
            if b:
                pool.wait_ge(sg("rot_done"), 2 * b)
            for h0, nh, f in ((0, 16, 1), (16, 4, 3)):
                x = qkv[0:n, b, h0 * 64:(h0 + nh) * 64].rearrange("p (h d) -> p h d", d=64)
                o = rtmp[0:n, h0 * 64:(h0 + nh) * 64].rearrange("p (h d) -> p h d", d=64)
                pool.tensor_tensor(o, x, gcs[0:n, b, f].unsqueeze(1).broadcast_to([n, nh, 64]), ALU.mult) \
                    .then_inc(sg("sine_ready"), 1)
        pool.wait_ge(sg("rot_done"), 6)
        flat = lambda x: x.rearrange("t h d -> t (h d)")
        pool.dma_start(flat(a["swa_k_prompt"][0, 0]), rot[:, 1, 1024:1280]).then_inc(out_sem, 16)
        pool.dma_start(flat(a["swa_v_prompt"][0, 0]), qkv[:, 1, 1280:1536]).then_inc(out_sem, 16)
        pool.dma_start(flat(a["swa_k_sample"][0, 0]), rot[0:TS, 2, 1024:1280]).then_inc(out_sem, 16)
        pool.dma_start(flat(a["swa_v_sample"][0, 0]), qkv[0:TS, 2, 1280:1536]).then_inc(out_sem, 16)
        pool.wait_ge(sg("y_final"), 1)
        pool.dma_start(a["y_prompt"][0].rearrange("(b p) n -> p b n", p=P), xnat[:, 0:2]).then_inc(out_sem, 16)
        pool.dma_start(a["y_sample"][0], xnat[0:TS, 2]).then_inc(out_sem, 16)
        pool.wait_ge(out_sem, 16 * 13)


    @block.tensor
    def _(pe):
        for name in ("scat_T", "hid_T", "scatter_done"):
            pe.sem_inc(sg(name), 1)
        mm = nc.tensor.matmul
        todo = list(order)

        def start(key):
            assert todo.pop(0) == key, key
            b, n = use[key]
            if n:
                pe.wait_ge(bank_free[b], n)
            return bank[b]

        def end(ins, key):
            ins.then_inc(bank_full[use[key][0]], 1)

        def transposes(key, parts):
            out = start(key)
            for at, x in parts:
                rows, n = x.shape[0], x.shape[1]
                ins = nc.tensor.transpose(out[0:n, at:at + rows], x, ident[0:rows, 0:rows])
            end(ins, key)

        def project(key, w, width, m, x, kc, ready=None):
            out = start(key)
            for k in range(kc):
                if ready:
                    ready(k)
                ins = mm(out[:, 0:T], w[:, k * width + m * P:k * width + (m + 1) * P], x[:, k, :],
                         start=k == 0, stop=k == kc - 1)
            end(ins, key)
            return ins

        def h_chunk(n):
            return lambda k: pe.wait_ge(sg("h_ready"), KC * n + k + 1)

        def mixed_chunk(k):
            if k < 4:
                read(pe, ("gate", k))
            if k >= 4:
                pe.wait_ge(sg("mixed"), k - 3)

        def norm(n):
            out = start(("norm", n))
            for c in range(KC):
                pe.wait_ge(sg("sq_ready"), KC * n + c + 1)
                ins = mm(out[:, 0:T], ones_d, sq[:, c], start=c == 0, stop=c == KC - 1)
            end(ins, ("norm", n))

        pe.wait_ge(sg("const_loaded"), 16)
        pe.wait_ge(sg("prm_loaded"), 16 * 14)
        transposes("prm", [(0, prow[0:NROW, :])])
        for b, (t0, n) in enumerate(BLOCKS):
            pe.wait_ge(sg("x_loaded"), 48)
            for k in range(2):
                transposes(("xin", b, k), [(i * P, xin[0:n, b, (4 * k + i) * P:(4 * k + i + 1) * P]) for i in range(4)])
        pe.wait_ge(sg("const_set"), 4)
        norm(0)
        def even_unit(name):
            w = weights(pe, name)
            for h in range(4):
                project((name, h), w, 512, h, hT, KC, ready=h_chunk(0))

        for name in "fqi":
            even_unit(name)
        for g in range(5):
            read(pe, ("i", 3))
            transposes(("iT", g), [(i * P, iT[:, (4 * g + i) * CH:(4 * g + i + 1) * CH]) for i in range(4)])
        even_unit("g")
        even_unit("v")

        def level(n):
            if n < 6:
                pe.wait_ge(sg("level_k"), n + 1)
                pe.wait_ge(sg("level_q"), n + 1)
            lhs, rhs = (X[n % 3], X[n % 3]) if n < 6 else (kT, qT)
            for g in range(3):
                out = start(("att", n, g))
                pairs = range(8 * g, min(8 * g + 8, 20))
                for hc in pairs:
                    t = slice(hc * CH, (hc + 1) * CH)
                    ins = mm(out[0:CH, (hc - 8 * g) * CH:(hc - 8 * g + 1) * CH], lhs[:, t], rhs[:, t], start=True, stop=True)
                end(ins, ("att", n, g))

        for n in range(3):
            level(n)
        even_unit("u")
        for g in range(4):
            read(pe, ("v", g))
            out = start(("mean", g))
            end(mm(out[:, 0:T], ones_h, vT[:, g * T:(g + 1) * T], start=True, stop=True), ("mean", g))
        level(3)
        for g in range(4):
            pe.wait_ge(sg("v_sq"), g + 1)
            out = start(("var", g))
            end(mm(out[:, 0:T], ones_h, gsq[:, g * T:(g + 1) * T], start=True, stop=True), ("var", g))
        for n in range(4, 7):
            level(n)
        pe.wait_ge(sg("ws_loaded"), 32)
        transposes("wsT", [(g * P, ws[:, g]) for g in range(4)])
        pe.wait_ge(sg("cache_loaded"), 64)
        pe.wait_ge(sg("memn_scaled"), 2)
        for l in range(2):
            raw = split(mem_kT_p[:, l].rearrange("p h m -> p (h m)"), 2)
            for c in range(2):
                transposes(("ckT", l, c), [(h * P, raw[:, c, h * P:(h + 1) * P]) for h in range(4)])
            for g in range(4):
                c, k = divmod(g, 2)
                transposes(("mT", l, g), [(i * P, memn[:, c, (4 * k + i) * P:(4 * k + i + 1) * P]) for i in range(4)])
            read(pe, ("mT", l, 3))
            for name in "kv":
                w = split(weights(pe, f"{name}{l}"), KC)
                for c in range(2):
                    out = start(("mem" + name, l, c))
                    for k in range(KC):
                        ins = mm(out, hT[:, k, c * P:(c + 1) * P], w[:, k], start=k == 0, stop=k == KC - 1)
                    end(ins, ("mem" + name, l, c))
            for c in range(2):
                pe.wait_ge(sg("mk_ready"), 2 * l + c + 1)
                transposes(("mkT", l, c), [(h * P, mkn[l][:, c, h * P:(h + 1) * P]) for h in range(4)])
        for b, (t0, n) in enumerate(BLOCKS):
            pe.wait_ge(sg("vn_ready"), 4)
            transposes(("vn", b), [(g * P, vT[:, g * T + t0:g * T + t0 + n]) for g in range(4)])
        read(pe, ("vn", 2))
        read(pe, "wsT")
        for g in range(4):
            out = start(("gate", g))
            for b, (t0, n) in enumerate(BLOCKS):
                mm(out[:, t0:t0 + n], vnat[0:n, b, g * P:(g + 1) * P], wsT[0:n, g, 0:n], start=True, stop=False)
                ins = mm(out[:, t0:t0 + n], ones[0:1, :], bsr[0:1, g * P:g * P + n], start=False, stop=True)
            end(ins, ("gate", g))
        pe.wait_ge(sg("kp_ready"), 1)
        for g in range(5):
            transposes(("kp", g), [(i * P, kT[:, (4 * g + i) * CH:(4 * g + i + 1) * CH]) for i in range(4)])
        read(pe, ("kp", 4))
        read(pe, ("iT", 4))
        pe.wait_ge(sg("qp_ready"), 1)
        read(pe, ("att", 6, 2))
        for c in range(NCH):
            out = start(("S", c))
            for h in range(4):
                hc = h * NCH + c
                ins = mm(out[:, h * P:(h + 1) * P], kp[0:CH, hc], vb[0:CH, hc], start=True, stop=True)
            end(ins, ("S", c))
            out = start(("o", c))
            if 1 <= c <= 3:
                read(pe, ("S", c - 1))
            if c == 4:
                pe.wait_ge(sg("state_loaded"), 16)
            S = Ss if c == 4 else Sp
            for h in range(4):
                hc = h * NCH + c
                t = slice(hc * CH, (hc + 1) * CH)
                if c:
                    mm(out[:, h * CH:(h + 1) * CH], S[:, h], qT[:, t], start=True, stop=False)
                ins = mm(out[:, h * CH:(h + 1) * CH], vb[0:CH, hc], att[0:CH, t], start=c == 0, stop=True)
            end(ins, ("o", c))
        for h in range(4):
            pe.wait_ge(sg("o_sq"), h + 1)
            out = start(("on", h))
            end(mm(out[:, 0:T], ones_h, vT[:, h * T:(h + 1) * T], start=True, stop=True), ("on", h))
        for m in range(KC):
            w = weights(pe, f"wo{m // 4}")
            project(("wo", m), w, 512, m % 4, hT, KC, ready=mixed_chunk)

        def xattn(l):
            w = weights(pe, f"xq{l}")
            for h in range(XH):
                project(("xq", l, h), w, 512, h, hT, KC, ready=h_chunk(1 if l == 0 else 4))
            for h in range(XH):
                pe.wait_ge(sg("xq_sq"), 4 * l + h + 1)
                out = start(("xqn", l, h))
                end(mm(out[:, 0:T], ones_h, xsq[:, h * T:(h + 1) * T], start=True, stop=True), ("xqn", l, h))

            def tail(b):
                t0, n = BLOCKS[b]
                v = mem_v_p if b < 2 else mem_v_s
                pe.wait_ge(sg("xprob"), 3 * l + b + 1)
                for k in range(2):
                    transposes(("xpT", l, b, k), [(h * P, prob[b % 2][0:n, h, k * P:(k + 1) * P]) for h in range(4)])
                read(pe, ("xpT", l, b, 0))
                read(pe, ("xpT", l, b, 1))
                out = start(("xpv", l, b))
                for h in range(4):
                    for k in range(2):
                        ins = mm(out[:, h * P:h * P + n], v[:, l, k, h * P:(h + 1) * P], probT[b % 2][:, 4 * k + h, 0:n],
                                 start=k == 0, stop=k == 1)
                end(ins, ("xpv", l, b))

            read(pe, ("mkT", 1, 1))
            for b, (t0, n) in enumerate(BLOCKS):
                keys = mem_kT_p if b < 2 else mem_kT_s
                for k in range(2):
                    out = start(("xs", l, b, k))
                    for hh in range(2):
                        h = 2 * k + hh
                        pe.wait_ge(sg("xq_ready"), 4 * l + h + 1)
                        ins = mm(out[0:n, hh * MEM:(hh + 1) * MEM], qn[:, h * T + t0:h * T + t0 + n], keys[:, l, h],
                                 start=True, stop=True)
                    end(ins, ("xs", l, b, k))
                if b:
                    tail(b - 1)
            tail(2)
            w = weights(pe, f"xo{l}")
            read(pe, ("xpv", l, 2))
            for m in range(KC):
                project(("xo", l, m), w, D, m, split(oxT, 4), 4)

        norm(1)
        xattn(0)
        norm(2)
        pe.wait_ge(sg("h_ready"), 3 * KC)
        pe.wait_ge(bank_free[0], uses_before_ffn[0])
        for b in range(1, 8):
            if uses_before_ffn[b]:
                pe.wait_ge(bank_free[b], uses_before_ffn[b])
        with pe.Fori(0, 11) as i:
            for s in range(2):
                pe.wait_ge(sg(f"w13_full{s}"), 32 * i + 32)
                pe.wait_ge(sg(f"ffn_g{s}"), i + 1)
                for w in range(2):
                    for k in range(KC):
                        ins = mm(bank[2 * s + w][:, 0:T], W13[s][:, k, w], hT[:, k], start=k == 0, stop=k == KC - 1)
                    if w == 0:
                        ins.then_inc(sg(f"ffn_h1_{s}"), 1)
                ins.then_inc(sg("ffn_h_done"), 1)
        pe.wait_ge(sg("ffn_g0"), 12)
        pe.wait_ge(sg("ffn_g1"), 12)
        with pe.Fori(0, 2) as mm2:
            for q in range(2):
                pe.wait_ge(sg("ffn_out"), 4 * mm2 + 1)
                for s in range(2):
                    pe.wait_ge(sg(f"w2_full{s}"), 32 * mm2 + 16 * q + 16)
                    for t in range(2):
                        for k in range(11):
                            ins = mm(bank[4 + 2 * q + t][:, 0:T], W2S[s][:, k, t * P:(t + 1) * P], gT[:, 11 * s + k],
                                     start=s == 0 and k == 0, stop=s == 1 and k == 10, skip_group_check=True)
                        if s == 1 and t == 0:
                            ins.then_inc(sg("ffn_y"), 1)
                    if s == 0:
                        ins.then_inc(sg("ffn_half"), 1)
                ins.then_inc(sg("ffn_y"), 1)
        norm(3)
        for u in range(3):
            weights(pe, f"qkv{u}")
        for b, (t0, n) in enumerate(BLOCKS):
            for u in range(3):
                w = split(RING[unit_slot(unit_no[f"qkv{u}"])], KC)
                out = start(("qkv", b, u))
                for k in range(KC):
                    pe.wait_ge(sg("h_ready"), 3 * KC + k + 1)
                    ins = mm(out[0:n, :], hT[:, k, t0:t0 + n], w[:, k], start=k == 0, stop=k == KC - 1)
                end(ins, ("qkv", b, u))
        pe.wait_ge(sg("swa_cache_loaded"), 32)
        transposes("cskT", [(kv * P, ckn[:, kv * 64:(kv + 1) * 64]) for kv in range(4)])
        for b, (t0, n) in enumerate(BLOCKS):
            pe.wait_ge(sg("rot_done"), 2 * b + 2)
            for g in range(5):
                transposes(("qkT", b, g), [(i * P, rot[0:n, b, (4 * g + i) * 64:(4 * g + i + 1) * 64]) for i in range(4)])

        def swa_tail(i, c, g):
            k0, nk, off, rows1 = KEYS[c]
            rows = [min(off + nk, P), rows1]
            pe.wait_ge(sg("sprob"), i + 1)
            for k in range(2):
                if rows[k]:
                    transposes(("spT", c, g, k), [(j * P, sp_prob[i % 2][:, j, k * P:k * P + rows[k]]) for j in range(4)])
            for k in range(2):
                if rows[k]:
                    read(pe, ("spT", c, g, k))
            out = start(("spv", c, g))
            for j in range(4):
                kv, par = 2 * g + j // 2, j % 2
                for k in range(2):
                    if not rows[k]:
                        continue
                    if c < 4:
                        v = qkv[0:rows[k], k, 1280 + kv * 64:1280 + (kv + 1) * 64]
                    else:
                        v = cvn[:, kv * 64:(kv + 1) * 64] if k == 0 else qkv[0:TS, 2, 1280 + kv * 64:1280 + (kv + 1) * 64]
                    ins = mm(out[par * 64:par * 64 + 64, (j // 2) * P:(j // 2 + 1) * P], v, sp_probT[i % 2][k][0:rows[k], j],
                             start=k == 0, stop=k == 1 or not rows[1])
            end(ins, ("spv", c, g))

        read(pe, ("qkT", 2, 4))
        for i, (c, g) in enumerate(GROUPS):
            k0, nk, off, rows1 = KEYS[c]
            for k in range(2):
                kv = 2 * g + k
                out = start(("ss", c, g, k))
                for par in range(2):
                    keys = kT2[:, kv, k0:k0 + nk] if c < 4 else kTs[:, kv, :]
                    ins = mm(out[:, par * 256 + off:par * 256 + off + nk], qT2[:, c, kv, par].rearrange("p hh t -> p (hh t)"), keys,
                             start=True, stop=True)
                end(ins, ("ss", c, g, k))
            if i:
                swa_tail(i - 1, *GROUPS[i - 1])
        swa_tail(9, *GROUPS[9])
        read(pe, ("spv", 4, 1))
        for m in range(KC):
            w = weights(pe, f"ao{m // 4}")
            project(("ao", m), w, 512, m % 4, hT, KC)
        norm(4)
        xattn(1)
        norm(5)
        for b, (t0, n) in enumerate(BLOCKS):
            out = start(("logit", b))
            for k in range(KC):
                pe.wait_ge(sg("h_ready"), 5 * KC + k + 1)
                ins = mm(out[0:n, 0:E], hT[:, k, t0:t0 + n], routr[:, k], start=k == 0, stop=k == KC - 1)
            end(ins, ("logit", b))
        for name, src in (("hnat", hT), ("xnat", xT)):
            for b, (t0, n) in enumerate(BLOCKS):
                for k in range(2):
                    transposes((name, b, k), [(i * P, src[:, 4 * k + i, t0:t0 + n]) for i in range(4)])
        pe.wait_ge(sg("chosen"), 3)
        for b, (t0, n) in enumerate(BLOCKS):
            out = start(("rank", b))
            for bb in range(b + 1):
                lhs = ones[:, 0:n] if bb < b else const[0:n, C_UT:C_UT + n]
                ins = mm(out[0:n, 0:E], lhs, chosen[0:BLOCKS[bb][1], bb], start=bb == 0, stop=bb == b)
            end(ins, ("rank", b))
        out = start("load")
        for b, (t0, n) in enumerate(BLOCKS):
            ins = mm(out[:, 0:E], ones[0:n, :], chosen[0:n, b], start=b == 0, stop=b == 2)
        end(ins, "load")
        assert not todo, todo[:3]
        for b in range(8):
            pe.wait_ge(bank_free[b], uses_of[b])

        def gather(i, half):
            for c in range(4):
                for b, (t0, n) in enumerate(BLOCKS):
                    ins = mm(GA[half][:, c * P:(c + 1) * P], hnat[0:n, b, (4 * half + c) * P:(4 * half + c + 1) * P],
                             onehot[0:n, b], start=b == 0, stop=b == 2)
            ins.then_inc(sg("gathered"), 1)

        def moe_pass(i, fills):
            pe.wait_ge(sg("xg_ready"), 2 * i + 2)
            for j in range(11):
                s = j % 4
                n_fill = fills * (3 if s < 3 else 2) + (j // 4 + 1)
                pe.wait_ge(sg(f"moe13_full{s}"), 32 * n_fill)
                pe.wait_ge(sg("hid_ready"), 11 * i + j + 1)
                for k in range(KC):
                    ins = mm(H, xg[:, k], WE[s][:, k].rearrange("p w n -> p (w n)"), start=k == 0, stop=k == KC - 1)
                ins.then_inc(sg("moe_h_done"), 1)
                if j:
                    moe_down(i, fills, j - 1)
                else:
                    pe.wait_ge(sg("gated"), 3 * i + 3)
                    pe.wait_ge(sg("scattered"), 6 * i + 1)
                    for b, (t0, n) in enumerate(BLOCKS):
                        ins = nc.tensor.transpose(O[0][:, t0:t0 + n], gated[0:n, b], ident[0:n, 0:n])
                    ins.then_inc(sg("scat_T"), 1)
                pe.wait_ge(sg("hid_ready"), 11 * i + j + 2)
                pe.wait_ge(sg("hidT_ready"), 11 * i + j + 1)
                for c in range(2):
                    ins = nc.tensor.transpose(TR[:, c * P:(c + 1) * P], hid[:, c * P:(c + 1) * P], ident)
                ins.then_inc(sg("hid_T"), 1)
            pe.wait_ge(sg("onehot"), 3 * i + 6)
            pe.wait_ge(sg("xg_ready"), 2 * i + 2)
            gather(i + 1, 0)
            moe_down(i, fills, 10)
            gather(i + 1, 1)
            pe.wait_ge(sg("scat_ready"), i + 1)
            for q in range(6):
                b, half = divmod(q, 2)
                t0, n = BLOCKS[b]
                pe.wait_ge(sg(f"ysb_ready{half}"), i + 2)
                if q >= 2:
                    pe.wait_ge(sg("scattered"), 6 * i + q)
                mm(O[q % 2][0:n, :], scat[:, t0:t0 + n], ysb[:, half * 512:(half + 1) * 512], start=True, stop=True) \
                    .then_inc(sg("scatter_done"), 1)

        def moe_down(i, fills, j):
            s = j % 4
            n_fill = fills * (3 if s < 3 else 2) + (j // 4 + 1)
            pe.wait_ge(sg(f"moe2_full{s}"), 16 * n_fill)
            pe.wait_ge(sg("hidT_ready"), 11 * i + j + 2)
            if j == 0:
                pe.wait_ge(sg("ysb_ready0"), i + 1)
                pe.wait_ge(sg("ysb_ready1"), i + 1)
            for c in range(2):
                for half in range(2):
                    ins = mm(Y[half], hidT[:, c], WD[s][:, c, half * 512:(half + 1) * 512],
                             start=j == 0 and c == 0, stop=j == 10 and c == 1, skip_group_check=True)
            ins.then_inc(sg("moe_y_done"), 1)

        read(pe, ("hnat", 2, 1))
        pe.wait_ge(sg("onehot"), 3)
        gather(0, 0)
        gather(0, 1)
        with pe.Fori(0, E) as i:
            moe_pass(i, i)
        pe.wait_ge(sg("flag_ready"), 1)
        overloaded = pe.value_load(flag[0:1, 0:1])
        with pe.If(overloaded > P):
            for r in (1, 2):
                with pe.Fori(0, E) as e:
                    moe_pass(e + E * r, e + E * r)

    @block.scalar
    def _(act):
        act.sem_inc(sg("ysb_ready0"), 1)
        A = nc.scalar.activation
        chain = [0]

        def link(ins):
            chain[0] += 1
            ins.then_inc(sg("act_chain"), 1)
            act.wait_ge(sg("act_chain"), chain[0])

        def head(x, h):
            return x[:, h * T:(h + 1) * T]

        def norm(n):
            source = [lambda c: read(act, ("xin", 2, 1)), lambda c: read(act, ("wo", c)), lambda c: read(act, ("xo", 0, c)),
                      lambda c: act.wait_ge(sg("ffn_out"), c + 2), lambda c: read(act, ("ao", c)),
                      lambda c: read(act, ("xo", 1, c))][n]
            if n:
                full(act, ("norm", n - 1))
            for c in range(KC):
                source(c)
                A(sq[:, c], xT[:, c], ACT.Square).then_inc(sg("sq_ready"), 1)
            out = full(act, ("norm", n))
            if n:
                act.wait_ge(sg("h_ready"), KC * n)
            root(("norm", n), rstd, out[:, 0:T]).then_inc(sg("rstd_ready"), 1)

        def root(key, out, x):
            b, n = use[key]
            A(out, x, ACT.Ln, bias=eps).then_inc(bank_free[b], 1)
            act.wait_ge(bank_free[b], n + 1)
            return A(out, out, ACT.Exp, scale=-0.5)

        act.wait_ge(sg("const_set"), 4)
        norm(0)
        act.wait_ge(sg("lb_pre"), 1)
        A(lb, lb, ACT.Exp).then_inc(sg("lb_exp"), 1)
        for h in range(4):
            out = full(act, ("f", h))
            A(head(G, h), out[:, 0:T], ACT.Sigmoid).then_inc(freed(("f", h)), 1)
        for h in range(4):
            out = full(act, ("q", h))
            A(head(qT, h), out[:, 0:T], ACT.Silu).then_inc(freed(("q", h)), 1)
        for h in range(4):
            act.wait_ge(sg("f_ready"), h + 1)
            A(head(X[1], h), head(kT, h), ACT.Ln).then_inc(sg("logf"), 1)
        act.wait_ge(sg("memn_loaded"), 16)
        for c in range(2):
            junk = mem_v_p[:, 0].rearrange("p c n -> p (c n)")
            link(A(junk, memn[:, c], ACT.Square, accum_out=stat[:, c:c + 1]))
        link(A(stat[:, 2:4], stat[:, 0:2], ACT.Ln, bias=eps, scale=1.0 / D))
        A(stat[:, 4:6], stat[:, 2:4], ACT.Exp, scale=-0.5).then_inc(sg("mem_rstd"), 1)

        def level(n):
            act.wait_ge(sg("level_pre"), n + 1)
            A(X[n % 3], X[n % 3], ACT.Exp).then_inc(sg("level_exp"), 1)

        level(0)
        for h in range(4):
            out = full(act, ("g", h))
            A(head(gateT, h), out[:, 0:T], ACT.Silu).then_inc(freed(("g", h)), 1)
        level(1)
        level(2)
        for h in range(4):
            out = full(act, ("v", h))
            A(head(vT, h), out[:, 0:T], ACT.Gelu_apprx_tanh).then_inc(freed(("v", h)), 1)
        for n in range(3, 6):
            level(n)
        for h in range(4):
            out = full(act, ("u", h))
            A(head(uT, h), out[:, 0:T], ACT.Gelu_apprx_tanh).then_inc(freed(("u", h)), 1)
        for g in range(4):
            read(act, ("mean", g))
            A(head(gsq, g), head(vT, g), ACT.Square).then_inc(sg("v_sq"), 1)
        for g in range(4):
            out = full(act, ("var", g))
            root(("var", g), head(gsq, g), out[:, 0:T]).then_inc(sg("v_rstd"), 1)
        full(act, ("att", 3, 2))
        A(X[0], G, ACT.Exp).then_inc(sg("start_exp"), 1)
        act.wait_ge(sg("end_pre"), 1)
        A(X[1], X[1], ACT.Exp).then_inc(sg("end_exp"), 1)
        A(gend, G.rearrange("p (c t) -> p c t", t=CH)[:, :, CH - 1], ACT.Exp).then_inc(sg("chunk_exp"), 1)
        for l in range(2):
            for c in range(2):
                out = full(act, ("ckT", l, c))
                A(mem_kT_s[:, l, :, c * P:(c + 1) * P], split(out, 4), ACT.Copy).then_inc(freed(("ckT", l, c)), 1)
            for c in range(2):
                act.wait_ge(sg("mk_squares"), 2 * l + c + 1)
                s = stat[:, 16 + 8 * (2 * l + c):24 + 8 * (2 * l + c)]
                link(A(s[:, 4:8], s[:, 0:4], ACT.Ln, bias=eps, scale=1.0 / P))
                A(s[:, 0:4], s[:, 4:8], ACT.Exp, scale=-0.5).then_inc(sg("mk_rstd"), 1)
            for c in range(2):
                out = full(act, ("memv", l, c))
                A(mem_v_p[:, l, c], out, ACT.Copy).then_inc(freed(("memv", l, c)), 1)
            for c in range(2):
                out = full(act, ("mkT", l, c))
                A(mem_kT_p[:, l, :, c * P:(c + 1) * P], split(out, 4), ACT.Copy).then_inc(freed(("mkT", l, c)), 1)
        for g in range(5):
            out = full(act, ("kp", g))
            A(kp[0:CH, 4 * g:4 * g + 4], split(out[0:CH, :], 4), ACT.Copy).then_inc(freed(("kp", g)), 1)
        for c in range(NCH):
            out = full(act, ("o", c))
            A(split(oT, 4)[:, :, c * CH:(c + 1) * CH], split(out[:, 0:256], 4), ACT.Copy).then_inc(freed(("o", c)), 1)
            act.wait_ge(freed(("o", c)), use[("o", c)][1] + 1)
        full(act, ("vn", 2))
        for h in range(4):
            A(head(vT, h), head(oT, h), ACT.Square).then_inc(sg("o_sq"), 1)
        for h in range(4):
            out = full(act, ("on", h))
            root(("on", h), head(vT, h), out[:, 0:T]).then_inc(sg("o_rstd"), 1)
        act.wait_ge(sg("out_written"), 16 * 7)
        norm(1)

        def xattn(l):
            for h in range(XH):
                out = full(act, ("xq", l, h))
                A(head(qx, h), out[:, 0:T], ACT.Copy).then_inc(freed(("xq", l, h)), 1)
                act.wait_ge(freed(("xq", l, h)), use[("xq", l, h)][1] + 1)
                A(head(xsq, h), head(qx, h), ACT.Square).then_inc(sg("xq_sq"), 1)
            for h in range(XH):
                out = full(act, ("xqn", l, h))
                root(("xqn", l, h), head(xsq, h), out[:, 0:T]).then_inc(sg("xq_rstd"), 1)

            def tail(b):
                t0, n = BLOCKS[b]
                key = ("xpT", l, b, 0)
                out = full(act, key)
                A(probT[b % 2][:, 0:4, 0:n], split(out, 4)[:, :, 0:n], ACT.Copy).then_inc(freed(key), 1)
                key = ("xpv", l, b)
                out = full(act, key)
                A(split(oxT, 4)[:, :, t0:t0 + n], split(out, 4)[:, :, 0:n], ACT.Copy).then_inc(freed(key), 1)

            for b, (t0, n) in enumerate(BLOCKS):
                st = xstat[b % 2]
                for k in range(2):
                    out = full(act, ("xs", l, b, k))
                    act.wait_ge(sg("xmax"), 2 * (3 * l + b) + k + 1)
                    for hh in range(2):
                        h = 2 * k + hh
                        ins = A(prob[b % 2][0:n, h], out[0:n, hh * MEM:(hh + 1) * MEM], ACT.Exp, scale=P ** -0.5,
                                bias=st[0:n, 4 + h:5 + h], accum_out=st[0:n, 8 + h:9 + h])
                    ins.then_inc(freed(("xs", l, b, k)), 1)
                if b:
                    tail(b - 1)
            tail(2)

        xattn(0)
        norm(2)
        with act.Fori(0, 11) as i:
            for s in range(2):
                act.wait_ge(sg(f"ffn_h1_{s}"), i + 1)
                act.wait_ge(sg(f"ffn_g{s}"), i + 1)
                A(sil[s], bank[2 * s][:, 0:T], ACT.Silu).then_inc(sg(f"ffn_sil{s}"), 1)
        norm(3)
        for b, (t0, n) in enumerate(BLOCKS):
            for u in range(3):
                key = ("qkv", b, u)
                out = full(act, key)
                A(qkv[0:n, b, u * 512:(u + 1) * 512], out[0:n], ACT.Copy).then_inc(freed(key), 1)
            act.wait_ge(sg("qk_squares"), b + 1)
            link(A(hstat[0:n, b, 24:44], hstat[0:n, b, 0:20], ACT.Ln, bias=eps[0:n], scale=1.0 / 64))
            A(hstat[0:n, b, 0:20], hstat[0:n, b, 24:44], ACT.Exp, scale=-0.5).then_inc(sg("qk_rstd"), 1)
        out = full(act, "cskT")
        A(kTs[:, :, 0:P], split(out[0:64], 4), ACT.Copy).then_inc(freed("cskT"), 1)
        for b, (t0, n) in enumerate(BLOCKS):
            for g in range(5):
                key = ("qkT", b, g)
                out = full(act, key)
                src = split(out[0:64], 4)[:, :, 0:n]
                if g < 4:
                    for cc in range(n // CH):
                        to = qT2[:, t0 // CH + cc, g].rearrange("p par hh t -> p hh par t")
                        of = src[:, :, cc * CH:(cc + 1) * CH].rearrange("p (hh par) t -> p hh par t", hh=2)
                        ins = A(to, of, ACT.Copy)
                    ins.then_inc(freed(key), 1)
                else:
                    if b == 2:
                        A(kTs[:, :, P:192], src, ACT.Copy).then_inc(sg("kTs_own"), 1)
                    A(kT2[:, :, t0:t0 + n], src, ACT.Copy).then_inc(freed(key), 1)

        def swa_tail(i, c, g):
            key = ("spT", c, g, 0)
            rows = min(KEYS[c][2] + KEYS[c][1], P)
            out = full(act, key)
            if i == 0:
                act.wait_ge(sg("out_written"), 16 * 11)
            A(sp_probT[i % 2][0][0:rows], split(out[0:rows], 4), ACT.Copy).then_inc(freed(key), 1)
            key = ("spv", c, g)
            out = full(act, key)
            A(hT[:, 4 * g:4 * g + 4, c * CH:(c + 1) * CH], split(out[:, 0:256], 4), ACT.Copy).then_inc(freed(key), 1)

        for i, (c, g) in enumerate(GROUPS):
            k0, nk, off, rows1 = KEYS[c]
            st = sstat[i % 2]
            for k in range(2):
                key = ("ss", c, g, k)
                out = full(act, key)
                act.wait_ge(sg("smax"), 2 * i + k + 1)
                if i == 0 and k == 0:
                    full(act, ("qkT", 2, 4))
                for par in range(2):
                    j = 2 * k + par
                    ins = A(sp_prob[i % 2][:, j, off:off + nk], out[:, par * 256 + off:par * 256 + off + nk], ACT.Exp,
                            scale=0.125, bias=st[:, 4 + j:5 + j], accum_out=st[:, 8 + j:9 + j])
                ins.then_inc(freed(key), 1)
            act.wait_ge(sg("sink_pre"), i + 1)
            A(st[:, 16:20], st[:, 12:16], ACT.Exp).then_inc(sg("sink_exp"), 1)
            if i:
                swa_tail(i - 1, *GROUPS[i - 1])
        swa_tail(9, *GROUPS[9])
        norm(4)
        xattn(1)
        norm(5)
        for b, (t0, n) in enumerate(BLOCKS):
            act.wait_ge(sg("gate_pre"), b + 1)
            A(gsel[0:n, b, 1:2], gsel[0:n, b, 0:1], ACT.Exp).then_inc(sg("gate_exp"), 1)
        for b, (t0, n) in enumerate(BLOCKS):
            for k in range(2):
                key = ("hnat", b, k)
                out = full(act, key)
                A(hnat[0:n, b, k * 512:(k + 1) * 512], out[0:n], ACT.Copy).then_inc(freed(key), 1)

        def xg_half(i, half):
            act.wait_ge(sg("gathered"), 2 * i + half + 1)
            A(xg[:, 4 * half:4 * half + 4], split(GA[half], 4), ACT.Copy).then_inc(sg("xg_ready"), 1)

        def moe_pass(i):
            for j in range(11):
                act.wait_ge(sg("moe_h_done"), 11 * i + j + 1)
                act.wait_ge(sg("hid_ready"), 11 * i + j + 1)
                A(act1, H[:, 0:256], ACT.Silu).then_inc(sg("act1_ready"), 1)
            xg_half(i + 1, 0)
            act.wait_ge(sg("moe_y_done"), 11 * i + 11)
            act.wait_ge(sg("scatter_done"), 6 * i + 1)
            A(ysb[:, 0:512], Y[0], ACT.Copy).then_inc(sg("ysb_ready0"), 1)
            xg_half(i + 1, 1)

        xg_half(0, 0)
        xg_half(0, 1)
        with act.Fori(0, E) as i:
            moe_pass(i)
        act.wait_ge(sg("flag_ready"), 1)
        overloaded = act.value_load(flag[0:1, 0:1])
        with act.If(overloaded > P):
            for r in (1, 2):
                with act.Fori(0, E) as e:
                    moe_pass(e + E * r)

    @block.vector
    def _(dve):
        for name in ("ffn_g0", "ffn_g1", "ffn_out", "hid_ready", "hidT_ready", "scattered", "ysb_ready1"):
            dve.sem_inc(sg(name), 1)
        V = nc.vector
        chain = [0]

        def link(ins):
            chain[0] += 1
            ins.then_inc(sg("dve_chain"), 1)
            dve.wait_ge(sg("dve_chain"), chain[0])

        def head(x, h):
            return x[:, h * T:(h + 1) * T]

        def norm(n):
            dve.wait_ge(sg("rstd_ready"), n + 1)
            for c in range(KC):
                g = prm[:, NORM_COL[n] + c:NORM_COL[n] + c + 1]
                V.scalar_tensor_tensor(hT[:, c], xT[:, c], g, rstd, ALU.mult, ALU.mult).then_inc(sg("h_ready"), 1)

        def residual(key, m):
            out = full(dve, key)
            V.tensor_tensor(xT[:, m], xT[:, m], out[:, 0:T], ALU.add).then_inc(freed(key), 1)

        out = full(dve, "prm")
        V.tensor_copy(prm[:, 0:NROW], out[:, 0:NROW]).then_inc(freed("prm"), 1)
        dve.wait_ge(freed("prm"), 1)
        for b, (t0, n) in enumerate(BLOCKS):
            for k in range(2):
                key = ("xin", b, k)
                out = full(dve, key)
                V.tensor_copy(xT[:, 4 * k:4 * k + 4, t0:t0 + n], split(out, 4)[:, :, 0:n]).then_inc(freed(key), 1)
        norm(0)
        V.tensor_tensor(lb, prm[:, R_LB1:R_LB1 + 4], prm[:, R_LB0:R_LB0 + 4], ALU.subtract).then_inc(sg("lb_pre"), 1)
        dve.wait_ge(sg("lb_exp"), 1)
        link(V.tensor_scalar(omlb, lb, 1.0, None, ALU.add))
        link(V.reciprocal(lb, omlb))
        link(V.tensor_scalar(omlb, lb, -1.0, 1.0, ALU.mult, ALU.add))
        for h in range(4):
            read(dve, ("f", h))
            V.tensor_scalar(head(kT, h), head(G, h), omlb[:, h:h + 1], lb[:, h:h + 1], ALU.mult, ALU.add) \
                .then_inc(sg("f_ready"), 1)
        for h in range(4):
            dve.wait_ge(sg("logf"), h + 1)
            V.tensor_scalar(head(kT, h), head(kT, h), -1.0, 1.0, ALU.mult, ALU.add).then_inc(sg("k_ready"), 1)
        dve.wait_ge(sg("scan_mask"), 1)
        link(V.tensor_tensor_scan(G, X[0], X[1], 0.0, ALU.mult, ALU.add))

        def level_pre(n):
            b = LEVELS[n]
            g = G.rearrange("p (n two b) -> p n two b", two=2, b=b)
            x = X[n % 3].rearrange("p (n two b) -> p n two b", two=2, b=b)
            mid = g[:, :, 0, b - 1:b].broadcast_to([P, HT // (2 * b), b])
            V.tensor_tensor(x[:, :, 0], mid, g[:, :, 0], ALU.subtract)
            ins = V.tensor_tensor(x[:, :, 1], g[:, :, 1], mid, ALU.subtract)
            ins.then_inc(sg("level_pre"), 1)

        def level_query(n):
            b = LEVELS[n]
            x = X[n % 3].rearrange("p (n two b) -> p n two b", two=2, b=b)[:, :, 1]
            q = qT.rearrange("p (n two b) -> p n two b", two=2, b=b)[:, :, 1]
            dve.wait_ge(sg("level_exp"), n + 1)
            V.tensor_tensor(x, x, q, ALU.mult).then_inc(sg("level_q"), 1)

        def level_scores(n):
            for g in range(3):
                key = ("att", n, g)
                out = full(dve, key)
                pairs = min(8, 20 - 8 * g)
                o = split(att[0:CH, g * 512:g * 512 + pairs * CH], pairs)
                mask = const[0:CH, C_LEV + n * CH:C_LEV + (n + 1) * CH].unsqueeze(1).broadcast_to([CH, pairs, CH])
                if n:
                    read(dve, ("att", n - 1, g))
                V.copy_predicated(o, mask.bitcast(U32), split(out[0:CH, 0:pairs * CH], pairs)).then_inc(freed(key), 1)

        level_pre(0)
        link(V.memset(att[0:CH, :], 0.0))
        for h in range(4):
            out = full(dve, ("i", h))
            V.tensor_copy(head(iT, h), out[:, 0:T]).then_inc(freed(("i", h)), 1)
        level_pre(1)
        level_pre(2)
        for g in range(5):
            key = ("iT", g)
            out = full(dve, key)
            V.tensor_copy(vb[0:CH, 4 * g:4 * g + 4], split(out[0:CH], 4)).then_inc(freed(key), 1)
        dve.wait_ge(sg("mem_rstd"), 1)
        for c in range(2):
            V.tensor_scalar(memn[:, c], memn[:, c], stat[:, 4 + c:5 + c], None, ALU.mult).then_inc(sg("memn_scaled"), 1)
        for n in range(3):
            level_query(n)
        for n in range(3):
            level_scores(n)
            level_pre(n + 3)
        for n in range(3, 6):
            level_query(n)
        for g in range(4):
            key = ("mean", g)
            out = full(dve, key)
            V.tensor_tensor(head(vT, g), head(vT, g), out[:, 0:T], ALU.subtract).then_inc(freed(key), 1)
        level_scores(3)
        for n in range(4, 6):
            level_scores(n)
        gc = G.rearrange("p (c t) -> p c t", t=CH)
        V.tensor_tensor(X[1].rearrange("p (c t) -> p c t", t=CH), gc[:, :, CH - 1:CH].broadcast_to([P, 20, CH]), gc,
                        ALU.subtract).then_inc(sg("end_pre"), 1)
        level_scores(6)
        dve.wait_ge(sg("start_exp"), 1)
        V.tensor_tensor(qT, qT, X[0], ALU.mult).then_inc(sg("qp_ready"), 1)
        for g in range(4):
            dve.wait_ge(sg("v_rstd"), g + 1)
            link(V.scalar_tensor_tensor(head(vT, g), head(vT, g), prm[:, R_LNG + g:R_LNG + g + 1], head(gsq, g),
                                        ALU.mult, ALU.mult))
            V.tensor_scalar(head(vT, g), head(vT, g), prm[:, R_LNB + g:R_LNB + g + 1], None, ALU.add) \
                .then_inc(sg("vn_ready"), 1)
        out = full(dve, "wsT")
        tril = const[:, C_TRIL:C_TRIL + P].unsqueeze(1).broadcast_to([P, 4, P])
        V.tensor_tensor(wsT, split(out, 4), tril, ALU.mult).then_inc(freed("wsT"), 1)
        dve.wait_ge(sg("small_loaded"), 96)
        dve.wait_ge(sg("qp_ready"), 1)
        dve.wait_ge(sg("vn_ready"), 4)
        for l in range(2):
            for g in range(4):
                c, k = divmod(g, 2)
                key = ("mT", l, g)
                out = full(dve, key)
                if g == 0:
                    full(dve, ("memv", 0, 1) if l else ("u", 3))
                gain = prm[:, R_MEM + 8 * l + 4 * k:R_MEM + 8 * l + 4 * k + 4].unsqueeze(2).broadcast_to([P, 4, P])
                V.tensor_tensor(hT[:, 4 * k:4 * k + 4, c * P:(c + 1) * P], split(out, 4), gain, ALU.mult) \
                    .then_inc(freed(key), 1)
            for c in range(2):
                key = ("memk", l, c)
                out = full(dve, key)
                y = mkn[l][:, c]
                junk = iT[:, 0:512]
                s = stat[:, 16 + 8 * (2 * l + c):24 + 8 * (2 * l + c)]
                V.tensor_copy(y, out).then_inc(freed(key), 1)
                dve.wait_ge(freed(key), use[key][1] + 1)
                link(V.tensor_tensor(junk, y, y, ALU.mult))
                V.reduce_sum(s[:, 0:4], split(junk, 4), axis=AX.X).then_inc(sg("mk_squares"), 1)
                dve.wait_ge(sg("mk_rstd"), 2 * l + c + 1)
                link(V.tensor_tensor(split(y, 4), split(y, 4), s[:, 0:4].unsqueeze(2).broadcast_to([P, 4, P]), ALU.mult))
                V.tensor_tensor(split(y, 4), split(y, 4), kg[:, l].unsqueeze(1).broadcast_to([P, 4, P]), ALU.mult) \
                    .then_inc(sg("mk_ready"), 1)
        for b, (t0, n) in enumerate(BLOCKS):
            key = ("vn", b)
            out = full(dve, key)
            V.tensor_copy(vnat[0:n, b], out[0:n]).then_inc(freed(key), 1)
        for g in range(4):
            key = ("gate", g)
            out = full(dve, key)
            V.tensor_tensor(hT[:, g], head(uT, g), out[:, 0:T], ALU.mult).then_inc(freed(key), 1)
        dve.wait_ge(sg("chunk_exp"), 1)
        dve.wait_ge(sg("state_loaded"), 16)
        for c in range(NCH):
            key = ("S", c)
            out = full(dve, key)
            if c:
                full(dve, ("o", c))
            if 1 <= c < 4:
                read(dve, ("S", c - 1))
            for h in range(4):
                S = Ss if c == 4 else Sp
                hc = h * NCH + c
                if c == 0:
                    ins = V.tensor_copy(S[:, h], out[:, h * P:(h + 1) * P])
                else:
                    ins = V.scalar_tensor_tensor(S[:, h], S[:, h], gend[:, hc:hc + 1], out[:, h * P:(h + 1) * P],
                                                 ALU.mult, ALU.add)
            ins.then_inc(freed(key), 1)
        for h in range(4):
            dve.wait_ge(sg("o_rstd"), h + 1)
            link(V.scalar_tensor_tensor(head(vT, h), head(oT, h), prm[:, R_OUT:R_OUT + 1], head(vT, h), ALU.mult, ALU.mult))
            V.tensor_tensor(hT[:, 4 + h], head(vT, h), head(gateT, h), ALU.mult).then_inc(sg("mixed"), 1)
        for m in range(KC):
            residual(("wo", m), m)
        norm(1)

        def xattn(l):
            for h in range(XH):
                dve.wait_ge(sg("xq_rstd"), 4 * l + h + 1)
                V.scalar_tensor_tensor(head(qn, h), head(qx, h), prm[:, R_XQ + l:R_XQ + l + 1], head(xsq, h),
                                       ALU.mult, ALU.mult).then_inc(sg("xq_ready"), 1)

            def tail(b):
                t0, n = BLOCKS[b]
                key = ("xpT", l, b, 1)
                out = full(dve, key)
                V.tensor_copy(probT[b % 2][:, 4:8, 0:n], split(out, 4)[:, :, 0:n]).then_inc(freed(key), 1)

            for b, (t0, n) in enumerate(BLOCKS):
                st = xstat[b % 2]
                for k in range(2):
                    out = full(dve, ("xs", l, b, k))
                    link(V.reduce_max(st[0:n, 2 * k:2 * k + 2], split(out[0:n], 2), axis=AX.X))
                    V.tensor_scalar(st[0:n, 4 + 2 * k:6 + 2 * k], st[0:n, 2 * k:2 * k + 2], -(P ** -0.5), None, ALU.mult) \
                        .then_inc(sg("xmax"), 1)
                for k in range(2):
                    key = ("xs", l, b, k)
                    dve.wait_ge(freed(key), use[key][1] + 1)
                link(V.reciprocal(st[0:n, 12:16], st[0:n, 8:12]))
                V.tensor_tensor(prob[b % 2][0:n], prob[b % 2][0:n], st[0:n, 12:16].unsqueeze(2).broadcast_to([n, 4, MEM]),
                                ALU.mult).then_inc(sg("xprob"), 1)
                if b:
                    tail(b - 1)
            tail(2)
            for m in range(KC):
                residual(("xo", l, m), m)

        xattn(0)
        norm(2)
        with dve.Fori(0, 11) as i:
            for s in range(2):
                dve.wait_ge(sg(f"ffn_sil{s}"), i + 1)
                dve.wait_ge(sg("ffn_h_done"), 2 * i + s + 1)
                V.tensor_tensor(gT[:, bass.ds(2 * i + s, 1)].rearrange("p o n -> p (o n)"), sil[s], bank[2 * s + 1][:, 0:T],
                                ALU.mult).then_inc(sg(f"ffn_g{s}"), 1)
        with dve.Fori(0, 2) as i:
            for q in range(2):
                for t in range(2):
                    dve.wait_ge(sg("ffn_y"), 4 * i + 2 * q + t + 1)
                    x = xT[:, bass.ds(4 * i + 2 * q + t, 1)].rearrange("p o n -> p (o n)")
                    V.tensor_tensor(x, x, bank[4 + 2 * q + t][:, 0:T], ALU.add).then_inc(sg("ffn_out"), 1)
        norm(3)
        for b, (t0, n) in enumerate(BLOCKS):
            read(dve, ("qkv", b, 2))
            x = qkv[0:n, b, 0:1280]
            if b:
                dve.wait_ge(sg("rot_done"), 2 * b)
            link(V.tensor_tensor(rot[0:n, b], x, x, ALU.mult))
            V.reduce_sum(hstat[0:n, b, 0:20], rot[0:n, b].rearrange("p (h d) -> p h d", d=64), axis=AX.X) \
                .then_inc(sg("qk_squares"), 1)
            dve.wait_ge(sg("qk_rstd"), b + 1)
            heads = x.rearrange("p (h d) -> p h d", d=64)
            V.tensor_tensor(heads, heads, hstat[0:n, b, 0:20].unsqueeze(2).broadcast_to([n, 20, 64]), ALU.mult) \
                .then_inc(sg("qk_scaled"), 1)
            dve.wait_ge(sg("qk_scaled"), b + 1)
            dve.wait_ge(sg("rope_tables"), 12)
            r = rot[0:n, b].rearrange("p (h d) -> p h d", d=64)
            m = rtmp[0:n].rearrange("p (h d) -> p h d", d=64)
            for h0, nh, f in ((0, 16, 0), (16, 4, 2)):
                ins = V.tensor_tensor(r[:, h0:h0 + nh], heads[:, h0:h0 + nh],
                                      gcs[0:n, b, f].unsqueeze(1).broadcast_to([n, nh, 64]), ALU.mult)
            link(ins)
            dve.wait_ge(sg("sine_ready"), 2 * b + 2)
            V.tensor_tensor(r[:, :, 0:32], r[:, :, 0:32], m[:, :, 32:64], ALU.subtract).then_inc(sg("rot_done"), 1)
            V.tensor_tensor(r[:, :, 32:64], r[:, :, 32:64], m[:, :, 0:32], ALU.add).then_inc(sg("rot_done"), 1)

        def swa_tail(i, c, g):
            if not KEYS[c][3]:
                return
            key = ("spT", c, g, 1)
            out = full(dve, key)
            rows = KEYS[c][3]
            dve.wait_ge(sg("out_written"), 16 * 11)
            V.tensor_copy(sp_probT[i % 2][1][0:rows], split(out[0:rows], 4)).then_inc(freed(key), 1)

        for i, (c, g) in enumerate(GROUPS):
            k0, nk, off, rows1 = KEYS[c]
            st = sstat[i % 2]
            pr = sp_prob[i % 2]
            for k in range(2):
                key = ("ss", c, g, k)
                out = full(dve, key)
                link(V.reduce_max(st[:, 2 * k:2 * k + 2], split(out, 2)[:, :, off:off + nk], axis=AX.X))
                sink = sinkc[:, 4 * g + 2 * k:4 * g + 2 * k + 2]
                link(V.scalar_tensor_tensor(st[:, 2 * k:2 * k + 2], st[:, 2 * k:2 * k + 2], 0.125, sink, ALU.mult, ALU.max))
                V.tensor_scalar(st[:, 4 + 2 * k:6 + 2 * k], st[:, 2 * k:2 * k + 2], -1.0, None, ALU.mult) \
                    .then_inc(sg("smax"), 1)
            dve.wait_ge(sg("smax"), 2 * i + 2)
            V.tensor_tensor(st[:, 12:16], st[:, 4:8], sinkc[:, 4 * g:4 * g + 4], ALU.add).then_inc(sg("sink_pre"), 1)
            dve.wait_ge(sg("sink_exp"), i + 1)
            for k in range(2):
                key = ("ss", c, g, k)
                dve.wait_ge(freed(key), use[key][1] + 1)
            link(V.tensor_tensor(st[:, 12:16], st[:, 8:12], st[:, 16:20], ALU.add))
            link(V.reciprocal(st[:, 20:24], st[:, 12:16]))
            if off:
                V.memset(pr[:, :, 0:off], 0.0)
            V.tensor_tensor(pr[:, :, off:off + nk], pr[:, :, off:off + nk],
                            st[:, 20:24].unsqueeze(2).broadcast_to([P, 4, nk]), ALU.mult).then_inc(sg("sprob"), 1)
            if i:
                swa_tail(i - 1, *GROUPS[i - 1])
        swa_tail(9, *GROUPS[9])
        for m in range(KC):
            residual(("ao", m), m)
        norm(4)
        xattn(1)
        norm(5)
        for b, (t0, n) in enumerate(BLOCKS):
            key = ("logit", b)
            out = full(dve, key)
            V.tensor_copy(logit[0:n, b], out[0:n, 0:E]).then_inc(freed(key), 1)
            dve.wait_ge(freed(key), use[key][1] + 1)
            link(V.max(top8[0:n, b], logit[0:n, b]))
            link(V.max_index(idx8[0:n, b].bitcast(U32), top8[0:n, b], logit[0:n, b]))
            link(V.tensor_copy(idxf[0:n, b], idx8[0:n, b].bitcast(U32)))
            for k in range(2):
                ins = V.tensor_scalar(eq[0:n, b, k], const[0:n, C_IOTA:C_IOTA + E], idxf[0:n, b, k:k + 1], None,
                                      ALU.is_equal)
            link(ins)
            V.tensor_tensor(gsel[0:n, b, 0:1], top8[0:n, b, 1:2], top8[0:n, b, 0:1], ALU.subtract) \
                .then_inc(sg("gate_pre"), 1)
            V.tensor_tensor(chosen[0:n, b], eq[0:n, b, 0], eq[0:n, b, 1], ALU.add).then_inc(sg("chosen"), 1)
        for b, (t0, n) in enumerate(BLOCKS):
            dve.wait_ge(sg("gate_exp"), b + 1)
            s = gsel[0:n, b]
            link(V.tensor_scalar(s[:, 2:3], s[:, 1:2], 1.0, None, ALU.add))
            link(V.reciprocal(s[:, 3:4], s[:, 2:3]))
            link(V.tensor_tensor(s[:, 0:1], s[:, 1:2], s[:, 3:4], ALU.mult))
            link(V.tensor_scalar(logit[0:n, b], eq[0:n, b, 0], s[:, 3:4], None, ALU.mult))
            link(V.scalar_tensor_tensor(logit[0:n, b], eq[0:n, b, 1], s[:, 0:1], logit[0:n, b], ALU.mult, ALU.add))
            times = PASSES // E + 1
            link(V.tensor_copy(gates[0:n, b].rearrange("p (r e) -> p r e", e=E),
                               logit[0:n, b].unsqueeze(1).broadcast_to([n, times, E])))
        for b, (t0, n) in enumerate(BLOCKS):
            for k in range(2):
                key = ("xnat", b, k)
                out = full(dve, key)
                V.tensor_copy(xnat[0:n, b, k * 512:(k + 1) * 512], out[0:n]).then_inc(freed(key), 1)
        for b, (t0, n) in enumerate(BLOCKS):
            key = ("rank", b)
            out = full(dve, key)
            link(V.scalar_tensor_tensor(rank[0:n, b], out[0:n, 0:E], 1.0, chosen[0:n, b], ALU.add, ALU.mult))
            V.tensor_scalar(rank[0:n, b], rank[0:n, b], -1.0, None, ALU.add).then_inc(freed(key), 1)
            dve.wait_ge(freed(key), use[key][1] + 1)
            times = PASSES // E + 1
            base = const[0:n, C_BASE:C_BASE + PASSES + 8].rearrange("p (r e) -> p r e", e=E)
            link(V.tensor_tensor(slot[0:n, b].rearrange("p (r e) -> p r e", e=E),
                                 rank[0:n, b].unsqueeze(1).broadcast_to([n, times, E]), base, ALU.subtract))
        out = full(dve, "load")
        link(V.tensor_copy(load, out[:, 0:E]))
        V.reduce_max(maxload, load, axis=AX.X).then_inc(freed("load"), 1)
        dve.wait_ge(freed("load"), use["load"][1] + 1)
        V.tensor_copy(flag[0:1, 0:1], maxload[0:1, :]).then_inc(sg("flag_ready"), 1)

        iota = const[:, C_IOTA:C_IOTA + P]

        def columns(i):
            for b, (t0, n) in enumerate(BLOCKS):
                V.tensor_scalar(onehot[0:n, b], iota[0:n], slot[0:n, b, bass.ds(i, 1)], None, ALU.is_equal) \
                    .then_inc(sg("onehot"), 1)

        for b, (t0, n) in enumerate(BLOCKS):
            V.tensor_scalar(onehot[0:n, b], iota[0:n], slot[0:n, b, 0:1], None, ALU.is_equal).then_inc(sg("onehot"), 1)

        def moe_pass(i):
            dve.wait_ge(sg("scat_T"), i + 1)
            for b, (t0, n) in enumerate(BLOCKS):
                V.tensor_scalar(gated[0:n, b], iota[0:n], slot[0:n, b, bass.ds(i, 1)], gates[0:n, b, bass.ds(i, 1)],
                                ALU.is_equal, ALU.mult).then_inc(sg("gated"), 1)
            for j in range(11):
                dve.wait_ge(sg("act1_ready"), 11 * i + j + 1)
                dve.wait_ge(sg("hid_T"), 11 * i + j + 1)
                V.tensor_tensor(hid, act1, H[:, 256:512], ALU.mult).then_inc(sg("hid_ready"), 1)
                dve.wait_ge(sg("hid_T"), 11 * i + j + 2)
                V.tensor_copy(hidT, split(TR[:, 0:256], 2)).then_inc(sg("hidT_ready"), 1)
                if j == 1:
                    dve.wait_ge(sg("scat_T"), i + 2)
                    dve.wait_ge(sg("scatter_done"), 6 * i + 1)
                    V.tensor_copy(scat, O[0][:, 0:T]).then_inc(sg("scat_ready"), 1)
                if j == 2:
                    dve.wait_ge(sg("gathered"), 2 * i + 2)
                    columns(i + 1)
            dve.wait_ge(sg("moe_y_done"), 11 * i + 11)
            dve.wait_ge(sg("scatter_done"), 6 * i + 1)
            V.tensor_copy(ysb[:, 512:1024], Y[1]).then_inc(sg("ysb_ready1"), 1)
            for q in range(6):
                b, half = divmod(q, 2)
                t0, n = BLOCKS[b]
                dve.wait_ge(sg("scatter_done"), 6 * i + q + 2)
                x = xnat[0:n, b, half * 512:(half + 1) * 512]
                V.tensor_tensor(x, x, O[q % 2][0:n, :], ALU.add).then_inc(sg("scattered"), 1)

        with dve.Fori(0, E) as i:
            moe_pass(i)
        dve.wait_ge(sg("flag_ready"), 1)
        dve.wait_ge(sg("scattered"), 6 * E + 1)
        overloaded = dve.value_load(flag[0:1, 0:1])
        with dve.If(overloaded > P):
            for r in (1, 2):
                with dve.Fori(0, E) as e:
                    moe_pass(e + E * r)
            dve.wait_ge(sg("scattered"), 6 * PASSES + 1)
        V.memset(maxload, 0.0).then_inc(sg("y_final"), 1)

    ctx.close()


OUTS = [("y_prompt", (1, TP, D)), ("y_sample", (1, TS, D)),
        ("mem_k_prompt", (2, 1, MEM, 4, 128)), ("mem_v_prompt", (2, 1, MEM, 4, 128)),
        ("hgrn_state_prompt", (1, 1, 4, 128, 128)), ("gmlp_v_sample", (1, 1, TS, 4, 128)),
        ("hgrn_state_sample", (1, 1, 4, 128, 128)),
        ("swa_k_prompt", (1, 1, 128, 4, 64)), ("swa_v_prompt", (1, 1, 128, 4, 64)),
        ("swa_k_sample", (1, 1, TS, 4, 64)), ("swa_v_sample", (1, 1, TS, 4, 64))]


def kernel(**inputs):
    import concourse.bacc as bacc
    from concourse.bass_utils import run_bass_kernel_spmd

    nc = bacc.Bacc("TRN2", target_bir_lowering=False, num_devices=1)
    arrays, a = {}, {}
    for name, x in list(inputs.items()) + [("shape_constants", constants())]:
        x = np.ascontiguousarray(x)
        arrays[f"in_{name}"] = x
        a[name] = nc.dram_tensor(f"in_{name}", x.shape, mybir.dt.from_np(x.dtype), kind="ExternalInput").ap()
    for name, shape in OUTS:
        a[name] = nc.dram_tensor(f"out_{name}", shape, F32, kind="ExternalOutput").ap()
    build(nc, a)
    r = run_bass_kernel_spmd(nc, [arrays], core_ids=[0])
    return tuple(r.results[0][f"out_{name}"] for name, _ in OUTS)
```

```python
from contextlib import ExitStack

import numpy as np
import concourse.bass as bass
from concourse import mybir

F32 = mybir.dt.float32
F32R = mybir.dt.float32r
I32 = mybir.dt.int32
U32 = mybir.dt.uint32
ALU = mybir.AluOpType
ACT = mybir.ActivationFunctionType
AX = mybir.AxisListType

P = 128
D = 1024
KC = D // P
TP = 256
TS = 64
T = TP + TS
BLOCKS = [(0, 128), (128, 128), (256, 64)]
MEM = 256
XH = 4
FF = 2816
FC = FF // P
E = 8
EPS = 1e-6
CH = 64
NCH = T // CH
HT = 4 * T
LEVELS = (32, 16, 8, 4, 2, 1)
ARENA = 53200
PASSES = 3 * E

C_ID, C_UT, C_TRIL, C_IOTA, C_LEV = 0, 128, 256, 384, 512
C_COS = C_LEV + 7 * 64
C_SIN = C_COS + 3 * 32
C_BASE = C_SIN + 3 * 32
NCONST = C_BASE + PASSES + 8

R_MIX, R_XAT, R_FFN, R_MEM, R_LNG, R_LNB, R_LB0, R_LB1, R_OUT, R_XQ = 0, 16, 32, 48, 64, 68, 72, 76, 80, 81
NROW = 83
NORM_COL = [R_MIX, R_XAT, R_FFN, R_MIX + 8, R_XAT + 8, R_FFN + 8]


def constants():
    c = np.zeros((P, NCONST), np.float32)
    r = np.arange(P)
    c[:, C_ID:C_ID + P] = np.eye(P)
    c[:, C_UT:C_UT + P] = r[:, None] < r[None, :]
    c[:, C_TRIL:C_TRIL + P] = r[:, None] <= r[None, :]
    c[:, C_IOTA:C_IOTA + P] = r[None, :]
    s, t = np.arange(CH)[:, None], np.arange(CH)[None, :]
    for n, b in enumerate(LEVELS):
        m = (s // (2 * b) == t // (2 * b)) & (s % (2 * b) < b) & (t % (2 * b) >= b)
        c[:CH, C_LEV + n * CH:C_LEV + (n + 1) * CH] = m
    c[:CH, C_LEV + 6 * CH:C_LEV + 7 * CH] = s == t
    half = 32
    inv = np.float32(1.0) / np.power(np.float32(10000.0), np.arange(half, dtype=np.float32) / np.float32(half))
    pos = np.concatenate([np.arange(TP), 512 + np.arange(TS)]).astype(np.float32)
    ang = (pos[:, None] * inv[None, :]).astype(np.float32)
    for b, (t0, n) in enumerate(BLOCKS):
        c[:n, C_COS + b * half:C_COS + (b + 1) * half] = np.cos(ang[t0:t0 + n])
        c[:n, C_SIN + b * half:C_SIN + (b + 1) * half] = np.sin(ang[t0:t0 + n])
    c[:, C_BASE:C_BASE + PASSES + 8] = P * (np.arange(PASSES + 8) // E)[None, :]
    return c


def build(nc, a):
    ctx = ExitStack()
    arena_at = -(-nc.sbuf_base // 32) * 32
    ctx.enter_context(nc.sbuf_tensor("arena", [P, ARENA], F32))
    flag = ctx.enter_context(nc.sbuf_tensor("flag", [1, 1], I32))
    bank = [ctx.enter_context(nc.psum_tensor(f"bank{b}", [P, 512], F32))[:, :] for b in range(8)]
    bank_full = [ctx.enter_context(nc.semaphore(f"bank_full{b}")) for b in range(8)]
    bank_free = [ctx.enter_context(nc.semaphore(f"bank_free{b}")) for b in range(8)]
    named = {}

    def sg(name):
        if name not in named:
            named[name] = ctx.enter_context(nc.semaphore(name))
        return named[name]

    top, views = [0], [0]

    def view(at, n, rows=P, dtype=F32, name="view"):
        assert at + n <= ARENA, at + n
        views[0] += 1
        return nc.alloc_sbuf_tensor_at(f"{name}_{views[0]}", [P, n], dtype, offset=arena_at + 4 * at)[0:rows, :]

    def take(n, rows=P):
        top[0] = -(-top[0] // 8) * 8 + n
        return view(top[0] - n, n, rows)

    def take_r(name, n):
        top[0] = -(-top[0] // 8) * 8 + n
        return view(top[0] - n, n, dtype=F32R, name=name)

    def split(ap, k):
        return ap.rearrange("p (k n) -> p k n", k=k)

    const = take(NCONST)
    ident = const[:, C_ID:C_ID + P]
    prow = take(P)
    prm = take(96)
    ones = take(P)
    ones_d = take(P)
    ones_h = take(P)
    eps = take(1)
    lb = take(4)
    omlb = take(4)
    kg = split(take(2 * P), 2)
    qkg = split(take(2 * 64), 2)
    sinkc = take(8)
    rstd = take(T)
    stat = take(64)
    routr = split(take(KC * E), KC)
    top[0] = -(-top[0] // 8) * 8
    x_region = top[0]
    xT = split(take(KC * T), KC)
    hT = split(take(KC * T), KC)
    ring_at = top[0]
    RING = [take(4096) for _ in range(3)]
    mem_kT_p = take(2 * 4 * MEM).rearrange("p (l h m) -> p l h m", l=2, h=XH)
    mem_kT_s = take(2 * 4 * MEM).rearrange("p (l h m) -> p l h m", l=2, h=XH)
    mem_v_p = take(2 * 2 * 512).rearrange("p (l c n) -> p l c n", l=2, c=2)
    mem_v_s = take(2 * 2 * 512).rearrange("p (l c n) -> p l c n", l=2, c=2)
    work = top[0]

    qT = take(HT)
    kT = take(HT)
    G = take(HT)
    gateT = take(HT)
    iT = take(HT)
    vT = take(HT)
    uT = take(HT)
    X = [take(HT) for _ in range(3)]
    att = take(HT)
    gsq = take(HT)
    vb = split(take(20 * P), 20)
    kp_at = top[0]
    kp = split(take(20 * P), 20)
    vnat = split(take(3 * 512), 3)
    ws = split(take(512), 4)
    wsT = split(take(512), 4)
    bsr = take(512, 1)
    Sp = split(take(512), 4)
    Ss = split(take(512), 4)
    gend = take(20)
    sq = split(view(work + 7 * HT, KC * T), KC)
    oT = X[2]
    memn = split(view(kp_at, 2 * D), 2)
    mkn = [split(gsq[:, 0:2 * 512], 2), split(X[0][:, 0:2 * 512], 2)]
    xin = split(view(work + 2 * HT, 3 * D), 3)

    top[0] = kp_at
    h0_parts = [split(take_r(f"h0_{r}", KC * T), KC) for r in range(2)]
    e_tiles = []
    for i in range(2):
        top[0] = ring_at + 3 * 4096 + (i + 1) * 2048
        e_tiles.append([take_r(f"e_tile{i}_{r}", 1024) for r in range(2)])
    top[0] = work
    qx = take(HT)
    qn = take(HT)
    xsq = take(HT)
    oxT = [split(take_r(f"oxT{r}", HT), 4) for r in range(2)]
    prob = [split(take(4 * MEM), 4) for _ in range(2)]
    probT = [split(take(8 * P), 8) for _ in range(2)]
    xstat = [take(16) for _ in range(2)]
    assert top[0] <= work + 9 * HT
    x_tiles = []
    for at in (work + 9 * HT, kp_at + 20 * P):
        top[0] = at
        x_tiles.append([take_r(f"x_tile{len(x_tiles)}_{r}", 1024) for r in range(2)])
    top[0] = work
    sil = [take(T) for _ in range(2)]
    g_raw = [take(T) for _ in range(2)]
    gT = [split(take_r(f"gT{r}", FC * T), FC) for r in range(2)]
    assert top[0] <= kp_at - 20 * P
    top[0] = kp_at - 20 * P
    hT_parts = [split(take_r(f"hT{r}", KC * T), KC) for r in range(2)]
    w2_at = top[0]
    W2S = [view(at, 11 * 256).rearrange("p (k n) -> p k n", k=11) for at in (w2_at, ring_at)]
    W13 = [RING[0][:, s * 2048:(s + 1) * 2048] for s in range(2)]
    w_parts = [None, None]
    top[0] = ring_at + 4096
    for s in (1, 0):
        w_parts[s] = [take_r(f"ffn_w{s}_{r}", 2048) for r in range(2)]
    top[0] = work + 9 * HT
    qkv = split(take(3 * 1536), 3)
    rot = split(take(3 * 1280), 3)
    rtmp = take(1280)
    top[0] = max(top[0], ARENA - (2 * 256 + 3 * 4 * 64 + 3 * 48))
    assert top[0] >= w2_at + 11 * 256
    ckn = take(256)
    cvn = take(256)
    gcs = take(3 * 4 * 64).rearrange("p (b f n) -> p b f n", b=3, f=4)
    hstat = split(take(3 * 48), 3)
    assert top[0] <= ARENA, top[0]
    top[0] = work
    qT2 = take(16 * T, 64).rearrange("p (c kv par hh t) -> p c kv par hh t", c=NCH, kv=4, par=2, hh=2)
    kT2 = split(take(4 * T, 64), 4)
    ao_tiles = [[take_r(f"ao_tile0_{r}", 1024) for r in range(2)]]
    assert top[0] <= work + 7 * HT
    kTs = split(take(4 * 192, 64), 4)
    sp_prob = [split(take(4 * 256), 4) for _ in range(2)]
    assert top[0] <= work + 9 * HT
    ao_tiles.append([])
    for r in range(2):
        top[0] = work + 9 * HT + 1536 * r
        ao_tiles[1].append(take_r(f"ao_tile1_{r}", 1024))
    top[0] = work + 9 * HT + 3 * 1536
    sp_probT = [[split(take(4 * P), 4) for _ in range(2)] for _ in range(2)]
    sstat = [take(24) for _ in range(2)]
    o2T = [split(take_r(f"o2T{r}", KC * T), KC) for r in range(2)]
    assert top[0] <= ARENA - (2 * 256 + 3 * 4 * 64 + 3 * 48)
    WE = [view(ring_at + s * 6144, 4096) for s in range(3)]
    WD = [view(ring_at + s * 6144 + 4096, 2048) for s in range(3)]
    top[0] = ring_at + 3 * 6144
    part = [[take_r(f"part{q}_{r}", 2048) for r in range(2)] for q in range(3)]
    hnat = [split(take_r(f"hnat{r}", 3 * D), 3) for r in range(2)]
    xnat = split(take(3 * D), 3)
    xg = [split(take_r(f"xg{r}", KC * P), KC) for r in range(2)]
    logit = split(take(24), 3)
    top8 = split(take(24), 3)
    idx8 = split(take(24), 3)
    idxf = split(take(24), 3)
    eq = take(48).rearrange("p (b k e) -> p b k e", b=3, k=2)
    gsel = take(12).rearrange("p (b n) -> p b n", b=3)
    chosen = split(take(24), 3)
    gates = split(take(3 * (PASSES + 8)), 3)
    slot = split(take(3 * (PASSES + 8)), 3)
    rank = split(take(24), 3)
    load = take(8)
    maxload = take(1)
    gslot = take(1)
    assert top[0] <= ARENA, top[0]
    top[0] = x_region
    ysb = [take_r(f"ysb{r}", D) for r in range(2)]
    act1 = take(256)
    hid = take(256)
    assert top[0] <= x_region + KC * T
    top[0] = x_region + KC * T
    xsel = [take(512) for _ in range(2)]
    hidT = [split(take_r(f"hidT{r}", 256), 2) for r in range(2)]
    onehot = split(take_r("onehot", 3 * P), 3)
    scat = split(take_r("scat", 3 * P), 3)
    assert top[0] <= x_region + 2 * KC * T
    assert top[0] <= ARENA, top[0]

    KEYS = [(0, 64, 0, 0), (0, 128, 0, 0), (0, 192, 0, 64), (64, 192, 64, 128), (0, 192, 0, 64)]
    use, uses_of, order, turn = {}, [0] * 8, [], {"proj": 0, "misc": 0}

    def plan(key, kind):
        if kind == "proj":
            b = turn["proj"] % 3
            turn["proj"] += 1
        elif kind == "misc":
            b = 4 + turn["misc"] % 4
            turn["misc"] += 1
        else:
            b = kind
        use[key] = (b, uses_of[b])
        uses_of[b] += 1
        order.append(key)

    def plan_norm(n):
        plan(("norm", n), 3)

    def plan_xattn(l):
        for h in range(XH):
            plan(("xq", l, h), "proj")
        for h in range(XH):
            plan(("xqn", l, h), "misc")
        plan_scores = lambda b: [plan(("xs", l, b, k), "misc") for k in range(2)] if b < 3 else None
        plan_scores(0)
        plan_scores(1)
        for b in range(3):
            plan(("xpT", l, b, 0), 0)
            plan(("xpT", l, b, 1), 1)
            plan_scores(b + 2)
            plan(("xpv", l, b), 2 + b % 2)
        for m in range(KC):
            plan(("xo", l, m), "proj")

    plan("prm", "misc")
    for b in range(3):
        for k in range(2):
            plan(("xin", b, k), "misc")
    plan_norm(0)
    for w in "fqig":
        for h in range(4):
            plan((w, h), "proj")
        if w == "i":
            for g in range(5):
                plan(("iT", g), "misc")
    for h in range(4):
        plan(("v", h), "proj")
    for n in range(3):
        for g in range(3):
            plan(("att", n, g), "misc")
    for h in range(4):
        plan(("u", h), "proj")
    for g in range(4):
        plan(("mean", g), "misc")
    for g in range(3):
        plan(("att", 3, g), "misc")
    for g in range(4):
        plan(("var", g), "misc")
    for n in range(4, 7):
        for g in range(3):
            plan(("att", n, g), "misc")
    plan("wsT", "misc")
    for l in range(2):
        for c in range(2):
            plan(("ckT", l, c), "misc")
        for g in range(4):
            plan(("mT", l, g), "misc")
        for w in "kv":
            for c in range(2):
                plan(("mem" + w, l, c), "proj")
        for c in range(2):
            plan(("mkT", l, c), "misc")
    for b in range(3):
        plan(("vn", b), "misc")
    for g in range(4):
        plan(("gate", g), "misc")
    for g in range(5):
        plan(("kp", g), "misc")
    for c in range(NCH):
        plan(("S", c), 6 + c % 2)
        plan(("o", c), 4 + c % 2)
    turn["misc"] = 0
    for h in range(4):
        plan(("on", h), "misc")
    for m in range(KC):
        plan(("wo", m), "proj")
    plan_norm(1)
    plan_xattn(0)
    plan_norm(2)
    uses_before_ffn = list(uses_of)
    plan_norm(3)
    for b in range(3):
        for u in range(3):
            plan(("qkv", b, u), "proj")
    plan("cskT", "misc")
    for b in range(3):
        for g in range(5):
            plan(("qkT", b, g), "misc")

    GROUPS = [(c, g) for c in range(NCH) for g in range(2)]

    def plan_window_scores(i):
        for k in range(2):
            if i < len(GROUPS):
                plan(("ss", *GROUPS[i], k), "misc")

    plan_window_scores(0)
    plan_window_scores(1)
    for i, (c, g) in enumerate(GROUPS):
        plan(("spT", c, g, 0), 0)
        if KEYS[c][3]:
            plan(("spT", c, g, 1), 1)
        plan_window_scores(i + 2)
        plan(("spv", c, g), 2 + i % 2)
    for m in range(KC):
        plan(("ao", m), "proj")
    plan_norm(4)
    plan_xattn(1)
    plan_norm(5)
    for b in range(3):
        plan(("logit", b), "misc")
    for b in range(3):
        for k in range(2):
            plan(("hnat", b, k), "misc")
    for b in range(3):
        plan(("rank", b), "misc")
        for k in range(2):
            plan(("xnat", b, k), 1 + k)
    plan("load", 3)
    RFILLS = [4, 4, 3]
    H, Y, TR, GA, O = bank[0], [bank[1], bank[2]], bank[4], [bank[5], bank[6]], [bank[7], bank[3]]

    def full(eng, key):
        b, n = use[key]
        eng.wait_ge(bank_full[b], n + 1)
        return bank[b]

    def read(eng, key):
        b, n = use[key]
        eng.wait_ge(bank_free[b], n + 1)

    def freed(key):
        return bank_free[use[key][0]]

    TERMS = [(0, 0), (1, 0), (0, 1)]
    UNITS = ["f", "q", "i", "g", "v", "u", "k0", "v0", "k1", "v1", "wo0", "wo1", "xq0", "xo0",
             "qkv0", "qkv1", "qkv2", "ao0", "ao1", "xq1", "xo1"]
    FIRST = 14
    unit_no = {u: n for n, u in enumerate(UNITS)}

    LAST_USE = {u: (u, 3) for u in "fqigvu"} | {f"{w}{l}": ("mem" + w, l, 1) for w in "kv" for l in (0, 1)} \
        | {"wo0": ("wo", 3), "wo1": ("wo", 7), "ao0": ("ao", 3), "ao1": ("ao", 7)} \
        | {f"xq{l}": ("xq", l, 3) for l in (0, 1)} | {f"xo{l}": ("xo", l, 7) for l in (0, 1)} \
        | {f"qkv{u}": ("qkv", 2, u) for u in range(3)}

    def unit_slot(n):
        return (n if n < FIRST else n - FIRST) % 3

    def unit_fill(n):
        return sum(unit_slot(k) == unit_slot(n) for k in range(n + 1))

    def weights(eng, name):
        n = unit_no[name]
        eng.wait_ge(sg(f"ring_full{unit_slot(n)}"), 16 * unit_fill(n))
        return RING[unit_slot(n)]

    def cols(w, c0):
        return w[:, c0:c0 + 512].rearrange("(k p) n -> p k n", p=P)

    def unit_source(name):
        even = {"u": 0, "v": 512, "q": 1024, "f": 1536, "i": 2048, "g": 2560}
        if name in even:
            return cols(a["even_w_in"][0], even[name])
        kind, n = name[:-1], int(name[-1])
        if kind == "k":
            return cols(a["xattn_w_k"][n], 0)
        if kind == "v":
            return cols(a["xattn_w_v"][n], 0)
        if kind == "xq":
            return cols(a["xattn_w_q"][n], 0)
        if kind == "xo":
            return a["xattn_w_o"][n].rearrange("(k p) n -> p k n", p=P)
        return cols({"wo": a["even_w_out"], "qkv": a["attn_w_in"], "ao": a["attn_w_out"]}[kind][0], 512 * n)

    TILES = [(unit, m, (unit, m)) for unit in "fqigvu" for m in range(4)] \
        + [("xq0", m, ("xq", 0, m)) for m in range(4)] + [("xo0", m, ("xo", 0, 2 * m + 1)) for m in range(4)] \
        + [(f"ao{m // 4}", m % 4, ("ao", m)) for m in range(8)] \
        + [("xq1", m, ("xq", 1, m)) for m in range(4)] + [("xo1", m, ("xo", 1, 2 * m + 1)) for m in range(4)]
    XQ, XO, AO = [24, 40], [28, 44], 32
    SPLIT_BEFORE = {0: 0, 1: 1, 2: 2, 4: 3}
    norm_parts = lambda n: hT_parts if n else h0_parts

    def tile_parts(t):
        return (e_tiles if t < XQ[0] else ao_tiles if AO <= t < AO + 8 else x_tiles)[t % 2]

    def tile_views(t, eng):
        unit, m, _ = TILES[t]
        k = 4 if unit[:2] == "xo" else KC
        raw = split(weights(eng, unit), k)[:, :, m * (1024 // k):(m + 1) * (1024 // k)]
        return raw, [split(x, k) for x in tile_parts(t)]

    block = ctx.enter_context(nc.Block())

    @block.sync
    def _(sp):
        for b, (t0, n) in enumerate(BLOCKS):
            src = a["x_prompt"][0, t0:t0 + n] if t0 < TP else a["x_sample"][0]
            sp.dma_start(xin[0:n, b], src).then_inc(sg("x_loaded"), 16)

        rows = lambda x: x.rearrange("l (k p) -> (l k) p", p=P)
        for at, src in ((R_MIX, rows(a["norm_mix"])), (R_XAT, rows(a["norm_xattn"])), (R_FFN, rows(a["norm_ffn"])),
                        (R_MEM, rows(a["xattn_mem_norm"])), (R_LB0, rows(a["hgrn_lb_logits"])),
                        (R_LNG, a["gmlp_ln_g"][0]), (R_LNB, a["gmlp_ln_b"][0]), (R_OUT, a["hgrn_out_norm"]),
                        (R_XQ, a["xattn_q_norm"])):
            sp.dma_start(prow[at:at + src.shape[0], :], src).then_inc(sg("prm_loaded"), 16)

        def load_unit(n):
            name = UNITS[n]
            k = 4 if name[:2] == "xo" else KC
            sp.dma_start(split(RING[unit_slot(n)], k), unit_source(name)).then_inc(sg(f"ring_full{unit_slot(n)}"), 16)

        for n in range(FIRST):
            if n >= 3:
                full(sp, LAST_USE[UNITS[n - 3]])
            if n >= 3 and UNITS[n - 3] == "u":
                sp.dma_start(memn, a["mem_prompt"][0].rearrange("(c p) n -> p c n", p=P)).then_inc(sg("memn_loaded"), 16)
                sp.dma_start(ws, a["gmlp_w_s"][0].rearrange("g t s -> t g s")).then_inc(sg("ws_loaded"), 16)
            load_unit(n)

        def load_w13(i, s):
            c0 = bass.ds(i * 256 + s * P, P)
            to = W13[s].rearrange("p (k w n) -> p k w n", k=KC, w=2)
            for w, src in enumerate((a["ffn_w1"][0], a["ffn_w3"][0])):
                sp.dma_start(to[:, :, w], src[:, c0].rearrange("(k p) n -> p k n", p=P)).then_inc(sg(f"w13_full{s}"), 16)

        def load_w2(m, s):
            src = a["ffn_w2"][0][s * 11 * P:(s + 1) * 11 * P, bass.ds(m * 256, 256)]
            sp.dma_start(W2S[s], src.rearrange("(k p) n -> p k n", p=P)).then_inc(sg(f"w2_full{s}"), 16)

        full(sp, LAST_USE["xq0"])
        load_w13(0, 0)
        load_w13(0, 1)
        full(sp, LAST_USE["xo0"])
        load_w2(0, 0)
        with sp.Fori(1, 11) as i:
            for s in range(2):
                sp.wait_ge(sg("w13_low"), 2 * i + s - 1)
                load_w13(i, s)
        sp.wait_ge(sg("w13_low"), FC)
        load_w2(0, 1)
        with sp.Fori(1, 4) as m:
            for s in range(2):
                sp.wait_ge(sg("w2_low"), 4 * m + 2 * s - 2)
                load_w2(m, s)
        for n in range(FIRST, len(UNITS)):
            if n == FIRST:
                sp.wait_ge(sg("w2_low"), 16)
            elif n < FIRST + 3:
                sp.wait_ge(sg(f"w2_used{FIRST + 2 - n}"), 9)
            else:
                full(sp, LAST_USE[UNITS[n - 3]])
            load_unit(n)

        def load_up(e, n, j):
            s = j % 3
            if n is not None:
                sp.wait_ge(sg("split_lo1"), n + (-1, -1, -2)[s] if j < 3 else n - 2)
            for w, src in enumerate((a["moe_w1"][0], a["moe_w3"][0])):
                v = src[bass.ds(e, 1), :, j * 256:(j + 1) * 256].rearrange("e (k p) n -> p (e k) n", p=P)
                to = WE[s].rearrange("p (k w n) -> p k w n", k=KC, w=2)[:, :, w]
                sp.dma_start(to, v).then_inc(sg(f"moe13_full{s}"), 16)

        def load_down(e, n, j):
            s = j % 3
            if n is not None:
                sp.wait_ge(sg("split_lo2"), n + (-1, -1, -2)[s] if j < 3 else n - 2)
            v = a["moe_w2"][0][bass.ds(e, 1), j * 256:(j + 1) * 256, :].rearrange("e (k p) n -> p (e k) n", p=P)
            sp.dma_start(split(WD[s], 2), v).then_inc(sg(f"moe2_full{s}"), 16)

        def load_expert(e, i, first=False):
            for j in range(11):
                load_up(e, None if first and j < 3 else 11 * i + j, j)
                if j:
                    load_down(e, None if first and j < 4 else 11 * i + j - 1, j - 1)
            load_down(e, 11 * i + 10, 10)

        full(sp, LAST_USE["xo1"])
        load_expert(0, 0, first=True)
        with sp.Fori(1, E) as e:
            load_expert(e, e)
        sp.wait_ge(sg("flag_ready"), 1)
        overloaded = sp.value_load(flag[0:1, 0:1])
        with sp.If(overloaded > P):
            for r in (1, 2):
                with sp.Fori(0, E) as e:
                    load_expert(e, e + E * r)

    @block.gpsimd
    def _(pool):
        pool.dma_start(const[:], a["shape_constants"]).then_inc(sg("const_loaded"), 16)
        pool.memset(ones, 1.0).then_inc(sg("const_set"), 1)
        pool.memset(ones_d, 1.0 / D).then_inc(sg("const_set"), 1)
        pool.memset(ones_h, 1.0 / P).then_inc(sg("const_set"), 1)
        pool.memset(eps, EPS).then_inc(sg("const_set"), 1)
        pool.dma_start(kg, a["xattn_k_norm"].partition_broadcast(P)).then_inc(sg("small_loaded"), 16)
        pool.dma_start(qkg[:, 0], a["attn_q_norm"][0].partition_broadcast(P)).then_inc(sg("small_loaded"), 16)
        pool.dma_start(qkg[:, 1], a["attn_k_norm"][0].partition_broadcast(P)).then_inc(sg("small_loaded"), 16)
        by_half = a["attn_sinks"][0].rearrange("(kv hh par) -> hh kv par", kv=4, hh=2)
        for hh in range(2):
            pool.dma_start(sinkc[hh * 64:hh * 64 + 64, :].rearrange("p (kv par) -> p kv par", kv=4),
                           by_half[hh].partition_broadcast(64)).then_inc(sg("small_loaded"), 16)
        pool.dma_start(routr, a["moe_router"][0].rearrange("(k p) e -> p k e", p=P)).then_inc(sg("small_loaded"), 16)
        for l in range(2):
            pool.dma_start(split(mem_kT_p[:, l].rearrange("p h m -> p (h m)"), 2),
                           a["cache_mem_k"][l, 0].rearrange("(c p) h d -> p c (h d)", p=P)) \
                .then_inc(sg("cache_loaded"), 16)
            pool.dma_start(mem_v_s[:, l], a["cache_mem_v"][l, 0].rearrange("(c p) h d -> p c (h d)", p=P)) \
                .then_inc(sg("cache_loaded"), 16)
        pool.dma_start(bsr, a["gmlp_b_s"].rearrange("o g t -> o (g t)")).then_inc(sg("bs_loaded"), 16)
        pool.dma_start(Ss, a["state_hgrn"][0, 0].rearrange("h k v -> k h v")).then_inc(sg("state_loaded"), 16)
        pool.wait_ge(bank_full[use[("norm", 0)][0]], use[("norm", 0)][1] + 1)
        pool.memset(X[0], 1.0).then_inc(sg("scan_ones"), 1)
        pool.wait_ge(sg("scan_ones"), 1)
        pool.memset(X[0].rearrange("p (c t) -> p c t", t=CH)[:, :, 0:1], 0.0).then_inc(sg("scan_mask"), 1)
        def level_keys(n):
            b = LEVELS[n]
            x = X[n % 3].rearrange("p (n two b) -> p n two b", two=2, b=b)[:, :, 0]
            k = kT.rearrange("p (n two b) -> p n two b", two=2, b=b)[:, :, 0]
            pool.wait_ge(sg("level_exp"), n + 1)
            pool.wait_ge(sg("k_ready"), 4)
            pool.tensor_tensor(x, x, k, ALU.mult).then_inc(sg("level_k"), 1)

        for n in range(6):
            level_keys(n)
        full(pool, ("att", 6, 2))
        pool.wait_ge(sg("end_exp"), 1)
        pool.tensor_tensor(kT, kT, X[1], ALU.mult).then_inc(sg("kp_ready"), 1)
        out_sem = sg("out_written")
        pool.wait_ge(sg("const_loaded"), 16)
        pool.wait_ge(sg("small_loaded"), 96)
        for l in range(2):
            pool.wait_ge(sg("mk_ready"), 2 * l + 2)
            pool.dma_start(a["mem_k_prompt"][l, 0].rearrange("(c p) h d -> p c (h d)", p=P), mkn[l]) \
                .then_inc(out_sem, 16)
            read(pool, ("memv", l, 1))
            pool.dma_start(a["mem_v_prompt"][l, 0].rearrange("(c p) h d -> p c (h d)", p=P), mem_v_p[:, l]) \
                .then_inc(out_sem, 16)
        read(pool, ("vn", 2))
        pool.dma_start(a["gmlp_v_sample"][0, 0].rearrange("t g d -> t (g d)"), vnat[0:TS, 2]).then_inc(out_sem, 16)
        read(pool, ("S", 4))
        pool.dma_start(a["hgrn_state_prompt"][0, 0].rearrange("h k v -> k h v"), Sp).then_inc(out_sem, 16)
        pool.dma_start(a["hgrn_state_sample"][0, 0].rearrange("h k v -> k h v"), Ss).then_inc(out_sem, 16)
        pool.wait_ge(out_sem, 16 * 7)
        full(pool, ("wo", KC - 1))
        pool.dma_start(ckn, a["cache_swa_k"][0, 0].rearrange("t h d -> t (h d)")).then_inc(sg("swa_cache_loaded"), 16)
        pool.dma_start(cvn, a["cache_swa_v"][0, 0].rearrange("t h d -> t (h d)")).then_inc(sg("swa_cache_loaded"), 16)
        for b, (t0, n) in enumerate(BLOCKS):
            for i in range(2):
                for f, at in enumerate((C_COS, C_SIN)):
                    trig = const[0:n, at + b * 32:at + b * 32 + 32].unsqueeze(1).broadcast_to([n, 2, 32])
                    pool.tensor_tensor(gcs[0:n, b, 2 * i + f].rearrange("p (x n) -> p x n", x=2),
                                       qkg[0:n, i].rearrange("p (x n) -> p x n", x=2), trig, ALU.mult) \
                        .then_inc(sg("rope_tables"), 1)
        pool.wait_ge(sg("rope_tables"), 12)
        for b, (t0, n) in enumerate(BLOCKS):
            pool.wait_ge(sg("qk_scaled"), b + 1)
            if b:
                pool.wait_ge(sg("rot_done"), 2 * b)
            for h0, nh, f in ((0, 16, 1), (16, 4, 3)):
                x = qkv[0:n, b, h0 * 64:(h0 + nh) * 64].rearrange("p (h d) -> p h d", d=64)
                o = rtmp[0:n, h0 * 64:(h0 + nh) * 64].rearrange("p (h d) -> p h d", d=64)
                pool.tensor_tensor(o, x, gcs[0:n, b, f].unsqueeze(1).broadcast_to([n, nh, 64]), ALU.mult) \
                    .then_inc(sg("sine_ready"), 1)
        pool.wait_ge(sg("rot_done"), 6)
        flat = lambda x: x.rearrange("t h d -> t (h d)")
        pool.dma_start(flat(a["swa_k_prompt"][0, 0]), rot[:, 1, 1024:1280]).then_inc(out_sem, 16)
        pool.dma_start(flat(a["swa_v_prompt"][0, 0]), qkv[:, 1, 1280:1536]).then_inc(out_sem, 16)
        pool.dma_start(flat(a["swa_k_sample"][0, 0]), rot[0:TS, 2, 1024:1280]).then_inc(out_sem, 16)
        pool.dma_start(flat(a["swa_v_sample"][0, 0]), qkv[0:TS, 2, 1280:1536]).then_inc(out_sem, 16)
        pool.wait_ge(sg("y_final"), 1)
        pool.dma_start(a["y_prompt"][0].rearrange("(b p) n -> p b n", p=P), xnat[:, 0:2]).then_inc(out_sem, 16)
        pool.dma_start(a["y_sample"][0], xnat[0:TS, 2]).then_inc(out_sem, 16)
        pool.wait_ge(out_sem, 16 * 13)


    @block.tensor
    def _(pe):
        for name in ("scat_T", "hid_T", "scatter_done", "part_used0", "part_used1", "part_used2",
                     "w13_used0", "w13_used1", "w2_used0", "w2_used1"):
            pe.sem_inc(sg(name), 1)
        mm = nc.tensor.matmul
        todo = list(order)

        def start(key):
            assert todo.pop(0) == key, key
            b, n = use[key]
            if n:
                pe.wait_ge(bank_free[b], n)
            return bank[b]

        def end(ins, key):
            ins.then_inc(bank_full[use[key][0]], 1)

        def transposes(key, parts):
            out = start(key)
            for at, x in parts:
                rows, n = x.shape[0], x.shape[1]
                ins = nc.tensor.transpose(out[0:n, at:at + rows], x, ident[0:rows, 0:rows])
            end(ins, key)

        def project(key, w, width, m, x, kc, ready=None):
            out = start(key)
            for k in range(kc):
                if ready:
                    ready(k)
                ins = mm(out[:, 0:T], w[:, k * width + m * P:k * width + (m + 1) * P], x[:, k, :],
                         start=k == 0, stop=k == kc - 1)
            end(ins, key)
            return ins

        def project_parts(key, t, c0, m, x, kc, ready=None):
            pe.wait_ge(sg("tile_low"), t + 1)
            out = start(key)
            w = [split(p, kc)[:, :, c0:c0 + P] for p in tile_parts(t)]
            for k in range(kc):
                if ready:
                    ready(k)
                for n, (i, j) in enumerate(TERMS):
                    ins = mm(out[:, 0:T], w[j][:, k], x[i][:, k], start=k == 0 and n == 0, stop=k == kc - 1 and n == 2)
            end(ins, key)

        def h_part(n):
            return lambda k: pe.wait_ge(sg("h_low"), KC * n + k + 1)

        def mixed_chunk(k):
            if k < 4:
                read(pe, ("gate", k))
            if k >= 4:
                pe.wait_ge(sg("mixed"), k - 3)

        def norm(n):
            out = start(("norm", n))
            for c in range(KC):
                pe.wait_ge(sg("sq_ready"), KC * n + c + 1)
                ins = mm(out[:, 0:T], ones_d, sq[:, c], start=c == 0, stop=c == KC - 1)
            end(ins, ("norm", n))

        pe.wait_ge(sg("const_loaded"), 16)
        pe.wait_ge(sg("prm_loaded"), 16 * 9)
        transposes("prm", [(0, prow[0:NROW, :])])
        for b, (t0, n) in enumerate(BLOCKS):
            pe.wait_ge(sg("x_loaded"), 48)
            for k in range(2):
                transposes(("xin", b, k), [(i * P, xin[0:n, b, (4 * k + i) * P:(4 * k + i + 1) * P]) for i in range(4)])
        pe.wait_ge(sg("const_set"), 4)
        norm(0)
        def even_unit(name):
            for h in range(4):
                project_parts((name, h), 4 * "fqigvu".index(name) + h, 0, h, h0_parts, KC, ready=h_part(0))

        for name in "fqi":
            even_unit(name)
        for g in range(5):
            read(pe, ("i", 3))
            transposes(("iT", g), [(i * P, iT[:, (4 * g + i) * CH:(4 * g + i + 1) * CH]) for i in range(4)])
        even_unit("g")
        even_unit("v")

        def level(n):
            if n < 6:
                pe.wait_ge(sg("level_k"), n + 1)
                pe.wait_ge(sg("level_q"), n + 1)
            lhs, rhs = (X[n % 3], X[n % 3]) if n < 6 else (kT, qT)
            for g in range(3):
                out = start(("att", n, g))
                pairs = range(8 * g, min(8 * g + 8, 20))
                for hc in pairs:
                    t = slice(hc * CH, (hc + 1) * CH)
                    ins = mm(out[0:CH, (hc - 8 * g) * CH:(hc - 8 * g + 1) * CH], lhs[:, t], rhs[:, t], start=True, stop=True)
                end(ins, ("att", n, g))

        for n in range(3):
            level(n)
        even_unit("u")
        for g in range(4):
            read(pe, ("v", g))
            out = start(("mean", g))
            end(mm(out[:, 0:T], ones_h, vT[:, g * T:(g + 1) * T], start=True, stop=True), ("mean", g))
        level(3)
        for g in range(4):
            pe.wait_ge(sg("v_sq"), g + 1)
            out = start(("var", g))
            end(mm(out[:, 0:T], ones_h, gsq[:, g * T:(g + 1) * T], start=True, stop=True), ("var", g))
        for n in range(4, 7):
            level(n)
        pe.wait_ge(sg("ws_loaded"), 16)
        pe.wait_ge(sg("bs_loaded"), 16)
        transposes("wsT", [(g * P, ws[:, g]) for g in range(4)])
        pe.wait_ge(sg("cache_loaded"), 64)
        pe.wait_ge(sg("memn_scaled"), 2)
        for l in range(2):
            raw = split(mem_kT_p[:, l].rearrange("p h m -> p (h m)"), 2)
            for c in range(2):
                transposes(("ckT", l, c), [(h * P, raw[:, c, h * P:(h + 1) * P]) for h in range(4)])
            for g in range(4):
                c, k = divmod(g, 2)
                transposes(("mT", l, g), [(i * P, memn[:, c, (4 * k + i) * P:(4 * k + i + 1) * P]) for i in range(4)])
            read(pe, ("mT", l, 3))
            for name in "kv":
                w = split(weights(pe, f"{name}{l}"), KC)
                for c in range(2):
                    out = start(("mem" + name, l, c))
                    for k in range(KC):
                        ins = mm(out, hT[:, k, c * P:(c + 1) * P], w[:, k], start=k == 0, stop=k == KC - 1)
                    end(ins, ("mem" + name, l, c))
            for c in range(2):
                pe.wait_ge(sg("mk_ready"), 2 * l + c + 1)
                transposes(("mkT", l, c), [(h * P, mkn[l][:, c, h * P:(h + 1) * P]) for h in range(4)])
        for b, (t0, n) in enumerate(BLOCKS):
            pe.wait_ge(sg("vn_ready"), 4)
            transposes(("vn", b), [(g * P, vT[:, g * T + t0:g * T + t0 + n]) for g in range(4)])
        read(pe, ("vn", 2))
        read(pe, "wsT")
        for g in range(4):
            out = start(("gate", g))
            for b, (t0, n) in enumerate(BLOCKS):
                mm(out[:, t0:t0 + n], vnat[0:n, b, g * P:(g + 1) * P], wsT[0:n, g, 0:n], start=True, stop=False)
                ins = mm(out[:, t0:t0 + n], ones[0:1, :], bsr[0:1, g * P:g * P + n], start=False, stop=True)
            end(ins, ("gate", g))
        pe.wait_ge(sg("kp_ready"), 1)
        for g in range(5):
            transposes(("kp", g), [(i * P, kT[:, (4 * g + i) * CH:(4 * g + i + 1) * CH]) for i in range(4)])
        read(pe, ("kp", 4))
        read(pe, ("iT", 4))
        pe.wait_ge(sg("qp_ready"), 1)
        read(pe, ("att", 6, 2))
        for c in range(NCH):
            out = start(("S", c))
            for h in range(4):
                hc = h * NCH + c
                ins = mm(out[:, h * P:(h + 1) * P], kp[0:CH, hc], vb[0:CH, hc], start=True, stop=True)
            end(ins, ("S", c))
            out = start(("o", c))
            if 1 <= c <= 3:
                read(pe, ("S", c - 1))
            if c == 4:
                pe.wait_ge(sg("state_loaded"), 16)
            S = Ss if c == 4 else Sp
            for h in range(4):
                hc = h * NCH + c
                t = slice(hc * CH, (hc + 1) * CH)
                if c:
                    mm(out[:, h * CH:(h + 1) * CH], S[:, h], qT[:, t], start=True, stop=False)
                ins = mm(out[:, h * CH:(h + 1) * CH], vb[0:CH, hc], att[0:CH, t], start=c == 0, stop=True)
            end(ins, ("o", c))
        for h in range(4):
            pe.wait_ge(sg("o_sq"), h + 1)
            out = start(("on", h))
            end(mm(out[:, 0:T], ones_h, vT[:, h * T:(h + 1) * T], start=True, stop=True), ("on", h))
        for m in range(KC):
            w = weights(pe, f"wo{m // 4}")
            project(("wo", m), w, 512, m % 4, hT, KC, ready=mixed_chunk)

        def xattn(l):
            for h in range(XH):
                project_parts(("xq", l, h), XQ[l] + h, 0, h, hT_parts, KC, ready=h_part(1 + 2 * l))
            for h in range(XH):
                pe.wait_ge(sg("xq_sq"), 4 * l + h + 1)
                out = start(("xqn", l, h))
                end(mm(out[:, 0:T], ones_h, xsq[:, h * T:(h + 1) * T], start=True, stop=True), ("xqn", l, h))

            def scores(b):
                t0, n = BLOCKS[b]
                keys = mem_kT_p if b < 2 else mem_kT_s
                for k in range(2):
                    out = start(("xs", l, b, k))
                    for hh in range(2):
                        h = 2 * k + hh
                        pe.wait_ge(sg("xq_ready"), 4 * l + h + 1)
                        ins = mm(out[0:n, hh * MEM:(hh + 1) * MEM], qn[:, h * T + t0:h * T + t0 + n], keys[:, l, h],
                                 start=True, stop=True)
                    end(ins, ("xs", l, b, k))

            def tail(b):
                t0, n = BLOCKS[b]
                v = mem_v_p if b < 2 else mem_v_s
                pe.wait_ge(sg("xprob"), 3 * l + b + 1)
                for k in range(2):
                    transposes(("xpT", l, b, k), [(h * P, prob[b % 2][0:n, h, k * P:(k + 1) * P]) for h in range(4)])
                if b == 0:
                    scores(2)
                read(pe, ("xpT", l, b, 0))
                read(pe, ("xpT", l, b, 1))
                out = start(("xpv", l, b))
                for h in range(4):
                    for k in range(2):
                        ins = mm(out[:, h * P:h * P + n], v[:, l, k, h * P:(h + 1) * P], probT[b % 2][:, 4 * k + h, 0:n],
                                 start=k == 0, stop=k == 1)
                end(ins, ("xpv", l, b))

            read(pe, ("mkT", 1, 1))
            scores(0)
            scores(1)
            for b in range(3):
                tail(b)
            read(pe, ("xpv", l, 2))
            for m in range(KC):
                project_parts(("xo", l, m), XO[l] + m // 2, m % 2 * P, m, oxT, 4)

        norm(1)
        xattn(0)
        norm(2)
        pe.wait_ge(bank_free[0], uses_before_ffn[0])
        for b in range(1, 8):
            if uses_before_ffn[b]:
                pe.wait_ge(bank_free[b], uses_before_ffn[b])

        def ffn_tile(i, s, first=False):
            pe.wait_ge(sg("w13_low"), 2 * i + s + 1)
            pe.wait_ge(sg(f"ffn_g{s}"), i + 1)
            for w in range(2):
                for k in range(KC):
                    if first:
                        pe.wait_ge(sg("h_low"), 2 * KC + k + 1)
                    for n, (x, y) in enumerate(TERMS):
                        at = (2 * k + w) * P
                        ins = mm(bank[2 * s + w][:, 0:T], w_parts[s][y][:, at:at + P], hT_parts[x][:, k],
                                 start=k == 0 and n == 0, stop=k == KC - 1 and n == 2)
                ins.then_inc(sg(f"ffn_h1_{s}" if w == 0 else f"w13_used{s}"), 1)

        ffn_tile(0, 0, first=True)
        ffn_tile(0, 1)
        with pe.Fori(1, 11) as i:
            ffn_tile(i, 0)
            ffn_tile(i, 1)
        with pe.Fori(0, 2) as m:
            for q in range(2):
                pe.wait_ge(sg("ffn_out"), 4 * m + 2 * q + 1)
                for s in range(2):
                    pe.wait_ge(sg("g_low"), 13 if s == 0 else FC + 2)
                    for t in range(2):
                        pe.wait_ge(sg("w2_low"), 8 * m + 4 * q + 2 * s + t + 1)
                        for k in range(11):
                            for n, (x, y) in enumerate(TERMS):
                                ins = mm(bank[4 + 2 * q + t][:, 0:T], w_parts[t][y][:, k * P:(k + 1) * P],
                                         gT[x][:, 11 * s + k], start=s == 0 and k == 0 and n == 0,
                                         stop=s == 1 and k == 10 and n == 2, skip_group_check=True)
                        ins.then_inc(sg(f"w2_used{t}"), 1)
        norm(3)
        for b, (t0, n) in enumerate(BLOCKS):
            for u in range(3):
                w = split(weights(pe, f"qkv{u}"), KC)
                out = start(("qkv", b, u))
                for k in range(KC):
                    pe.wait_ge(sg("h_ready"), 3 * KC + k + 1)
                    ins = mm(out[0:n, :], hT[:, k, t0:t0 + n], w[:, k], start=k == 0, stop=k == KC - 1)
                end(ins, ("qkv", b, u))
        pe.wait_ge(sg("swa_cache_loaded"), 32)
        transposes("cskT", [(kv * P, ckn[:, kv * 64:(kv + 1) * 64]) for kv in range(4)])
        for b, (t0, n) in enumerate(BLOCKS):
            pe.wait_ge(sg("rot_done"), 2 * b + 2)
            for g in range(5):
                transposes(("qkT", b, g), [(i * P, rot[0:n, b, (4 * g + i) * 64:(4 * g + i + 1) * 64]) for i in range(4)])

        def scores(c, g):
            k0, nk, off, rows1 = KEYS[c]
            for k in range(2):
                kv = 2 * g + k
                out = start(("ss", c, g, k))
                for par in range(2):
                    keys = kT2[:, kv, k0:k0 + nk] if c < 4 else kTs[:, kv, :]
                    ins = mm(out[:, par * 256 + off:par * 256 + off + nk], qT2[:, c, kv, par].rearrange("p hh t -> p (hh t)"),
                             keys, start=True, stop=True)
                end(ins, ("ss", c, g, k))

        def swa_tail(i, c, g):
            k0, nk, off, rows1 = KEYS[c]
            rows = [min(off + nk, P), rows1]
            pe.wait_ge(sg("sprob"), i + 1)
            for k in range(2):
                if rows[k]:
                    transposes(("spT", c, g, k), [(j * P, sp_prob[i % 2][:, j, k * P:k * P + rows[k]]) for j in range(4)])
            if i + 2 < len(GROUPS):
                scores(*GROUPS[i + 2])
            for k in range(2):
                if rows[k]:
                    read(pe, ("spT", c, g, k))
            out = start(("spv", c, g))
            for j in range(4):
                kv, par = 2 * g + j // 2, j % 2
                for k in range(2):
                    if not rows[k]:
                        continue
                    if c < 4:
                        v = qkv[0:rows[k], k, 1280 + kv * 64:1280 + (kv + 1) * 64]
                    else:
                        v = cvn[:, kv * 64:(kv + 1) * 64] if k == 0 else qkv[0:TS, 2, 1280 + kv * 64:1280 + (kv + 1) * 64]
                    ins = mm(out[par * 64:par * 64 + 64, (j // 2) * P:(j // 2 + 1) * P], v, sp_probT[i % 2][k][0:rows[k], j],
                             start=k == 0, stop=k == 1 or not rows[1])
            end(ins, ("spv", c, g))

        read(pe, ("qkT", 2, 4))
        scores(*GROUPS[0])
        scores(*GROUPS[1])
        for i, (c, g) in enumerate(GROUPS):
            swa_tail(i, c, g)
        read(pe, ("spv", 4, 1))
        for m in range(KC):
            project_parts(("ao", m), AO + m, 0, m, o2T, KC)
        norm(4)
        xattn(1)
        norm(5)
        for b, (t0, n) in enumerate(BLOCKS):
            out = start(("logit", b))
            for k in range(KC):
                pe.wait_ge(sg("h_ready"), 5 * KC + k + 1)
                ins = mm(out[0:n, 0:E], hT[:, k, t0:t0 + n], routr[:, k], start=k == 0, stop=k == KC - 1)
            end(ins, ("logit", b))

        def natural(name, src, b):
            t0, n = BLOCKS[b]
            for k in range(2):
                transposes((name, b, k), [(i * P, src[:, 4 * k + i, t0:t0 + n]) for i in range(4)])

        for b in range(3):
            natural("hnat", hT, b)
        pe.wait_ge(sg("chosen"), 3)
        for b, (t0, n) in enumerate(BLOCKS):
            out = start(("rank", b))
            for bb in range(b + 1):
                lhs = ones[:, 0:n] if bb < b else const[0:n, C_UT:C_UT + n]
                ins = mm(out[0:n, 0:E], lhs, chosen[0:BLOCKS[bb][1], bb], start=bb == 0, stop=bb == b)
            end(ins, ("rank", b))
            natural("xnat", xT, b)
        out = start("load")
        for b, (t0, n) in enumerate(BLOCKS):
            ins = mm(out[:, 0:E], ones[0:n, :], chosen[0:n, b], start=b == 0, stop=b == 2)
        end(ins, "load")
        assert not todo, todo[:3]

        def select(i):
            pe.wait_ge(sg("onehot"), 3 * i + 3)
            pe.wait_ge(sg("xg_low"), 2 * i + 1)
            for half in range(2):
                for b, (t0, n) in enumerate(BLOCKS):
                    for r in range(2):
                        ins = mm(GA[half], onehot[0:n, b], hnat[r][0:n, b, half * 512:(half + 1) * 512],
                                 start=b == 0 and r == 0, stop=b == 2 and r == 1)
                ins.then_inc(sg("selected"), 1)

        def turn_selected(i):
            for half in range(2):
                for h in range(2):
                    pe.wait_ge(sg(f"sel_copied{h}"), i + 1)
                for c in range(4):
                    ins = nc.tensor.transpose(GA[half][:, c * P:(c + 1) * P], xsel[half][:, c * P:(c + 1) * P], ident)
                ins.then_inc(sg("turned"), 1)

        def moe_up(i, j, q):
            pe.wait_ge(sg(f"split_lo{q}"), 11 * i + j + 1)
            for k in range(4):
                for n, (x, w) in enumerate(TERMS):
                    ins = mm(H, xg[x][:, 4 * q + k], split(part[q][w], 4)[:, k],
                             start=q == 0 and k == 0 and n == 0, stop=q == 1 and k == 3 and n == 2)
            ins.then_inc(sg(f"part_used{q}"), 1)

        def moe_down(i, j):
            pe.wait_ge(sg("split_lo2"), 11 * i + j + 1)
            pe.wait_ge(sg("hidT_ready"), 11 * i + j + 2)
            if j == 0:
                pe.wait_ge(sg("ysb_ready0"), i + 1)
                pe.wait_ge(sg("ysb_ready1"), i + 1)
            for c in range(2):
                for n, (x, w) in enumerate(TERMS):
                    for half in range(2):
                        ins = mm(Y[half], hidT[x][:, c], split(part[2][w], 2)[:, c, half * 512:(half + 1) * 512],
                                 start=j == 0 and c == 0 and n == 0, stop=j == 10 and c == 1 and n == 2,
                                 skip_group_check=True)
            ins.then_inc(sg("part_used2"), 1)

        def scatter(i, q):
            b, half = divmod(q, 2)
            if q < 2:
                pe.wait_ge(sg(f"ysb_ready{half}"), i + 2)
            pe.wait_ge(sg("scattered"), 6 * i + q)
            for r in range(2):
                ins = mm(O[q % 2], scat[:, b], ysb[r][:, half * 512:(half + 1) * 512], start=r == 0, stop=r == 1)
            ins.then_inc(sg("scatter_done"), 1)

        def moe_pass(i, first=False):
            if not first:
                turn_selected(i)
            for j in range(11):
                pe.wait_ge(sg("hid_ready"), 11 * i + j + 1)
                if j == 0:
                    pe.wait_ge(sg("xg_low"), 2 * i + 3)
                moe_up(i, j, 0)
                moe_up(i, j, 1)
                if j:
                    moe_down(i, j - 1)
                elif not first:
                    moe_down(i - 1, 10)
                pe.wait_ge(sg("hid_ready"), 11 * i + j + 2)
                pe.wait_ge(sg("hidT_ready"), 11 * i + j + 1)
                for c in range(2):
                    ins = nc.tensor.transpose(TR[:, c * P:(c + 1) * P], hid[:, c * P:(c + 1) * P], ident)
                ins.then_inc(sg("hid_T"), 1)
                if j in (2, 3, 4) and not first:
                    scatter(i - 1, 2 * j - 4)
                    scatter(i - 1, 2 * j - 3)
                if j == 5:
                    pe.wait_ge(sg("scattered"), 6 * i + 1)
                    for b, (t0, n) in enumerate(BLOCKS):
                        mm(O[0][:, 384:385], onehot[0:n, b].bitcast(F32), gates[0:n, b, bass.ds(i, 1)],
                           start=b == 0, stop=b == 2)
                    for b, (t0, n) in enumerate(BLOCKS):
                        ins = nc.tensor.transpose(O[0][:, t0:t0 + n], onehot[0:n, b].bitcast(F32), ident[0:n, 0:n])
                    ins.then_inc(sg("scat_T"), 1)
                if j == 9:
                    select(i + 1)

        def moe_last(i):
            moe_down(i, 10)
            for q in range(6):
                scatter(i, q)

        read(pe, ("hnat", 2, 1))
        for b in range(8):
            pe.wait_ge(bank_free[b], uses_of[b])
        select(0)
        turn_selected(0)
        moe_pass(0, first=True)
        with pe.Fori(1, E) as i:
            moe_pass(i)
        moe_last(E - 1)
        pe.wait_ge(sg("flag_ready"), 1)
        overloaded = pe.value_load(flag[0:1, 0:1])
        with pe.If(overloaded > P):
            turn_selected(E)
            moe_pass(E, first=True)
            with pe.Fori(E + 1, 2 * E) as i:
                moe_pass(i)
            with pe.Fori(2 * E, PASSES) as i:
                moe_pass(i)
            moe_last(PASSES - 1)

    @block.scalar
    def _(act):
        A = nc.scalar.activation
        chain = [0]

        def link(ins):
            chain[0] += 1
            ins.then_inc(sg("act_chain"), 1)
            act.wait_ge(sg("act_chain"), chain[0])

        def head(x, h):
            return x[:, h * T:(h + 1) * T]

        def tile_high(t):
            raw, parts = tile_views(t, act)
            if t == XQ[1]:
                full(act, TILES[AO + 7][2])
            elif t not in (0, 1, XQ[0], XQ[0] + 1, AO, AO + 1):
                full(act, TILES[t - 2][2])
            A(parts[0], raw, ACT.Copy).then_inc(sg("tile_high"), 1)

        def norm(n, tiles=None):
            source = [lambda c: read(act, ("xin", 2, 1)), lambda c: read(act, ("wo", c)), lambda c: read(act, ("xo", 0, c)),
                      lambda c: act.wait_ge(sg("ffn_out"), c + 4), lambda c: read(act, ("ao", c)),
                      lambda c: read(act, ("xo", 1, c))][n]
            if n:
                full(act, ("norm", n - 1))
            for c in range(KC):
                if tiles and c in tiles:
                    tile_high(tiles[c])
                source(c)
                A(sq[:, c], xT[:, c], ACT.Square).then_inc(sg("sq_ready"), 1)
            if tiles and KC in tiles:
                tile_high(tiles[KC])
            out = full(act, ("norm", n))
            if n:
                act.wait_ge(sg("h_ready"), KC * n)
            root(("norm", n), rstd, out[:, 0:T]).then_inc(sg("rstd_ready"), 1)

        def root(key, out, x):
            b, n = use[key]
            A(out, x, ACT.Ln, bias=eps).then_inc(bank_free[b], 1)
            act.wait_ge(bank_free[b], n + 1)
            return A(out, out, ACT.Exp, scale=-0.5)

        def logs():
            nc.scalar.preload_act_table_set("natural_log_exp_and_others")

        def h_high(n):
            for c in range(KC):
                act.wait_ge(sg("h_ready"), KC * n + c + 1)
                A(norm_parts(n)[0][:, c], hT[:, c], ACT.Copy).then_inc(sg("h_high"), 1)

        act.wait_ge(sg("const_set"), 4)
        logs()
        norm(0, tiles={KC: 0})
        tile_high(1)
        h_high(0)
        act.wait_ge(sg("lb_pre"), 1)
        A(lb, lb, ACT.Exp).then_inc(sg("lb_exp"), 1)
        for h in range(4):
            tile_high(2 + h)
            out = full(act, ("f", h))
            A(head(G, h), out[:, 0:T], ACT.Sigmoid).then_inc(freed(("f", h)), 1)
        for h in range(4):
            tile_high(6 + h)
            out = full(act, ("q", h))
            A(head(qT, h), out[:, 0:T], ACT.Silu).then_inc(freed(("q", h)), 1)
        logs()
        for h in range(4):
            act.wait_ge(sg("f_ready"), h + 1)
            A(head(X[1], h), head(kT, h), ACT.Ln).then_inc(sg("logf"), 1)
        for h in range(4):
            tile_high(10 + h)

        def level(n):
            act.wait_ge(sg("level_pre"), n + 1)
            A(X[n % 3], X[n % 3], ACT.Exp).then_inc(sg("level_exp"), 1)

        level(0)
        for h in range(4):
            tile_high(14 + h)
            out = full(act, ("g", h))
            A(head(gateT, h), out[:, 0:T], ACT.Silu).then_inc(freed(("g", h)), 1)
        level(1)
        level(2)
        for h in range(4):
            tile_high(18 + h)
            out = full(act, ("v", h))
            A(head(vT, h), out[:, 0:T], ACT.Gelu_apprx_tanh).then_inc(freed(("v", h)), 1)
        for n in range(3, 6):
            level(n)
        for h in range(4):
            if h < 2:
                tile_high(22 + h)
            out = full(act, ("u", h))
            A(head(uT, h), out[:, 0:T], ACT.Gelu_apprx_tanh).then_inc(freed(("u", h)), 1)
        logs()
        for g in range(4):
            read(act, ("mean", g))
            A(head(gsq, g), head(vT, g), ACT.Square).then_inc(sg("v_sq"), 1)
        for g in range(4):
            out = full(act, ("var", g))
            root(("var", g), head(gsq, g), out[:, 0:T]).then_inc(sg("v_rstd"), 1)
        act.wait_ge(sg("memn_loaded"), 16)
        for c in range(2):
            junk = mem_v_p[:, 0].rearrange("p c n -> p (c n)")
            link(A(junk, memn[:, c], ACT.Square, accum_out=stat[:, c:c + 1]))
        link(A(stat[:, 2:4], stat[:, 0:2], ACT.Ln, bias=eps, scale=1.0 / D))
        A(stat[:, 4:6], stat[:, 2:4], ACT.Exp, scale=-0.5).then_inc(sg("mem_rstd"), 1)
        full(act, ("att", 3, 2))
        A(X[0], G, ACT.Exp).then_inc(sg("start_exp"), 1)
        act.wait_ge(sg("end_pre"), 1)
        A(X[1], X[1], ACT.Exp).then_inc(sg("end_exp"), 1)
        A(gend, G.rearrange("p (c t) -> p c t", t=CH)[:, :, CH - 1], ACT.Exp).then_inc(sg("chunk_exp"), 1)
        for l in range(2):
            for c in range(2):
                out = full(act, ("ckT", l, c))
                A(mem_kT_s[:, l, :, c * P:(c + 1) * P], split(out, 4), ACT.Copy).then_inc(freed(("ckT", l, c)), 1)
            for c in range(2):
                act.wait_ge(sg("mk_squares"), 2 * l + c + 1)
                s = stat[:, 16 + 8 * (2 * l + c):24 + 8 * (2 * l + c)]
                link(A(s[:, 4:8], s[:, 0:4], ACT.Ln, bias=eps, scale=1.0 / P))
                A(s[:, 0:4], s[:, 4:8], ACT.Exp, scale=-0.5).then_inc(sg("mk_rstd"), 1)
            for c in range(2):
                out = full(act, ("memv", l, c))
                A(mem_v_p[:, l, c], out, ACT.Copy).then_inc(freed(("memv", l, c)), 1)
            for c in range(2):
                out = full(act, ("mkT", l, c))
                A(mem_kT_p[:, l, :, c * P:(c + 1) * P], split(out, 4), ACT.Copy).then_inc(freed(("mkT", l, c)), 1)
        for g in range(5):
            out = full(act, ("kp", g))
            A(kp[0:CH, 4 * g:4 * g + 4], split(out[0:CH, :], 4), ACT.Copy).then_inc(freed(("kp", g)), 1)
        for c in range(NCH):
            out = full(act, ("o", c))
            A(split(oT, 4)[:, :, c * CH:(c + 1) * CH], split(out[:, 0:256], 4), ACT.Copy).then_inc(freed(("o", c)), 1)
            act.wait_ge(freed(("o", c)), use[("o", c)][1] + 1)
        full(act, ("vn", 2))
        for h in range(4):
            A(head(vT, h), head(oT, h), ACT.Square).then_inc(sg("o_sq"), 1)
        for h in range(4):
            out = full(act, ("on", h))
            root(("on", h), head(vT, h), out[:, 0:T]).then_inc(sg("o_rstd"), 1)
        act.wait_ge(sg("out_written"), 16 * 7)
        act.wait_ge(sg("mixed"), 4)
        act.wait_ge(sg("out_written"), 16 * 7)
        tile_high(XQ[0])
        tile_high(XQ[0] + 1)
        norm(1)

        def xattn(l):
            h_high((1, 4)[l])
            if l:
                tile_high(XQ[1] + 1)
            for h in range(XH):
                if h < 2:
                    tile_high(XQ[l] + 2 + h)
                out = full(act, ("xq", l, h))
                A(head(xsq, h), out[:, 0:T], ACT.Square).then_inc(sg("xq_sq"), 1)
            for h in range(XH):
                out = full(act, ("xqn", l, h))
                root(("xqn", l, h), head(xsq, h), out[:, 0:T]).then_inc(sg("xq_rstd"), 1)

            def tail(b):
                t0, n = BLOCKS[b]
                key = ("xpT", l, b, 0)
                out = full(act, key)
                A(probT[b % 2][:, 0:4, 0:n], split(out, 4)[:, :, 0:n], ACT.Copy).then_inc(freed(key), 1)

            def attended_high(b):
                t0, n = BLOCKS[b]
                out = full(act, ("xpv", l, b))
                A(oxT[0][:, :, t0:t0 + n], split(out, 4)[:, :, 0:n], ACT.Copy).then_inc(sg("ox_high"), 1)

            def exponentials(b):
                t0, n = BLOCKS[b]
                st = xstat[b % 2]
                for k in range(2):
                    out = full(act, ("xs", l, b, k))
                    act.wait_ge(sg("xmax"), 2 * (3 * l + b) + k + 1)
                    for hh in range(2):
                        h = 2 * k + hh
                        ins = A(prob[b % 2][0:n, h], out[0:n, hh * MEM:(hh + 1) * MEM], ACT.Exp, scale=P ** -0.5,
                                bias=st[0:n, 4 + h:5 + h], accum_out=st[0:n, 8 + h:9 + h])
                    ins.then_inc(freed(("xs", l, b, k)), 1)

            exponentials(0)
            exponentials(1)
            tail(0)
            tile_high(XO[l])
            attended_high(0)
            tail(1)
            exponentials(2)
            attended_high(1)
            tile_high(XO[l] + 1)
            tail(2)
            attended_high(2)

        def w13_high(i, s):
            act.wait_ge(sg(f"w13_full{s}"), 32 * i + 32)
            act.wait_ge(sg(f"w13_used{s}"), i + 1)
            A(w_parts[s][0], W13[s], ACT.Copy).then_inc(sg("w13_high"), 1)

        def w2_high(m, s, t):
            act.wait_ge(sg(f"w2_full{s}"), 16 * m + 16)
            act.wait_ge(sg(f"w2_used{t}"), 2 * m + s + 1)
            A(split(w_parts[t][0][:, 0:11 * P], 11), W2S[s][:, :, t * P:(t + 1) * P], ACT.Copy).then_inc(sg("w2_high"), 1)

        xattn(0)
        full(act, LAST_USE["wo1"])
        w13_high(0, 0)
        norm(2, tiles={0: XO[0] + 2, 2: XO[0] + 3})
        h_high(2)

        def gate(i, s):
            act.wait_ge(sg(f"ffn_h1_{s}"), i + 1)
            act.wait_ge(sg(f"ffn_g{s}"), i + 1)
            A(sil[s], bank[2 * s][:, 0:T], ACT.Silu).then_inc(sg(f"ffn_sil{s}"), 1)

        def g_high(i, s):
            act.wait_ge(sg(f"ffn_g{s}"), i + 2)
            A(gT[0][:, bass.ds(2 * i + s, 1)].rearrange("p o n -> p (o n)"), g_raw[s], ACT.Copy).then_inc(sg("g_high"), 1)

        w13_high(0, 1)
        gate(0, 0)
        with act.Fori(1, 11) as i:
            w13_high(i, 0)
            g_high(i - 1, 0)
            gate(i - 1, 1)
            w13_high(i, 1)
            g_high(i - 1, 1)
            gate(i, 0)
        act.wait_ge(sg("w13_used0"), 12)
        w2_high(0, 0, 0)
        g_high(10, 0)
        gate(10, 1)
        g_high(10, 1)
        act.wait_ge(sg("w13_used1"), 12)
        for m in range(4):
            for s in range(2):
                for t in range(2):
                    if m + s + t:
                        w2_high(m, s, t)
        logs()
        norm(3)
        for b, (t0, n) in enumerate(BLOCKS):
            for u in range(3):
                key = ("qkv", b, u)
                out = full(act, key)
                A(qkv[0:n, b, u * 512:(u + 1) * 512], out[0:n], ACT.Copy).then_inc(freed(key), 1)
            act.wait_ge(sg("qk_squares"), b + 1)
            link(A(hstat[0:n, b, 24:44], hstat[0:n, b, 0:20], ACT.Ln, bias=eps[0:n], scale=1.0 / 64))
            A(hstat[0:n, b, 0:20], hstat[0:n, b, 24:44], ACT.Exp, scale=-0.5).then_inc(sg("qk_rstd"), 1)
        out = full(act, "cskT")
        A(kTs[:, :, 0:P], split(out[0:64], 4), ACT.Copy).then_inc(freed("cskT"), 1)
        for b, (t0, n) in enumerate(BLOCKS):
            for g in range(5):
                key = ("qkT", b, g)
                out = full(act, key)
                src = split(out[0:64], 4)[:, :, 0:n]
                if g < 4:
                    for cc in range(n // CH):
                        to = qT2[:, t0 // CH + cc, g].rearrange("p par hh t -> p hh par t")
                        of = src[:, :, cc * CH:(cc + 1) * CH].rearrange("p (hh par) t -> p hh par t", hh=2)
                        ins = A(to, of, ACT.Copy)
                    ins.then_inc(freed(key), 1)
                else:
                    if b == 2:
                        A(kTs[:, :, P:192], src, ACT.Copy).then_inc(sg("kTs_own"), 1)
                    A(kT2[:, :, t0:t0 + n], src, ACT.Copy).then_inc(freed(key), 1)

        def swa_tail(i, c, g):
            key = ("spT", c, g, 0)
            rows = min(KEYS[c][2] + KEYS[c][1], P)
            out = full(act, key)
            if i == 0:
                act.wait_ge(sg("out_written"), 16 * 11)
            A(sp_probT[i % 2][0][0:rows], split(out[0:rows], 4), ACT.Copy).then_inc(freed(key), 1)

        def window_high(c, g):
            out = full(act, ("spv", c, g))
            A(o2T[0][:, 4 * g:4 * g + 4, c * CH:(c + 1) * CH], split(out[:, 0:256], 4), ACT.Copy).then_inc(sg("o2_high"), 1)

        def exponentials(i):
            c, g = GROUPS[i]
            k0, nk, off, rows1 = KEYS[c]
            st = sstat[i % 2]
            for k in range(2):
                key = ("ss", c, g, k)
                out = full(act, key)
                act.wait_ge(sg("smax"), 2 * i + k + 1)
                if i == 0 and k == 0:
                    full(act, ("qkT", 2, 4))
                for par in range(2):
                    j = 2 * k + par
                    ins = A(sp_prob[i % 2][:, j, off:off + nk], out[:, par * 256 + off:par * 256 + off + nk], ACT.Exp,
                            scale=0.125, bias=st[:, 4 + j:5 + j], accum_out=st[:, 8 + j:9 + j])
                ins.then_inc(freed(key), 1)
            act.wait_ge(sg("sink_pre"), i + 1)
            A(st[:, 16:20], st[:, 12:16], ACT.Exp).then_inc(sg("sink_exp"), 1)

        exponentials(0)
        exponentials(1)
        for i, (c, g) in enumerate(GROUPS):
            swa_tail(i, c, g)
            window_high(c, g)
            if i < len(GROUPS) - 2:
                exponentials(i + 2)
            if i < 2:
                tile_high(AO + i)
        norm(4, tiles={**{c: AO + c + 2 for c in range(6)}, KC: XQ[1]})
        xattn(1)
        norm(5, tiles={0: XO[1] + 2, 2: XO[1] + 3})

        def high(i, j, q):
            s = j % 3
            fill = RFILLS[s] * i + j // 3 + 1
            if q == 0:
                act.wait_ge(sg(f"moe13_full{s}"), 32 * fill)
            if q == 2:
                act.wait_ge(sg(f"moe2_full{s}"), 16 * fill)
            act.wait_ge(sg(f"part_used{q}"), 11 * i + j + 1)
            raw = WD[s] if q == 2 else WE[s][:, q * 2048:(q + 1) * 2048]
            A(part[q][0], raw, ACT.Copy).then_inc(sg(f"split_hi{q}"), 1)

        full(act, ("norm", 5))
        high(0, 0, 0)
        high(0, 0, 1)
        for b, (t0, n) in enumerate(BLOCKS):
            act.wait_ge(sg("gate_pre"), b + 1)
            A(gsel[0:n, b, 1:2], gsel[0:n, b, 0:1], ACT.Exp).then_inc(sg("gate_exp"), 1)
        for b, (t0, n) in enumerate(BLOCKS):
            for k in range(2):
                key = ("hnat", b, k)
                out = full(act, key)
                A(hnat[0][0:n, b, k * 512:(k + 1) * 512], out[0:n], ACT.Copy).then_inc(sg("hnat_high"), 1)

        def selected_0(i):
            act.wait_ge(sg("selected"), 2 * i + 1)
            A(xsel[0], GA[0], ACT.Copy).then_inc(sg("sel_copied0"), 1)

        def gathered_high(i, half):
            act.wait_ge(sg("turned"), 2 * i + half + 1)
            A(xg[0][:, 4 * half:4 * half + 4], split(GA[half], 4), ACT.Copy).then_inc(sg("xg_high"), 1)

        def hidden(i, j):
            act.wait_ge(sg("part_used1"), 11 * i + j + 2)
            act.wait_ge(sg("hid_ready"), 11 * i + j + 1)
            A(act1, H[:, 0:256], ACT.Silu).then_inc(sg("act1_ready"), 1)

        def hidden_high(i, j):
            act.wait_ge(sg("hid_T"), 11 * i + j + 2)
            A(hidT[0], split(TR[:, 0:256], 2), ACT.Copy).then_inc(sg("hidT_high"), 1)

        def output_high(i):
            act.wait_ge(sg("part_used2"), 11 * i + 12)
            act.wait_ge(sg("scat_ready"), i + 1)
            for half in range(2):
                A(ysb[0][:, half * 512:(half + 1) * 512], Y[half], ACT.Copy, scale=gslot).then_inc(sg("ysb_high"), 1)

        def moe_pass(i, first=False):
            for j in range(11):
                before = (i, j - 1) if j else None if first else (i - 1, 10)
                if j or not first:
                    high(i, j, 0)
                if before:
                    hidden(*before)
                if j or not first:
                    high(i, j, 1)
                if before:
                    hidden_high(*before)
                if j == 0 and not first:
                    gathered_high(i, 0)
                    gathered_high(i, 1)
                if j == 1 and not first:
                    output_high(i - 1)
                if before:
                    high(*before, 2)
                if j == 10:
                    selected_0(i + 1)

        def moe_last(i):
            hidden(i, 10)
            hidden_high(i, 10)
            high(i, 10, 2)
            output_high(i)

        for b, (t0, n) in enumerate(BLOCKS):
            for k in range(2):
                key = ("xnat", b, k)
                out = full(act, key)
                A(xnat[0:n, b, k * 512:(k + 1) * 512], out[0:n], ACT.Copy).then_inc(freed(key), 1)
        nc.scalar.preload_act_table(ACT.Silu)
        selected_0(0)
        gathered_high(0, 0)
        gathered_high(0, 1)
        moe_pass(0, first=True)
        with act.Fori(1, E) as i:
            moe_pass(i)
        moe_last(E - 1)
        act.wait_ge(sg("flag_ready"), 1)
        overloaded = act.value_load(flag[0:1, 0:1])
        with act.If(overloaded > P):
            high(E, 0, 0)
            high(E, 0, 1)
            gathered_high(E, 0)
            gathered_high(E, 1)
            moe_pass(E, first=True)
            with act.Fori(E + 1, 2 * E) as i:
                moe_pass(i)
            with act.Fori(2 * E, PASSES) as i:
                moe_pass(i)
            moe_last(PASSES - 1)

    @block.vector
    def _(dve):
        dve.sem_inc(sg("g_low"), 2)
        dve.sem_inc(sg("ffn_out"), 3)
        for name in ("ffn_g0", "ffn_g1", "hid_ready", "hidT_ready", "scattered", "ysb_ready0",
                     "ysb_ready1", "xg_low"):
            dve.sem_inc(sg(name), 1)
        V = nc.vector
        chain = [0]

        def link(ins):
            chain[0] += 1
            ins.then_inc(sg("dve_chain"), 1)
            dve.wait_ge(sg("dve_chain"), chain[0])

        def head(x, h):
            return x[:, h * T:(h + 1) * T]

        def tile_low(t):
            raw, parts = tile_views(t, dve)
            dve.wait_ge(sg("tile_high"), t + 1)
            V.tensor_tensor(parts[1], raw, parts[0].bitcast(F32), ALU.subtract).then_inc(sg("tile_low"), 1)

        def norm(n):
            dve.wait_ge(sg("rstd_ready"), n + 1)
            parts = norm_parts(n) if n in SPLIT_BEFORE else None

            def low(c):
                dve.wait_ge(sg("h_high"), KC * SPLIT_BEFORE[n] + c + 1)
                V.tensor_tensor(parts[1][:, c], hT[:, c], parts[0][:, c].bitcast(F32), ALU.subtract) \
                    .then_inc(sg("h_low"), 1)

            for c in range(KC):
                g = prm[:, NORM_COL[n] + c:NORM_COL[n] + c + 1]
                V.scalar_tensor_tensor(hT[:, c], xT[:, c], g, rstd, ALU.mult, ALU.mult).then_inc(sg("h_ready"), 1)
                if parts and c:
                    low(c - 1)
            if parts:
                low(KC - 1)

        def residual(key, m):
            out = full(dve, key)
            V.tensor_tensor(xT[:, m], xT[:, m], out[:, 0:T], ALU.add).then_inc(freed(key), 1)

        out = full(dve, "prm")
        V.tensor_copy(prm[:, 0:NROW], out[:, 0:NROW]).then_inc(freed("prm"), 1)
        dve.wait_ge(freed("prm"), 1)
        for b, (t0, n) in enumerate(BLOCKS):
            for k in range(2):
                key = ("xin", b, k)
                out = full(dve, key)
                V.tensor_copy(xT[:, 4 * k:4 * k + 4, t0:t0 + n], split(out, 4)[:, :, 0:n]).then_inc(freed(key), 1)
        tile_low(0)
        norm(0)
        tile_low(1)
        V.tensor_tensor(lb, prm[:, R_LB1:R_LB1 + 4], prm[:, R_LB0:R_LB0 + 4], ALU.subtract).then_inc(sg("lb_pre"), 1)
        dve.wait_ge(sg("lb_exp"), 1)
        link(V.tensor_scalar(omlb, lb, 1.0, None, ALU.add))
        link(V.reciprocal(lb, omlb))
        link(V.tensor_scalar(omlb, lb, -1.0, 1.0, ALU.mult, ALU.add))
        for h in range(4):
            tile_low(2 + h)
            read(dve, ("f", h))
            V.tensor_scalar(head(kT, h), head(G, h), omlb[:, h:h + 1], lb[:, h:h + 1], ALU.mult, ALU.add) \
                .then_inc(sg("f_ready"), 1)
        for h in range(4):
            tile_low(6 + h)
        for h in range(4):
            dve.wait_ge(sg("logf"), h + 1)
            V.tensor_scalar(head(kT, h), head(kT, h), -1.0, 1.0, ALU.mult, ALU.add).then_inc(sg("k_ready"), 1)

        def level_pre(n):
            b = LEVELS[n]
            g = G.rearrange("p (n two b) -> p n two b", two=2, b=b)
            x = X[n % 3].rearrange("p (n two b) -> p n two b", two=2, b=b)
            mid = g[:, :, 0, b - 1:b].broadcast_to([P, HT // (2 * b), b])
            V.tensor_tensor(x[:, :, 0], mid, g[:, :, 0], ALU.subtract)
            ins = V.tensor_tensor(x[:, :, 1], g[:, :, 1], mid, ALU.subtract)
            ins.then_inc(sg("level_pre"), 1)

        def level_query(n):
            b = LEVELS[n]
            x = X[n % 3].rearrange("p (n two b) -> p n two b", two=2, b=b)[:, :, 1]
            q = qT.rearrange("p (n two b) -> p n two b", two=2, b=b)[:, :, 1]
            dve.wait_ge(sg("level_exp"), n + 1)
            V.tensor_tensor(x, x, q, ALU.mult).then_inc(sg("level_q"), 1)

        def level_scores(n):
            for g in range(3):
                key = ("att", n, g)
                out = full(dve, key)
                pairs = min(8, 20 - 8 * g)
                o = split(att[0:CH, g * 512:g * 512 + pairs * CH], pairs)
                mask = const[0:CH, C_LEV + n * CH:C_LEV + (n + 1) * CH].unsqueeze(1).broadcast_to([CH, pairs, CH])
                if n:
                    read(dve, ("att", n - 1, g))
                V.copy_predicated(o, mask.bitcast(U32), split(out[0:CH, 0:pairs * CH], pairs)).then_inc(freed(key), 1)

        def inputs(h):
            out = full(dve, ("i", h))
            V.tensor_copy(head(iT, h), out[:, 0:T]).then_inc(freed(("i", h)), 1)
            tile_low(10 + h)

        inputs(0)
        dve.wait_ge(sg("scan_mask"), 1)
        link(V.tensor_tensor_scan(G, X[0], X[1], 0.0, ALU.mult, ALU.add))
        inputs(1)
        level_pre(0)
        inputs(2)
        link(V.memset(att[0:CH, :], 0.0))
        inputs(3)
        for g in range(5):
            key = ("iT", g)
            out = full(dve, key)
            V.tensor_copy(vb[0:CH, 4 * g:4 * g + 4], split(out[0:CH], 4)).then_inc(freed(key), 1)
        tile_low(14)
        level_pre(1)
        tile_low(15)
        level_pre(2)
        tile_low(16)
        tile_low(17)
        for n in range(3):
            tile_low(18 + n)
            level_query(n)
        tile_low(21)
        for n in range(3):
            level_scores(n)
            level_pre(n + 3)
        tile_low(22)
        level_query(3)
        tile_low(23)
        level_query(4)
        level_query(5)
        for g in range(4):
            key = ("mean", g)
            out = full(dve, key)
            V.tensor_tensor(head(vT, g), head(vT, g), out[:, 0:T], ALU.subtract).then_inc(freed(key), 1)
        level_scores(3)
        for n in range(4, 6):
            level_scores(n)
        gc = G.rearrange("p (c t) -> p c t", t=CH)
        V.tensor_tensor(X[1].rearrange("p (c t) -> p c t", t=CH), gc[:, :, CH - 1:CH].broadcast_to([P, 20, CH]), gc,
                        ALU.subtract).then_inc(sg("end_pre"), 1)
        dve.wait_ge(sg("mem_rstd"), 1)
        for c in range(2):
            V.tensor_scalar(memn[:, c], memn[:, c], stat[:, 4 + c:5 + c], None, ALU.mult).then_inc(sg("memn_scaled"), 1)
        level_scores(6)
        out = full(dve, "wsT")
        tril = const[:, C_TRIL:C_TRIL + P].unsqueeze(1).broadcast_to([P, 4, P])
        V.tensor_tensor(wsT, split(out, 4), tril, ALU.mult).then_inc(freed("wsT"), 1)

        def memory_tokens(l):
            for g in range(4):
                c, k = divmod(g, 2)
                key = ("mT", l, g)
                out = full(dve, key)
                if g == 0:
                    full(dve, ("memv", 0, 1) if l else ("u", 3))
                gain = prm[:, R_MEM + 8 * l + 4 * k:R_MEM + 8 * l + 4 * k + 4].unsqueeze(2).broadcast_to([P, 4, P])
                V.tensor_tensor(hT[:, 4 * k:4 * k + 4, c * P:(c + 1) * P], split(out, 4), gain, ALU.mult) \
                    .then_inc(freed(key), 1)

        dve.wait_ge(sg("small_loaded"), 96)
        memory_tokens(0)
        dve.wait_ge(sg("start_exp"), 1)
        V.tensor_tensor(qT, qT, X[0], ALU.mult).then_inc(sg("qp_ready"), 1)
        for g in range(4):
            dve.wait_ge(sg("v_rstd"), g + 1)
            link(V.scalar_tensor_tensor(head(vT, g), head(vT, g), prm[:, R_LNG + g:R_LNG + g + 1], head(gsq, g),
                                        ALU.mult, ALU.mult))
            V.tensor_scalar(head(vT, g), head(vT, g), prm[:, R_LNB + g:R_LNB + g + 1], None, ALU.add) \
                .then_inc(sg("vn_ready"), 1)
        dve.wait_ge(sg("small_loaded"), 96)
        dve.wait_ge(sg("qp_ready"), 1)
        dve.wait_ge(sg("vn_ready"), 4)
        for l in range(2):
            if l:
                memory_tokens(l)
            for c in range(2):
                key = ("memk", l, c)
                out = full(dve, key)
                y = mkn[l][:, c]
                junk = iT[:, 0:512]
                s = stat[:, 16 + 8 * (2 * l + c):24 + 8 * (2 * l + c)]
                V.tensor_copy(y, out).then_inc(freed(key), 1)
                dve.wait_ge(freed(key), use[key][1] + 1)
                link(V.tensor_tensor(junk, y, y, ALU.mult))
                V.reduce_sum(s[:, 0:4], split(junk, 4), axis=AX.X).then_inc(sg("mk_squares"), 1)
                dve.wait_ge(sg("mk_rstd"), 2 * l + c + 1)
                link(V.tensor_tensor(split(y, 4), split(y, 4), s[:, 0:4].unsqueeze(2).broadcast_to([P, 4, P]), ALU.mult))
                V.tensor_tensor(split(y, 4), split(y, 4), kg[:, l].unsqueeze(1).broadcast_to([P, 4, P]), ALU.mult) \
                    .then_inc(sg("mk_ready"), 1)
        for b, (t0, n) in enumerate(BLOCKS):
            key = ("vn", b)
            out = full(dve, key)
            V.tensor_copy(vnat[0:n, b], out[0:n]).then_inc(freed(key), 1)
        for g in range(4):
            key = ("gate", g)
            out = full(dve, key)
            V.tensor_tensor(hT[:, g], head(uT, g), out[:, 0:T], ALU.mult).then_inc(freed(key), 1)
        dve.wait_ge(sg("chunk_exp"), 1)
        dve.wait_ge(sg("state_loaded"), 16)
        for c in range(NCH):
            key = ("S", c)
            out = full(dve, key)
            if c:
                full(dve, ("o", c))
            if 1 <= c < 4:
                read(dve, ("S", c - 1))
            for h in range(4):
                S = Ss if c == 4 else Sp
                hc = h * NCH + c
                if c == 0:
                    ins = V.tensor_copy(S[:, h], out[:, h * P:(h + 1) * P])
                else:
                    ins = V.scalar_tensor_tensor(S[:, h], S[:, h], gend[:, hc:hc + 1], out[:, h * P:(h + 1) * P],
                                                 ALU.mult, ALU.add)
            ins.then_inc(freed(key), 1)
        for h in range(4):
            dve.wait_ge(sg("o_rstd"), h + 1)
            link(V.scalar_tensor_tensor(head(vT, h), head(oT, h), prm[:, R_OUT:R_OUT + 1], head(vT, h), ALU.mult, ALU.mult))
            V.tensor_tensor(hT[:, 4 + h], head(vT, h), head(gateT, h), ALU.mult).then_inc(sg("mixed"), 1)
        tile_low(XQ[0])
        tile_low(XQ[0] + 1)
        for m in range(KC):
            residual(("wo", m), m)
        norm(1)

        def w13_low(i, s):
            dve.wait_ge(sg("w13_high"), 2 * i + s + 1)
            V.tensor_tensor(w_parts[s][1], W13[s], w_parts[s][0].bitcast(F32), ALU.subtract).then_inc(sg("w13_low"), 1)

        def w2_low(m, s, t):
            dve.wait_ge(sg("w2_high"), 4 * m + 2 * s + t + 1)
            V.tensor_tensor(split(w_parts[t][1][:, 0:11 * P], 11), W2S[s][:, :, t * P:(t + 1) * P],
                            split(w_parts[t][0][:, 0:11 * P], 11).bitcast(F32), ALU.subtract).then_inc(sg("w2_low"), 1)

        def xattn(l):
            if l:
                tile_low(XQ[1] + 1)
            for h in range(XH):
                if h < 2:
                    tile_low(XQ[l] + 2 + h)
                out = full(dve, ("xq", l, h))
                dve.wait_ge(sg("xq_sq"), 4 * l + h + 1)
                V.tensor_copy(head(qx, h), out[:, 0:T]).then_inc(freed(("xq", l, h)), 1)
            for h in range(XH):
                read(dve, ("xq", l, h))
                dve.wait_ge(sg("xq_rstd"), 4 * l + h + 1)
                V.scalar_tensor_tensor(head(qn, h), head(qx, h), prm[:, R_XQ + l:R_XQ + l + 1], head(xsq, h),
                                       ALU.mult, ALU.mult).then_inc(sg("xq_ready"), 1)

            def tail(b):
                t0, n = BLOCKS[b]
                key = ("xpT", l, b, 1)
                out = full(dve, key)
                V.tensor_copy(probT[b % 2][:, 4:8, 0:n], split(out, 4)[:, :, 0:n]).then_inc(freed(key), 1)

            def peaks(b):
                t0, n = BLOCKS[b]
                st = xstat[b % 2]
                for k in range(2):
                    out = full(dve, ("xs", l, b, k))
                    link(V.reduce_max(st[0:n, 2 * k:2 * k + 2], split(out[0:n], 2), axis=AX.X))
                    V.tensor_scalar(st[0:n, 4 + 2 * k:6 + 2 * k], st[0:n, 2 * k:2 * k + 2], -(P ** -0.5), None, ALU.mult) \
                        .then_inc(sg("xmax"), 1)

            def normalise(b):
                t0, n = BLOCKS[b]
                st = xstat[b % 2]
                for k in range(2):
                    key = ("xs", l, b, k)
                    dve.wait_ge(freed(key), use[key][1] + 1)
                link(V.reciprocal(st[0:n, 12:16], st[0:n, 8:12]))
                V.tensor_tensor(prob[b % 2][0:n], prob[b % 2][0:n], st[0:n, 12:16].unsqueeze(2).broadcast_to([n, 4, MEM]),
                                ALU.mult).then_inc(sg("xprob"), 1)

            def attended_low(b):
                t0, n = BLOCKS[b]
                dve.wait_ge(sg("ox_high"), 3 * l + b + 1)
                V.tensor_tensor(oxT[1][:, :, t0:t0 + n], split(bank[use[("xpv", l, b)][0]], 4)[:, :, 0:n],
                                oxT[0][:, :, t0:t0 + n].bitcast(F32), ALU.subtract).then_inc(freed(("xpv", l, b)), 1)

            peaks(0)
            peaks(1)
            normalise(0)
            tail(0)
            normalise(1)
            peaks(2)
            attended_low(0)
            tail(1)
            tile_low(XO[l])
            normalise(2)
            attended_low(1)
            tail(2)
            tile_low(XO[l] + 1)
            attended_low(2)
            if l == 0:
                w13_low(0, 0)
            for m in range(KC):
                residual(("xo", l, m), m)
                if m in (1, 3):
                    tile_low(XO[l] + 2 + m // 2)

        xattn(0)
        norm(2)

        def gated(i, s):
            dve.wait_ge(sg(f"ffn_sil{s}"), i + 1)
            dve.wait_ge(sg(f"w13_used{s}"), i + 2)
            dve.wait_ge(sg("g_low"), 2 * i + s + 1)
            V.tensor_tensor(g_raw[s], sil[s], bank[2 * s + 1][:, 0:T], ALU.mult).then_inc(sg(f"ffn_g{s}"), 1)

        def g_low(i, s):
            dve.wait_ge(sg("g_high"), 2 * i + s + 1)
            at = bass.ds(2 * i + s, 1)
            V.tensor_tensor(gT[1][:, at].rearrange("p o n -> p (o n)"), g_raw[s],
                            gT[0][:, at].rearrange("p o n -> p (o n)").bitcast(F32), ALU.subtract).then_inc(sg("g_low"), 1)

        w13_low(0, 1)
        gated(0, 0)
        with dve.Fori(1, 11) as i:
            w13_low(i, 0)
            g_low(i - 1, 0)
            gated(i - 1, 1)
            w13_low(i, 1)
            g_low(i - 1, 1)
            gated(i, 0)
        w2_low(0, 0, 0)
        g_low(10, 0)
        gated(10, 1)
        g_low(10, 1)

        def ffn_out(m, t):
            dve.wait_ge(sg(f"w2_used{t}"), 2 * m + 3)
            x = xT[:, 2 * m + t]
            V.tensor_tensor(x, x, bank[4 + 2 * (m % 2) + t][:, 0:T], ALU.add).then_inc(sg("ffn_out"), 1)

        for m in range(4):
            for s in range(2):
                for t in range(2):
                    if m + s + t:
                        w2_low(m, s, t)
                    if s == 0 and m:
                        ffn_out(m - 1, t)
        ffn_out(3, 0)
        ffn_out(3, 1)
        norm(3)
        for b, (t0, n) in enumerate(BLOCKS):
            read(dve, ("qkv", b, 2))
            x = qkv[0:n, b, 0:1280]
            if b:
                dve.wait_ge(sg("rot_done"), 2 * b)
            link(V.tensor_tensor(rot[0:n, b], x, x, ALU.mult))
            V.reduce_sum(hstat[0:n, b, 0:20], rot[0:n, b].rearrange("p (h d) -> p h d", d=64), axis=AX.X) \
                .then_inc(sg("qk_squares"), 1)
            dve.wait_ge(sg("qk_rstd"), b + 1)
            heads = x.rearrange("p (h d) -> p h d", d=64)
            V.tensor_tensor(heads, heads, hstat[0:n, b, 0:20].unsqueeze(2).broadcast_to([n, 20, 64]), ALU.mult) \
                .then_inc(sg("qk_scaled"), 1)
            dve.wait_ge(sg("qk_scaled"), b + 1)
            dve.wait_ge(sg("rope_tables"), 12)
            r = rot[0:n, b].rearrange("p (h d) -> p h d", d=64)
            m = rtmp[0:n].rearrange("p (h d) -> p h d", d=64)
            for h0, nh, f in ((0, 16, 0), (16, 4, 2)):
                ins = V.tensor_tensor(r[:, h0:h0 + nh], heads[:, h0:h0 + nh],
                                      gcs[0:n, b, f].unsqueeze(1).broadcast_to([n, nh, 64]), ALU.mult)
            link(ins)
            dve.wait_ge(sg("sine_ready"), 2 * b + 2)
            V.tensor_tensor(r[:, :, 0:32], r[:, :, 0:32], m[:, :, 32:64], ALU.subtract).then_inc(sg("rot_done"), 1)
            V.tensor_tensor(r[:, :, 32:64], r[:, :, 32:64], m[:, :, 0:32], ALU.add).then_inc(sg("rot_done"), 1)

        def swa_tail(i, c, g):
            if not KEYS[c][3]:
                return
            key = ("spT", c, g, 1)
            out = full(dve, key)
            rows = KEYS[c][3]
            dve.wait_ge(sg("out_written"), 16 * 11)
            V.tensor_copy(sp_probT[i % 2][1][0:rows], split(out[0:rows], 4)).then_inc(freed(key), 1)

        def peaks(i):
            c, g = GROUPS[i]
            k0, nk, off, rows1 = KEYS[c]
            st = sstat[i % 2]
            for k in range(2):
                key = ("ss", c, g, k)
                out = full(dve, key)
                link(V.reduce_max(st[:, 2 * k:2 * k + 2], split(out, 2)[:, :, off:off + nk], axis=AX.X))
                sink = sinkc[:, 4 * g + 2 * k:4 * g + 2 * k + 2]
                link(V.scalar_tensor_tensor(st[:, 2 * k:2 * k + 2], st[:, 2 * k:2 * k + 2], 0.125, sink, ALU.mult, ALU.max))
                V.tensor_scalar(st[:, 4 + 2 * k:6 + 2 * k], st[:, 2 * k:2 * k + 2], -1.0, None, ALU.mult) \
                    .then_inc(sg("smax"), 1)
            dve.wait_ge(sg("smax"), 2 * i + 2)
            V.tensor_tensor(st[:, 12:16], st[:, 4:8], sinkc[:, 4 * g:4 * g + 4], ALU.add).then_inc(sg("sink_pre"), 1)

        def normalise(i):
            c, g = GROUPS[i]
            k0, nk, off, rows1 = KEYS[c]
            st = sstat[i % 2]
            pr = sp_prob[i % 2]
            dve.wait_ge(sg("sink_exp"), i + 1)
            for k in range(2):
                key = ("ss", c, g, k)
                dve.wait_ge(freed(key), use[key][1] + 1)
            link(V.tensor_tensor(st[:, 12:16], st[:, 8:12], st[:, 16:20], ALU.add))
            link(V.reciprocal(st[:, 20:24], st[:, 12:16]))
            if off:
                V.memset(pr[:, :, 0:off], 0.0)
            V.tensor_tensor(pr[:, :, off:off + nk], pr[:, :, off:off + nk],
                            st[:, 20:24].unsqueeze(2).broadcast_to([P, 4, nk]), ALU.mult).then_inc(sg("sprob"), 1)

        def window_low(i, c, g):
            dve.wait_ge(sg("o2_high"), i + 1)
            at = o2T[1][:, 4 * g:4 * g + 4, c * CH:(c + 1) * CH]
            V.tensor_tensor(at, split(bank[use[("spv", c, g)][0]][:, 0:256], 4),
                            o2T[0][:, 4 * g:4 * g + 4, c * CH:(c + 1) * CH].bitcast(F32), ALU.subtract) \
                .then_inc(freed(("spv", c, g)), 1)

        peaks(0)
        peaks(1)
        normalise(0)
        for i, (c, g) in enumerate(GROUPS):
            if i:
                window_low(i - 1, *GROUPS[i - 1])
            swa_tail(i, c, g)
            if i < len(GROUPS) - 1:
                normalise(i + 1)
            if i < len(GROUPS) - 2:
                peaks(i + 2)
            if i in (1, 2):
                tile_low(AO + i - 1)
        window_low(9, *GROUPS[9])
        for m in range(KC):
            residual(("ao", m), m)
            if m < 6:
                tile_low(AO + m + 2)
        tile_low(XQ[1])
        norm(4)
        xattn(1)
        norm(5)
        for b, (t0, n) in enumerate(BLOCKS):
            key = ("logit", b)
            out = full(dve, key)
            V.tensor_copy(logit[0:n, b], out[0:n, 0:E]).then_inc(freed(key), 1)
            dve.wait_ge(freed(key), use[key][1] + 1)
            link(V.max(top8[0:n, b], logit[0:n, b]))
            link(V.max_index(idx8[0:n, b].bitcast(U32), top8[0:n, b], logit[0:n, b]))
            link(V.tensor_copy(idxf[0:n, b], idx8[0:n, b].bitcast(U32)))
            for k in range(2):
                ins = V.tensor_scalar(eq[0:n, b, k], const[0:n, C_IOTA:C_IOTA + E], idxf[0:n, b, k:k + 1], None,
                                      ALU.is_equal)
            link(ins)
            V.tensor_tensor(gsel[0:n, b, 0:1], top8[0:n, b, 1:2], top8[0:n, b, 0:1], ALU.subtract) \
                .then_inc(sg("gate_pre"), 1)
            V.tensor_tensor(chosen[0:n, b], eq[0:n, b, 0], eq[0:n, b, 1], ALU.add).then_inc(sg("chosen"), 1)
        for b, (t0, n) in enumerate(BLOCKS):
            for k in range(2):
                key = ("hnat", b, k)
                out = full(dve, key)
                dve.wait_ge(sg("hnat_high"), 2 * b + k + 1)
                c = slice(k * 512, (k + 1) * 512)
                V.tensor_tensor(hnat[1][0:n, b, c], out[0:n], hnat[0][0:n, b, c].bitcast(F32), ALU.subtract) \
                    .then_inc(freed(key), 1)
        for b, (t0, n) in enumerate(BLOCKS):
            key = ("rank", b)
            out = full(dve, key)
            link(V.scalar_tensor_tensor(rank[0:n, b], out[0:n, 0:E], 1.0, chosen[0:n, b], ALU.add, ALU.mult))
            V.tensor_scalar(rank[0:n, b], rank[0:n, b], -1.0, None, ALU.add).then_inc(freed(key), 1)
            dve.wait_ge(freed(key), use[key][1] + 1)
            times = PASSES // E + 1
            base = const[0:n, C_BASE:C_BASE + PASSES + 8].rearrange("p (r e) -> p r e", e=E)
            link(V.tensor_tensor(slot[0:n, b].rearrange("p (r e) -> p r e", e=E),
                                 rank[0:n, b].unsqueeze(1).broadcast_to([n, times, E]), base, ALU.subtract))
        out = full(dve, "load")
        link(V.tensor_copy(load, out[:, 0:E]))
        V.reduce_max(maxload, load, axis=AX.X).then_inc(freed("load"), 1)
        dve.wait_ge(freed("load"), use["load"][1] + 1)
        V.tensor_copy(flag[0:1, 0:1], maxload[0:1, :]).then_inc(sg("flag_ready"), 1)

        iota = const[:, C_IOTA:C_IOTA + P]

        def columns(i):
            for b, (t0, n) in enumerate(BLOCKS):
                V.tensor_scalar(onehot[0:n, b], iota[0:n], slot[0:n, b, bass.ds(i, 1)], None, ALU.is_equal) \
                    .then_inc(sg("onehot"), 1)

        def low(i, j, q):
            s = j % 3
            dve.wait_ge(sg(f"split_hi{q}"), 11 * i + j + 1)
            raw = WD[s] if q == 2 else WE[s][:, q * 2048:(q + 1) * 2048]
            V.tensor_tensor(part[q][1], raw, part[q][0].bitcast(F32), ALU.subtract).then_inc(sg(f"split_lo{q}"), 1)

        def gathered_low(i, half):
            dve.wait_ge(sg("xg_high"), 2 * i + half + 1)
            c = slice(4 * half, 4 * half + 4)
            V.tensor_tensor(xg[1][:, c], split(GA[half], 4), xg[0][:, c].bitcast(F32), ALU.subtract).then_inc(sg("xg_low"), 1)

        def selected_1(i):
            dve.wait_ge(sg("selected"), 2 * i + 2)
            V.tensor_copy(xsel[1], GA[1]).then_inc(sg("sel_copied1"), 1)

        full(dve, ("hnat", 2, 1))
        V.memset(scat[:, 2].bitcast(F32), 0.0).then_inc(sg("scat_clear"), 1)
        for b, (t0, n) in enumerate(BLOCKS):
            V.tensor_scalar(onehot[0:n, b], iota[0:n], slot[0:n, b, 0:1], None, ALU.is_equal).then_inc(sg("onehot"), 1)
        low(0, 0, 0)
        low(0, 0, 1)
        dve.wait_ge(sg("scat_clear"), 1)

        def hidden(i, j):
            dve.wait_ge(sg("act1_ready"), 11 * i + j + 1)
            dve.wait_ge(sg("hid_T"), 11 * i + j + 1)
            V.tensor_tensor(hid, act1, H[:, 256:512], ALU.mult).then_inc(sg("hid_ready"), 1)

        def hidden_low(i, j):
            dve.wait_ge(sg("hidT_high"), 11 * i + j + 1)
            V.tensor_tensor(hidT[1], split(TR[:, 0:256], 2), hidT[0].bitcast(F32), ALU.subtract) \
                .then_inc(sg("hidT_ready"), 1)

        def output_low(i):
            for half in range(2):
                dve.wait_ge(sg("ysb_high"), 2 * i + half + 1)
                c = slice(half * 512, (half + 1) * 512)
                V.scalar_tensor_tensor(ysb[1][:, c], Y[half], gslot, ysb[0][:, c].bitcast(F32), ALU.mult, ALU.subtract) \
                    .then_inc(sg(f"ysb_ready{half}"), 1)

        def scattered(i, q):
            b, half = divmod(q, 2)
            t0, n = BLOCKS[b]
            dve.wait_ge(sg("scatter_done"), 6 * i + q + 2)
            x = xnat[0:n, b, half * 512:(half + 1) * 512]
            V.tensor_tensor(x, x, O[q % 2][0:n, :], ALU.add).then_inc(sg("scattered"), 1)

        def token_gates(b, n):
            dve.wait_ge(sg("gate_exp"), b + 1)
            s = gsel[0:n, b]
            link(V.tensor_scalar(s[:, 2:3], s[:, 1:2], 1.0, None, ALU.add))
            link(V.reciprocal(s[:, 3:4], s[:, 2:3]))
            link(V.tensor_tensor(s[:, 0:1], s[:, 1:2], s[:, 3:4], ALU.mult))
            link(V.tensor_scalar(logit[0:n, b], eq[0:n, b, 0], s[:, 3:4], None, ALU.mult))
            link(V.scalar_tensor_tensor(logit[0:n, b], eq[0:n, b, 1], s[:, 0:1], logit[0:n, b], ALU.mult, ALU.add))
            times = PASSES // E + 1
            link(V.tensor_copy(gates[0:n, b].rearrange("p (r e) -> p r e", e=E),
                               logit[0:n, b].unsqueeze(1).broadcast_to([n, times, E])))

        def moe_pass(i, first=False):
            for j in range(11):
                before = (i, j - 1) if j else None if first else (i - 1, 10)
                if j or not first:
                    low(i, j, 0)
                if before:
                    hidden(*before)
                if j or not first:
                    low(i, j, 1)
                if before:
                    hidden_low(*before)
                if j == 0 and not first:
                    gathered_low(i, 0)
                    gathered_low(i, 1)
                if j == 1 and not first:
                    output_low(i - 1)
                if before:
                    low(*before, 2)
                if first and i == 0 and j in (1, 2, 3):
                    token_gates(j - 1, BLOCKS[j - 1][1])
                if j in (3, 4, 5) and not first:
                    scattered(i - 1, 2 * j - 6)
                    scattered(i - 1, 2 * j - 5)
                if j == 6:
                    dve.wait_ge(sg("scat_T"), i + 2)
                    V.tensor_copy(scat[:, 0:2], split(O[0][:, 0:2 * P], 2)).then_inc(sg("scat_parts"), 1)
                    V.tensor_copy(scat[:, 2, 0:TS], O[0][:, 2 * P:T]).then_inc(sg("scat_parts"), 1)
                    V.tensor_copy(gslot, O[0][:, 384:385]).then_inc(sg("scat_ready"), 1)
                if j == 7:
                    columns(i + 1)
                if j == 10:
                    selected_1(i + 1)

        def moe_last(i):
            hidden(i, 10)
            hidden_low(i, 10)
            low(i, 10, 2)
            output_low(i)
            for q in range(6):
                scattered(i, q)
            dve.wait_ge(sg("scattered"), 6 * i + 7)

        selected_1(0)
        read(dve, ("xnat", 2, 1))
        gathered_low(0, 0)
        gathered_low(0, 1)
        moe_pass(0, first=True)
        with dve.Fori(1, E) as i:
            moe_pass(i)
        moe_last(E - 1)
        overloaded = dve.value_load(flag[0:1, 0:1])
        with dve.If(overloaded > P):
            low(E, 0, 0)
            low(E, 0, 1)
            gathered_low(E, 0)
            gathered_low(E, 1)
            moe_pass(E, first=True)
            with dve.Fori(E + 1, 2 * E) as i:
                moe_pass(i)
            with dve.Fori(2 * E, PASSES) as i:
                moe_pass(i)
            moe_last(PASSES - 1)
        V.memset(maxload, 0.0).then_inc(sg("y_final"), 1)

    ctx.close()


OUTS = [("y_prompt", (1, TP, D)), ("y_sample", (1, TS, D)),
        ("mem_k_prompt", (2, 1, MEM, 4, 128)), ("mem_v_prompt", (2, 1, MEM, 4, 128)),
        ("hgrn_state_prompt", (1, 1, 4, 128, 128)), ("gmlp_v_sample", (1, 1, TS, 4, 128)),
        ("hgrn_state_sample", (1, 1, 4, 128, 128)),
        ("swa_k_prompt", (1, 1, 128, 4, 64)), ("swa_v_prompt", (1, 1, 128, 4, 64)),
        ("swa_k_sample", (1, 1, TS, 4, 64)), ("swa_v_sample", (1, 1, TS, 4, 64))]


def kernel(**inputs):
    import concourse.bacc as bacc
    from concourse.bass_utils import run_bass_kernel_spmd

    nc = bacc.Bacc("TRN2", target_bir_lowering=False, num_devices=1)
    arrays, a = {}, {}
    for name, x in list(inputs.items()) + [("shape_constants", constants())]:
        x = np.ascontiguousarray(x)
        arrays[f"in_{name}"] = x
        a[name] = nc.dram_tensor(f"in_{name}", x.shape, mybir.dt.from_np(x.dtype), kind="ExternalInput").ap()
    for name, shape in OUTS:
        a[name] = nc.dram_tensor(f"out_{name}", shape, F32, kind="ExternalOutput").ap()
    build(nc, a)
    r = run_bass_kernel_spmd(nc, [arrays], core_ids=[0])
    return tuple(r.results[0][f"out_{name}"] for name, _ in OUTS)
```
